# Optimizing a Trainium2 kernel written in Bass

```python
import math, functools
import jax, jax.numpy as jnp
from jax import lax
import numpy as np

D_MODEL = 1024
BATCH = 1
SEQ = 512
DEPTH = 2
DEC_BATCH = 1
DEC_SEQ = 32
PAST_LEN = 256

CHUNK = 64
Q_BLOCK = 128
EPS = 1e-6
H_A = 8
A_NOPE = 64
A_ROPE = 32
A_V = 64
Q_LORA = 384
KV_LORA = 256
ROPE_THETA = 10000.0
H_B = 8
D_B = 64
H_C = 8
D_C = 64
H_IDX = 8
D_IDX = 64
TOPK_MAX = 256
NUM_BUCKETS = 32
MAX_DISTANCE = 256
N_BRANCH = 3
MIX_W = 512
D_FF = 2816
IN_SPLITS = (Q_LORA, KV_LORA, A_ROPE,
             H_B * D_B, H_B * D_B, H_B * D_B,
             H_C * D_C, D_C, D_C, H_IDX * D_IDX, D_IDX, H_IDX,
             D_MODEL, D_MODEL, D_MODEL)
IN_OFFSETS = tuple(int(o) for o in np.cumsum(IN_SPLITS)[:-1])
N_IN = int(sum(IN_SPLITS))

kernel_name = 'hybrid_mla_stickbreak_dsa_stream'

def rmsnorm(x, g):
    xf = x.astype(jnp.float32)
    y = xf * lax.rsqrt(jnp.mean(xf * xf, axis=-1, keepdims=True) + EPS)
    return (y * g.astype(jnp.float32)).astype(x.dtype)

def rope(x, pos):
    half = x.shape[-1] // 2
    inv = ROPE_THETA ** (-jnp.arange(half, dtype=jnp.float32) / half)
    ang = pos.astype(jnp.float32)[:, None] * inv[None, :]
    ang = ang.reshape((1, ang.shape[0]) + (1,) * (x.ndim - 3) + (half,))
    c, s = jnp.cos(ang), jnp.sin(ang)
    xf = x.astype(jnp.float32)
    x1, x2 = xf[..., :half], xf[..., half:]
    return jnp.concatenate([x1 * c - x2 * s, x1 * s + x2 * c], axis=-1).astype(x.dtype)

def chunk_visible(q_pos, k_pos):
    return (k_pos // CHUNK) <= (q_pos // CHUNK)

def t5_bucket(rel):
    nb = NUM_BUCKETS // 2
    max_exact = nb // 2
    ret = jnp.where(rel > 0, nb, 0)
    n = jnp.abs(rel)
    nf = jnp.maximum(n, 1).astype(jnp.float32)
    large = max_exact + (jnp.log(nf / max_exact) / math.log(MAX_DISTANCE / max_exact)
                         * (nb - max_exact)).astype(jnp.int32)
    large = jnp.minimum(large, nb - 1)
    return ret + jnp.where(n < max_exact, n, large)

def sweep(attend, q_args, kv_args, q_pos, k_pos):
    t_q = q_pos.shape[0]
    if t_q <= Q_BLOCK:
        return attend(q_args, kv_args, q_pos, k_pos)
    past = k_pos.shape[0] - t_q
    outs = []
    for s in range(0, t_q, Q_BLOCK):
        e = min(s + Q_BLOCK, t_q)
        outs.append(attend(tuple(a[:, s:e] for a in q_args),
                           tuple(a[:, :past + e] for a in kv_args),
                           q_pos[s:e], k_pos[:past + e]))
    return jnp.concatenate(outs, axis=1)

def mla_attend(q_args, kv_args, q_pos, k_pos):
    q_nope, q_rope = q_args
    k_nope, k_rope, v = kv_args
    s = (jnp.einsum('bqhd,bkhd->bhqk', q_nope, k_nope)
         + jnp.einsum('bqhd,bkd->bhqk', q_rope, k_rope)).astype(jnp.float32)
    s = s * (A_NOPE + A_ROPE) ** -0.5
    s = jnp.where(chunk_visible(q_pos[:, None], k_pos[None, :]), s, -jnp.inf)
    p = jax.nn.softmax(s, axis=-1)
    return jnp.einsum('bhqk,bkhd->bqhd', p.astype(v.dtype), v)

def sb_attend(q_args, kv_args, q_pos, k_pos):
    (q,) = q_args
    k, v = kv_args
    z = jnp.einsum('bqhd,bkhd->bhqk', q, k).astype(jnp.float32) * D_B ** -0.5
    strict = k_pos[None, :] < q_pos[:, None]
    log_beta = jax.nn.log_sigmoid(z)
    log_keep = jnp.where(strict, jax.nn.log_sigmoid(-z), 0.0)
    log_stick = lax.cumsum(log_keep, axis=3, reverse=True) - log_keep
    a = jnp.where(strict, jnp.exp(log_beta + log_stick), 0.0)
    return jnp.einsum('bhqk,bkhd->bqhd', a, v.astype(jnp.float32)).astype(v.dtype)

def dsa_attend(topk, rel_bias, q_args, kv_args, q_pos, k_pos):
    q, qi, wi = q_args
    k, v, ki = kv_args
    vis = chunk_visible(q_pos[:, None], k_pos[None, :])
    rel = jax.nn.relu(jnp.einsum('bqhd,bkd->bqhk', qi, ki).astype(jnp.float32) * D_IDX ** -0.5)
    score = jnp.einsum('bqhk,bqh->bqk', rel, wi.astype(jnp.float32) * H_IDX ** -0.5)
    score = jnp.where(vis[None], score, -jnp.inf)
    kk = min(topk, k_pos.shape[0])
    _, sel = lax.top_k(score, kk)
    gather = jax.vmap(lambda a, i: a[i])
    k_sel = gather(k, sel)
    v_sel = gather(v, sel)
    pos_sel = k_pos[sel]
    valid = chunk_visible(q_pos[None, :, None], pos_sel)
    bias = rel_bias[t5_bucket(pos_sel - q_pos[None, :, None])]
    logits = (jnp.einsum('bqhd,bqjd->bhqj', q, k_sel).astype(jnp.float32) * D_C ** -0.5
              + jnp.moveaxis(bias.astype(jnp.float32), -1, 1))
    logits = jnp.where(valid[:, None], logits, -jnp.inf)
    p = jax.nn.softmax(logits, axis=-1)
    return jnp.einsum('bhqj,bqjd->bqhd', p.astype(v.dtype), v_sel)

def ffn_half(x, pre_g, w_up, w_down, post_g):
    h = rmsnorm(x, pre_g)
    gate, up = jnp.split(h @ w_up, 2, axis=-1)
    y = (jax.nn.silu(gate) * up) @ w_down
    return x + 0.5 * rmsnorm(y, post_g)

def mixer(x, l, past, P, rel_bias):
    b, t, _ = x.shape
    p_len = 0 if past is None else past[0].shape[1]
    q_pos = p_len + jnp.arange(t, dtype=jnp.int32)
    k_pos = jnp.arange(p_len + t, dtype=jnp.int32)
    u = rmsnorm(x, P['mix_pre_gain'][l])
    (q_lat, kv_lat, k_r, q_b, k_b, v_b, q_c, k_c, v_c, q_i, k_i, w_i,
     g_a, g_b, g_c) = jnp.split(u @ P['w_in'][l], IN_OFFSETS, axis=-1)
    c_q = rmsnorm(q_lat, P['mla_q_norm'][l])
    qa = (c_q @ P['w_mla_uq'][l]).reshape(b, t, H_A, A_NOPE + A_ROPE)
    qa_nope, qa_rope = qa[..., :A_NOPE], rope(qa[..., A_NOPE:], q_pos)
    c_kv = rmsnorm(kv_lat, P['mla_kv_norm'][l])
    k_rope = rope(k_r, q_pos)
    new_rows = (c_kv, k_rope,
                k_b.reshape(b, t, H_B, D_B), v_b.reshape(b, t, H_B, D_B),
                k_c, v_c, k_i)
    if past is None:
        full = new_rows
    else:
        full = tuple(jnp.concatenate([pa, nr], axis=1) for pa, nr in zip(past, new_rows))
    ckv_all, krope_all, kb_all, vb_all, kc_all, vc_all, ki_all = full
    kv = (ckv_all @ P['w_mla_ukv'][l]).reshape(b, -1, H_A, A_NOPE + A_V)
    o_a = sweep(mla_attend, (qa_nope, qa_rope),
                (kv[..., :A_NOPE], krope_all, kv[..., A_NOPE:]), q_pos, k_pos)
    o_b = sweep(sb_attend, (q_b.reshape(b, t, H_B, D_B),), (kb_all, vb_all), q_pos, k_pos)
    topk = min(TOPK_MAX, k_pos.shape[0] // 4)
    o_c = sweep(functools.partial(dsa_attend, topk, rel_bias),
                (q_c.reshape(b, t, H_C, D_C), q_i.reshape(b, t, H_IDX, D_IDX), w_i),
                (kc_all, vc_all, ki_all), q_pos, k_pos)
    w_br = P['w_branch'][l]
    merged = (jax.nn.sigmoid(g_a) * (o_a.reshape(b, t, MIX_W) @ w_br[0])
              + jax.nn.sigmoid(g_b) * (o_b.reshape(b, t, MIX_W) @ w_br[1])
              + jax.nn.sigmoid(g_c) * (o_c.reshape(b, t, MIX_W) @ w_br[2]))
    y = merged @ P['w_o'][l]
    return x + rmsnorm(y, P['mix_post_gain'][l]), new_rows

def trunk(x, past, P, rel_bias):
    rows = []
    for l in range(DEPTH):
        x = ffn_half(x, P['ffn_pre_gain'][l, 0], P['w_ffn_up'][l, 0],
                     P['w_ffn_down'][l, 0], P['ffn_post_gain'][l, 0])
        x, new = mixer(x, l, None if past is None else past[l], P, rel_bias)
        x = ffn_half(x, P['ffn_pre_gain'][l, 1], P['w_ffn_up'][l, 1],
                     P['w_ffn_down'][l, 1], P['ffn_post_gain'][l, 1])
        rows.append(new)
    return x, tuple(jnp.stack(group) for group in zip(*rows))

def setup_inputs(seed: int = 0) -> dict:
    key = jax.random.key(seed)
    ks = jax.random.split(key, 24)
    def nrm(k, shape, scale):
        return jax.random.normal(k, shape, jnp.float32) * scale
    def gain(k, shape):
        return 1.0 + 0.02 * jax.random.normal(k, shape, jnp.float32)
    return {
        'x_prompt': nrm(ks[0], (BATCH, SEQ, D_MODEL), 1.0),
        'x_sample': nrm(ks[1], (DEC_BATCH, DEC_SEQ, D_MODEL), 1.0),
        'cache_mla_ckv': nrm(ks[2], (DEPTH, DEC_BATCH, PAST_LEN, KV_LORA), 1.0),
        'cache_mla_krope': nrm(ks[3], (DEPTH, DEC_BATCH, PAST_LEN, A_ROPE), 1.0),
        'cache_sb_k': nrm(ks[4], (DEPTH, DEC_BATCH, PAST_LEN, H_B, D_B), 1.0),
        'cache_sb_v': nrm(ks[5], (DEPTH, DEC_BATCH, PAST_LEN, H_B, D_B), 1.0),
        'cache_dsa_k': nrm(ks[6], (DEPTH, DEC_BATCH, PAST_LEN, D_C), 1.0),
        'cache_dsa_v': nrm(ks[7], (DEPTH, DEC_BATCH, PAST_LEN, D_C), 1.0),
        'cache_dsa_kidx': nrm(ks[8], (DEPTH, DEC_BATCH, PAST_LEN, D_IDX), 1.0),
        'rel_bias': nrm(ks[9], (NUM_BUCKETS, H_C), 0.3),
        'ffn_pre_gain': gain(ks[10], (DEPTH, 2, D_MODEL)),
        'w_ffn_up': nrm(ks[11], (DEPTH, 2, D_MODEL, 2 * D_FF), D_MODEL ** -0.5),
        'w_ffn_down': nrm(ks[12], (DEPTH, 2, D_FF, D_MODEL), D_FF ** -0.5),
        'ffn_post_gain': gain(ks[13], (DEPTH, 2, D_MODEL)),
        'mix_pre_gain': gain(ks[14], (DEPTH, D_MODEL)),
        'w_in': nrm(ks[15], (DEPTH, D_MODEL, N_IN), D_MODEL ** -0.5),
        'mla_q_norm': gain(ks[16], (DEPTH, Q_LORA)),
        'w_mla_uq': nrm(ks[17], (DEPTH, Q_LORA, H_A * (A_NOPE + A_ROPE)), Q_LORA ** -0.5),
        'mla_kv_norm': gain(ks[18], (DEPTH, KV_LORA)),
        'w_mla_ukv': nrm(ks[19], (DEPTH, KV_LORA, H_A * (A_NOPE + A_V)), KV_LORA ** -0.5),
        'w_branch': nrm(ks[20], (DEPTH, N_BRANCH, MIX_W, D_MODEL), MIX_W ** -0.5),
        'w_o': nrm(ks[21], (DEPTH, D_MODEL, D_MODEL), D_MODEL ** -0.5),
        'mix_post_gain': gain(ks[22], (DEPTH, D_MODEL)),
    }

def reference(x_prompt, x_sample, cache_mla_ckv, cache_mla_krope, cache_sb_k, cache_sb_v,
              cache_dsa_k, cache_dsa_v, cache_dsa_kidx, rel_bias,
              ffn_pre_gain, w_ffn_up, w_ffn_down, ffn_post_gain,
              mix_pre_gain, w_in, mla_q_norm, w_mla_uq, mla_kv_norm, w_mla_ukv,
              w_branch, w_o, mix_post_gain):
    P = dict(ffn_pre_gain=ffn_pre_gain, w_ffn_up=w_ffn_up, w_ffn_down=w_ffn_down,
             ffn_post_gain=ffn_post_gain, mix_pre_gain=mix_pre_gain, w_in=w_in,
             mla_q_norm=mla_q_norm, w_mla_uq=w_mla_uq, mla_kv_norm=mla_kv_norm,
             w_mla_ukv=w_mla_ukv, w_branch=w_branch, w_o=w_o, mix_post_gain=mix_post_gain)
    y_prompt, (p_ckv, p_krope, p_sbk, p_sbv, p_dk, p_dv, p_dki) = trunk(x_prompt, None, P, rel_bias)
    caches = (cache_mla_ckv, cache_mla_krope, cache_sb_k, cache_sb_v,
              cache_dsa_k, cache_dsa_v, cache_dsa_kidx)
    past = [tuple(c[l] for c in caches) for l in range(DEPTH)]
    y_sample, (s_ckv, s_krope, s_sbk, s_sbv, s_dk, s_dv, s_dki) = trunk(x_sample, past, P, rel_bias)
    return (y_prompt, y_sample,
            p_ckv, p_krope, p_sbk, p_sbv, p_dk, p_dv, p_dki,
            s_ckv, s_krope, s_sbk, s_sbv, s_dk, s_dv, s_dki)


_drawn_inputs = setup_inputs


def setup_inputs(seed=0):
    import zlib

    import numpy as np

    out = dict(_drawn_inputs(seed))
    spreads = {}
    factors = {'mla_q_norm': 6.367, 'mla_kv_norm': 2.973}
    for name, (base, spread) in spreads.items():
        noise = np.random.default_rng([zlib.crc32(name.encode()), seed]).standard_normal(out[name].shape)
        drawn = base * np.exp(spread * noise) if base else spread * noise
        out[name] = __import__('jax').numpy.asarray(drawn.astype(out[name].dtype))
    for name, factor in factors.items():
        out[name] = (out[name] * factor).astype(out[name].dtype)
    return out
```

```python
import math
from contextlib import ExitStack

import numpy as np

import concourse.bass as bass
from concourse import mybir

F32 = mybir.dt.float32
F32R = mybir.dt.float32r
BF16 = mybir.dt.bfloat16
ALU = mybir.AluOpType
ACT = mybir.ActivationFunctionType
AX_X = mybir.AxisListType.X

P = 128
DEPTH, D, D_FF = 2, 1024, 2816
SEQ, NEW, PAST = 512, 32, 256
TOK = SEQ + NEW
HALF = TOK // 2
NKEY = SEQ + PAST + NEW
KEY_NEW = SEQ + PAST
CHUNK, QB = 64, 128
NBLK = SEQ // QB
H, DH, ROPE = 8, 64, 32
Q_LORA, KV_LORA = 384, 256
MIX = H * DH
KD, KF = D // P, D_FF // P
KQ, KKV = Q_LORA // P, KV_LORA // P
EPS = 1e-6
TOPK = min(256, SEQ // 4)
TOPK_S = min(256, (PAST + NEW) // 4)
BIG = 1.0e30
LOWEST = -3.0e38
SCALE_A = (64 + 32) ** -0.5
SCALE_C = DH ** -0.5
SCALE_I = DH ** -0.5 * H ** -0.5
NREL = 640
W_S = PAST + NEW

SLOT = 2048
NSLOT = 4
CH_FFN = KF + 2 * KD
CH_MIX = 48
CH_LAYER = 2 * CH_FFN + CH_MIX
assert CH_LAYER % NSLOT == 0
CH_A, CH_M, CH_B = 0, CH_FFN, CH_FFN + CH_MIX

PC_FFN = 2 * KF + 2 * KD
PC_A, PC_B = 0, PC_FFN
PC_LAYER = 2 * PC_FFN
PIECE = 1408

T_FFN = (2 * KF + KD) // 2
T_MIX = 51
T_LAYER = 2 * T_FFN + T_MIX
T_A, T_M, T_B = 0, T_FFN, T_FFN + T_MIX

NORMS = {"pre_a": (0, 0, 8), "post_a": (1, 8, 8), "mix": (2, 16, 8), "q": (3, 24, 3), "kv": (4, 27, 2),
         "mix_post": (5, 29, 8), "pre_b": (6, 37, 8), "post_b": (7, 45, 8)}
N_NORM, N_SQ = 8, 53

UNITS = [(p, s, e) for p in range(4) for s in range(NBLK) for e in range(2)] + [(4, 4, 0), (4, 4, 1)]
N_UNIT = 2 * len(UNITS)
N_PAIR = 10
N_B = H * NBLK
MASK_AT = [0, 128, 384, 768, 1280]
MASK_W = [128, 256, 384, 512, W_S]
ACC_AT = {1: 0, 2: 256, 3: 640, 4: 1152}


def mixer_tiles():
    t = ["kI"] + [f"qI{i}" for i in range(4)] + ["kC"] + [f"v{i}" for i in range(5)]
    t += [f"qC{i}" for i in range(4)] + [f"qB{i}" for i in range(4)] + [f"kB{i}" for i in range(4)]
    t += ["kr", "krs"] + [f"ql{i}" for i in range(KQ)] + [f"kv{i}" for i in range(KKV)]
    t += [f"uq{i}" for i in range(4)] + ["qr0", "qs0", "qr1", "qs1"]
    t += [f"kA{i}" for i in range(4)] + [f"vA{i}" for i in range(4)]
    for n in range(KD):
        t += [f"g0_{n}", f"b0_{n}", f"g1_{n}", f"b1_{n}", f"g2_{n}", f"b2_{n}"]
    return t + [f"wo{n}" for n in range(KD)]


TILES = mixer_tiles()
assert len(TILES) == 2 * T_MIX
TILE = {name: i for i, name in enumerate(TILES)}
MIX_CHUNKS = ([("w_in", i, 2048, TILES[2 * i + 1]) for i in range(3)]
              + [("w_vb", 0, 2048, "v4"), ("w_vb", 1, 2048, "v4"), ("w_vc", 0, 576, "v4")]
              + [("w_in", 3 + i, 2048 if i < 9 else 1024, TILES[min(12 + 2 * i, 29)]) for i in range(10)]
              + [("w_uq", 0, 1536, "uq3"), ("w_uq", 1, 1536, "qs1"), ("w_ukn", 0, 1024, "kA3"), ("w_ukv", 0, 1024, "vA3")]
              + [("w_mg", 3 * n + b, 1536, f"b{b}_{n}") for n in range(KD) for b in range(3)]
              + [("w_out", i, 2048, f"wo{2 * i + 1}") for i in range(4)])
assert len(MIX_CHUNKS) == CH_MIX


def build(nc, d):
    with ExitStack() as ctx:
        def sb(name, shape, dt=F32):
            return ctx.enter_context(nc.sbuf_tensor(name, shape, dt))

        def sem(name):
            return ctx.enter_context(nc.semaphore(name))

        PS = ctx.enter_context(nc.psum_tensor("PS", [P, 8, 512], F32))
        xT = sb("xT", [P, KD, TOK])
        uT_at = nc.sbuf_base
        uT = sb("uT", [P, KD, SEQ + P])
        uT_r = nc.alloc_sbuf_tensor_at("uT_r", [P, KD, SEQ + P], F32R, offset=uT_at)
        ring_at = nc.sbuf_base
        ring = sb("ring", [P, NSLOT, SLOT])
        ring_r = nc.alloc_sbuf_tensor_at("ring_r", [P, NSLOT, SLOT], F32R, offset=ring_at)
        cst = sb("cst", [P, 6, P])
        ropes = sb("ropes", [P, 2, TOK])
        gain = sb("gain", [P, DEPTH, N_SQ])
        g_now = sb("g_now", [P, N_SQ])
        sq = sb("sq", [P, 2, TOK])
        rstd = sb("rstd", [P, TOK])
        eps_c = sb("eps_c", [P, 1])
        m8 = sb("m8", [P, 8])
        cnt = sb("cnt", [P, 4])
        mx = sb("mx", [P, 2])
        nbias = sb("nbias", [P, 2])
        sums = sb("sums", [P, 2, 8])
        rinv = sb("rinv", [P, 2, 8])
        ARENA = 28472 + 3100
        arena_at = nc.sbuf_base
        arena = sb("arena", [P, ARENA])

        ones, neg_ones, neg_tri, ident, sb_mask, chunk_mask = (cst[:, i, :] for i in range(6))

        def region_r(name, at, *shape):
            return nc.alloc_sbuf_tensor_at(name, [P, *shape], F32R, offset=arena_at + 4 * at)

        def region(at, *shape):
            n = int(np.prod(shape))
            v = arena[:, at:at + n]
            if len(shape) == 2:
                v = v.rearrange("p (a b) -> p a b", a=shape[0])
            return v

        act_h = region_r("act_h", 0, KF, TOK)
        act_l = region_r("act_l", KF * TOK, KF, TOK)
        y_f = region(2 * KF * TOK, KD, TOK)
        u_l = region_r("u_l", 2 * KF * TOK, KD, TOK)
        piece_h = region_r("piece_h", (ARENA - 2 * PIECE) // 8 * 8, 2, PIECE)
        qI = region(0, 4, SEQ + P)
        qAn = region(0, 4, TOK)
        kI = region(2560, NKEY)
        VB = region(3360, 7, 512)
        VC = region(6944, 7, DH)
        wI = region(7392, 5, H)
        kC = region(7432, NKEY)
        qC = region(8232, 4, TOK)
        qB = region(10408, 4, TOK)
        kB = region(12584, 4, NKEY)
        kr = region(15784, NKEY)
        qAr = region(16584, 2, TOK)
        kA = region(17672, 4, NKEY)
        VA = region(20872, 7, 512)
        msk = arena[:, 24456:24456 + 784].bitcast(BF16)
        WK = 25240
        ql = region(WK, KQ, TOK)
        ckv = region(WK + KQ * TOK, KKV, NKEY)
        XW = WK + KQ * TOK + KKV * NKEY
        gate_s = sq
        kr_raw = region(XW, 2, TOK)
        rope_t = region(XW + 2 * TOK, TOK)
        acc = region(17672, 1440)
        topw = region(17672 + 1440, 512)
        eqv = region(17672 + 1952, 512)
        cum = region(17672 + 2464, 512)
        rel = region(20872, 2, 512)
        sb_sp = region(WK, 2, 1280)
        sb_a = region(WK + 2560, 2, 1280)
        sb_e = region(WK + 5120, 2, 512)
        prob = region(WK, 2, 512)
        probT = region(WK + 1024, 2, 512)
        OT = region(WK + 2048, 2, 512)
        T5 = region(WK + 3072, 4, 512)
        T5s = region(WK + 5120, 2, W_S)
        assert WK + 6332 <= ARENA
        topw_tab = region(0, NREL)
        onehot = region(NREL, NREL)
        relb = region(2 * NREL, H)
        merged = region(17672, KD, TOK)
        y_m = region(3360, KD, TOK)
        sig = region(WK, 2, TOK)
        mt = region(WK + 2 * TOK, 2, TOK)

        S = {n: sem(n) for n in (
            "consts_in", "x_in", "gain_in", "table_out", "table_in", "gain_now", "xnew", "hready", "sq_ready", "sq_used",
            "root", "inv", "yscaled", "cache_in", "rows_out", "y_out", "idx_done", "idx_rel", "idx_acc",
            "sel_ready", "lat_ready", "rope_step", "qr_ready", "dve_step", "act_step", "sb_done", "sb_soft",
            "sb_sp_ready", "sb_cum", "sb_a_ready", "sb_pv", "sb_out", "s_done", "bias_ready", "probs_ready",
            "pt_done", "pt_copied", "pv_done", "heads_normed", "ot_done", "branch_out", "t5_in01", "t5_in2", "t5_in3", "t5s_in",
            "merge_ready", "merge_step", "init_ready", "tab_ps", "tab_sb", "u_norm", "u_high",
            "w_high", "w_low", "half_read", "gate_step")}
        done = [sem("tile_done0"), sem("tile_done1")]
        vacated = [sem("tile_vacated0"), sem("tile_vacated1")]
        loaded = [sem(f"slot_loaded{i}") for i in range(NSLOT)]
        blk = ctx.enter_context(nc.Block())

        def alone(eng):
            eng.nop(nofuse=True)

        def unit(u):
            return PS[:, 2 * u:2 * u + 2, :]

        def turn_of(name):
            return T_M + TILE[name] // 2

        def keys(s):
            return (SEQ, W_S) if s == 4 else (0, QB * (s + 1))

        def key_tiles(s):
            k0, w = keys(s)
            return [(k0 + 128 * t, min(128, w - 128 * t), 128 * t, (4 + t) if s == 4 else t)
                    for t in range((w + 127) // 128)]

        def copy_probs(eng, copy, n0, i):
            eng.wait_ge(S["pt_done"], n0 + i + 3)
            eng.wait_ge(S["pv_done"], n0 + i + 1)
            tiles = key_tiles(UNITS[i][1])
            full = [t for t in tiles if t[1] == P]
            ins = copy(probT[:, i % 2, 0:P * len(full)], PS[:, 2 + i % 2, 0:P * len(full)])
            for _, m, at, _ in tiles[len(full):]:
                ins = copy(probT[0:m, i % 2, at:at + P], PS[0:m, 2 + i % 2, at:at + P])
            ins.then_inc(S["pt_copied"], 1)

        @blk.sync
        def _(sp):
            sp.dma_start(xT[:], d["x"]).then_inc(S["x_in"], 16)
            sp.dma_start(cst[:], d["cst"]).then_inc(S["consts_in"], 16)
            sp.dma_start(gain[:], d["gains"]).then_inc(S["gain_in"], 16)

            def load(src, n, ch):
                slot = ch % NSLOT
                sp.dma_start(ring[:, slot, 0:n], src).then_inc(loaded[slot], 16)

            def one(name, l, i):
                return d[name][bass.ds(l, 1), bass.ds(i, 1)].rearrange("l c p n -> p (l c n)")

            def consumed(l, u, turn):
                sp.wait_ge(done[u], l * T_LAYER + turn + 1)

            for f in range(NSLOT):
                load(one("w_up", 0, f), 2048, f)
            sp.dma_start(ropes[:], d["ropes"]).then_inc(S["consts_in"], 16)

            def ffn(l, ab, t0, c0, after):
                w0 = ab * KF
                with sp.Fori(0, 4) as i:
                    for j in range(4):
                        consumed(l, 1, t0 + i * 4 + j)
                        load(one("w_up", l, w0 + i * 4 + j + 4), 2048, c0 + j)
                for f in range(16, KF - 4):
                    consumed(l, 1, t0 + f)
                    load(one("w_up", l, w0 + f + 4), 2048, c0 + f)
                for f in range(KF - 4, KF):
                    consumed(l, 1, t0 + f)
                    load(one("w_dn", l, ab * 16 + f - KF + 4), 1408, c0 + f)
                with sp.Fori(0, 3) as i:
                    for j in range(4):
                        if j % 2 == 0:
                            consumed(l, j // 2, t0 + KF + i)
                        load(one("w_dn", l, ab * 16 + i * 4 + j + 4), 1408, c0 + KF + j)
                for j in range(4):
                    if j % 2 == 0:
                        consumed(l, j // 2, t0 + KF + 3)
                    after(j, c0 + KF + 12 + j)

            def mixer(l):
                for k in range(CH_MIX):
                    u, turn = TILE[MIX_CHUNKS[k][3]] % 2, turn_of(MIX_CHUNKS[k][3])
                    consumed(l, u, turn)
                    if k + NSLOT < CH_MIX:
                        name, i, n, _ = MIX_CHUNKS[k + NSLOT]
                        load(one(name, l, i)[:, 0:n], n, CH_M + k)
                    else:
                        load(one("w_up", l, KF + k + NSLOT - CH_MIX), 2048, CH_M + k)

            with sp.Fori(0, DEPTH) as l:
                ffn(l, 0, T_A, CH_A, lambda j, ch: load(one(MIX_CHUNKS[j][0], l, MIX_CHUNKS[j][1]), 2048, ch))
                mixer(l)
                ffn(l, 1, T_B, CH_B, lambda j, ch: load(one("w_up", l * -1 + (DEPTH - 1), j), 2048, ch))
            sp.wait_ge(S["xnew"], 8 + DEPTH * 24)
            sp.dma_start(d["y"], xT[:]).then_inc(S["y_out"], 16)
            sp.wait_ge(S["y_out"], 16)
            for i in range(NSLOT):
                sp.wait_ge(loaded[i], 16 * (DEPTH * CH_LAYER // NSLOT + 1))

        N_ROWS = 12
        N_CACHE = 7

        @blk.gpsimd
        def _(pool):
            pool.wait_ge(S["tab_sb"], 1)
            pool.dma_start(d["t5"], topw_tab[0:H, :].unsqueeze(1).broadcast_to([H, P, NREL])).then_inc(S["table_out"], 16)
            pool.wait_ge(S["table_out"], 16)

            def t5_sem(h):
                return "t5_in01" if h < 4 else f"t5_in{h // 2}"

            def toeplitz(h, rows, c0, n):
                return bass.AP(d["t5"].tensor, h * P * NREL + c0 + P - 1, [[NREL - 1, rows], [1, n]])

            def low(l, p0, i, ch, at, n, t=0):
                pool.wait_ge(S["w_high"], l * PC_LAYER + p0 + i + 1)
                hi, w = piece_h[:, ch[1], 0:n].bitcast(F32), ring[:, ch[0] % NSLOT, at:at + n]
                nc.gpsimd.tensor_tensor(ring_r[:, ch[0] % NSLOT, at:at + n], w, hi, ALU.subtract).then_inc(S["w_low"], 1)

            def ffn(l, p0, c0):
                with pool.Fori(0, 5) as i:
                    for j in range(8):
                        low(l, p0, i * 8 + j, (c0 + j // 2, j % 2), (j % 2) * 1024, 1024)
                for j in range(40, 2 * KF):
                    low(l, p0, j, (c0 + j // 2, j % 2), (j % 2) * 1024, 1024)
                for j in range(2 * KD):
                    low(l, p0, 2 * KF + j, (c0 + KF + j, j % 2), 0, PIECE)

            with pool.Fori(0, DEPTH) as l:
                ffn(l, PC_A, CH_A)

                def cached(dst, name):
                    pool.dma_start(dst, d[name][bass.ds(l, 1)].rearrange(
                        "l p a b -> p (l a) b" if len(dst.shape) == 3 else "l p a b -> p (l a b)")).then_inc(S["cache_in"], 16)

                pool.wait_ge(S["xnew"], l * 24 + 16)
                alone(pool)
                cached(kI[:, SEQ:KEY_NEW], "c_kidx")
                cached(kC[:, SEQ:KEY_NEW], "c_dsk")
                cached(VC[:, 4:6, :], "c_dsv")
                cached(kB[:, :, SEQ:KEY_NEW], "c_sbk")
                cached(VB[:, 4:6, :], "c_sbv")
                cached(kr[:, SEQ:KEY_NEW], "c_kr")
                cached(ckv[:, :, SEQ:KEY_NEW], "c_ckv")

                def row(name, src):
                    dst = d[name][bass.ds(l, 1)]
                    dst = dst.rearrange("l p a b -> p (l a) b" if len(src.shape) == 3 else "l p a b -> p (l a b)")
                    pool.dma_start(dst, src).then_inc(S["rows_out"], 16)

                def evacuated(name):
                    pool.wait_ge(vacated[TILE[name] % 2], l * T_LAYER + turn_of(name) + 3)
                    alone(pool)

                evacuated("kI")
                row("p_ki", kI[0:DH, 0:SEQ])
                row("s_ki", kI[0:DH, KEY_NEW:NKEY])
                evacuated("v4")
                evacuated("kC")
                row("p_kc", kC[0:DH, 0:SEQ])
                row("s_kc", kC[0:DH, KEY_NEW:NKEY])
                row("p_vb", VB[:, 0:4, :])
                row("s_vb", VB[0:NEW, 6, :])
                row("p_vc", VC[:, 0:4, :])
                row("s_vc", VC[0:NEW, 6, :])
                evacuated("kB3")
                evacuated("kB2")
                row("p_kb", kB[:, :, 0:SEQ])
                row("s_kb", kB[:, :, KEY_NEW:NKEY])
                pool.wait_ge(S["rope_step"], l * 3 + 3)
                alone(pool)
                pool.dma_start(d["o_kr"][bass.ds(l, 1)].rearrange("l p b -> p (l b)")[:, 0:SEQ], kr[0:ROPE, 0:SEQ]).then_inc(S["rows_out"], 16)
                pool.dma_start(d["o_kr"][bass.ds(l, 1)].rearrange("l p b -> p (l b)")[:, SEQ:TOK], kr[0:ROPE, KEY_NEW:NKEY]).then_inc(S["rows_out"], 16)
                pool.wait_ge(S["lat_ready"], l * 7 + 7)
                alone(pool)
                row("p_ckv", ckv[:, :, 0:SEQ])
                row("s_ckv", ckv[:, :, KEY_NEW:NKEY])
                pool.wait_ge(S["sb_out"], l * 5 + 5)
                alone(pool)
                for h in range(4):
                    pool.dma_start(T5[:, h, :], toeplitz(h, P, 0, 512)).then_inc(S[t5_sem(h)], 16)
                for h in range(H):
                    j, g = h % 4, h // 4
                    pool.dma_start(T5s[32 * j:32 * j + 32, g, :], toeplitz(h, NEW, 128, W_S)).then_inc(S["t5s_in"], 16)
                for h in range(4, H):
                    pool.wait_ge(S["bias_ready"], l * N_UNIT + 34 + 8 * ((h - 4) // 2 + 1))
                    alone(pool)
                    pool.dma_start(T5[:, h % 4, :], toeplitz(h, P, 0, 512)).then_inc(S[t5_sem(h)], 16)
                ffn(l, PC_B, CH_B)
            pool.wait_ge(S["rows_out"], 16 * 14 * DEPTH)

        @blk.tensor
        def _(pe):
            mm = nc.tensor.matmul
            pe.sem_inc(vacated[0], 2)
            pe.sem_inc(vacated[1], 2)
            pe.sem_inc(S["sq_used"], 2)
            pe.sem_inc(S["root"], 1)
            for n in ("idx_rel", "idx_acc", "probs_ready", "pt_done", "pt_copied", "pv_done", "heads_normed",
                      "ot_done", "branch_out"):
                pe.sem_inc(S[n], 2)
            pe.sem_inc(S["sb_a_ready"], 4)
            pe.sem_inc(S["sb_pv"], 2)

            pe.wait_ge(S["table_in"], 32)
            for c in range(2):
                last = mm(PS[0:H, c, 0:320], relb[0:32, :], onehot[0:32, 320 * c:320 * c + 320], start=True, stop=True)
            last.then_inc(S["tab_ps"], 1)
            pe.wait_ge(S["tab_sb"], 1)
            pe.wait_ge(S["consts_in"], 32)

            def chunk(l, ch, i=0):
                pe.wait_ge(loaded[ch % NSLOT], (l * (CH_LAYER // NSLOT) + ch // NSLOT + i + 1) * 16)
                return ring[:, ch % NSLOT, :]

            def open_tile(l, u, turn):
                pe.wait_ge(vacated[u], l * T_LAYER + turn + 2)

            def product(u, steps, n=(0, HALF, TOK), first=True, last=True, m=P):
                ins = None
                for s, (w, x) in enumerate(steps):
                    for b in range(2):
                        ins = mm(PS[0:m, 2 * u + b, 0:n[b + 1] - n[b]], w, x[:, n[b]:n[b + 1]],
                                 start=first and s == 0, stop=last and s == len(steps) - 1)
                if last:
                    ins.then_inc(done[u], 1)

            def square_sum(l, norm, k):
                j, q0, K = NORMS[norm]
                if k == 0:
                    pe.wait_ge(S["root"], l * N_NORM + j + 1)
                pe.wait_ge(S["sq_ready"], l * N_SQ + q0 + k + 1)
                for b in range(2):
                    ins = mm(PS[:, 4 + b, 0:HALF], ones, sq[:, k % 2, HALF * b:HALF * b + HALF],
                             start=k == 0, stop=k == K - 1)
                ins.then_inc(S["sq_used"], 1)

            def square_sum_at(l, q0, expr, k2):
                pe.wait_ge(S["sq_ready"], l * N_SQ + q0 + expr + 1)
                for b in range(2):
                    ins = mm(PS[:, 4 + b, 0:HALF], ones, sq[:, k2, HALF * b:HALF * b + HALF], start=False, stop=False)
                ins.then_inc(S["sq_used"], 1)

            def split_product(l, u, piece, hs, w_l, x_h, x_l, first=True, last=True, step=None):
                K = len(x_h)
                pe.wait_ge(S["w_high"], piece + 1)
                for k in range(K):
                    if step:
                        step(k)
                    w = piece_h[:, hs, k * P:(k + 1) * P]
                    for n, x in enumerate((x_h, x_l)):
                        for b in range(2):
                            mm(PS[:, 2 * u + b, 0:HALF], w, x[k][:, HALF * b:HALF * b + HALF],
                               start=first and k == 0 and n == 0, stop=False)
                pe.wait_ge(S["w_low"], piece + 1)
                for k in range(K):
                    for b in range(2):
                        ins = mm(PS[:, 2 * u + b, 0:HALF], w_l[:, k * P:(k + 1) * P], x_h[k][:, HALF * b:HALF * b + HALF],
                                 start=False, stop=last and k == K - 1)
                ins.then_inc(done[u] if last else S["half_read"], 1)

            def ffn(l, t0, c0, p0, pre, post, h0):
                for k in range(KD):
                    square_sum(l, pre, k)
                u_h = [uT_r[:, k, 0:TOK] for k in range(KD)]
                u_lo = [u_l[:, k, :] for k in range(KD)]

                def up(f, ch, step=None):
                    for g in range(2):
                        open_tile(l, g, t0 + f)
                        split_product(l, g, l * PC_LAYER + p0 + f * 2 + g, g, ring_r[:, ch % NSLOT, g * 1024:g * 1024 + 1024],
                                      u_h, u_lo, step=step if g == 0 else None)

                def input_ready(k):
                    pe.wait_ge(S["hready"], l * 25 + h0 + k + 1)

                up(0, c0, input_ready)
                alone(pe)
                with pe.Fori(0, 5) as i:
                    for j in range(4):
                        up(i * 4 + j + 1, c0 + j + 1)
                up(KF - 1, c0 + KF - 1)
                pe.wait_ge(vacated[1], l * T_LAYER + t0 + KF + 2)

                def down(u, turn, n, ch):
                    open_tile(l, u, turn)
                    for kh in range(2):
                        split_product(l, u, l * PC_LAYER + p0 + 2 * KF + n * 2 + kh, kh, ring_r[:, (ch + kh) % NSLOT, :],
                                      [act_h[:, 11 * kh + k, :] for k in range(11)], [act_l[:, 11 * kh + k, :] for k in range(11)],
                                      first=kh == 0, last=kh == 1)

                q0 = NORMS[post][1]
                down(0, t0 + KF, 0, c0 + KF)
                down(1, t0 + KF, 1, c0 + KF + 2)
                square_sum(l, post, 0)
                down(0, t0 + KF + 1, 2, c0 + KF + 4)
                square_sum(l, post, 1)
                alone(pe)
                with pe.Fori(0, 2) as i:
                    down(1, t0 + KF + 1 + i, i * 2 + 3, c0 + KF + 6)
                    square_sum_at(l, q0, 2 + i * 2, 0)
                    down(0, t0 + KF + 2 + i, i * 2 + 4, c0 + KF + 8)
                    square_sum_at(l, q0, 3 + i * 2, 1)
                down(1, t0 + KF + 3, 7, c0 + KF + 14)
                square_sum(l, post, 6)
                square_sum(l, post, 7)

            def mixer(l):
                for k in range(KD):
                    square_sum(l, "mix", k)
                pe.wait_ge(S["hready"], l * 25 + 17)
                ch = CH_M

                def tile(name, steps, **kw):
                    t = TILE[name]
                    open_tile(l, t % 2, T_M + t // 2)
                    product(t % 2, steps, **kw)

                u_steps = lambda w, at: [(w[:, at + k * P:at + (k + 1) * P], uT[:, k, 0:TOK]) for k in range(KD)]
                for i in range(3):
                    w = chunk(l, ch + i)
                    for e in range(2):
                        tile(TILES[2 * i + e], u_steps(w, e * 1024))
                wb = [chunk(l, ch + 3), chunk(l, ch + 4)]
                wc = chunk(l, ch + 5)
                for s in range(5):
                    t = TILE[f"v{s}"]
                    u = t % 2
                    open_tile(l, u, T_M + t // 2)
                    for k in range(KD):
                        tok = uT[:, k, P * s:P * s + P]
                        mm(PS[:, 2 * u, :], tok, wb[k // 4][:, (k % 4) * 512:(k % 4) * 512 + 512], start=k == 0, stop=k == KD - 1)
                        ins = mm(PS[:, 2 * u + 1, 0:72], tok, wc[:, k * 72:k * 72 + 72], start=k == 0, stop=k == KD - 1)
                    ins.then_inc(done[u], 1)
                pe.wait_ge(S["cache_in"], (l * N_CACHE + N_CACHE) * 16)
                pe.wait_ge(vacated[0], l * T_LAYER + turn_of("v3" if TILE["v3"] % 2 == 0 else "v4") + 3)
                pe.wait_ge(vacated[1], l * T_LAYER + turn_of("v4" if TILE["v4"] % 2 else "v3") + 3)
                i = 0
                for s in range(1, 5):
                    k0, w = keys(s)
                    for h in range(H):
                        r = 64 * (h % 2)
                        pe.wait_ge(S["idx_rel"], l * 32 + i + 1)
                        mm(PS[:, 6 + i % 2, 0:w], qI[r:r + 64, h // 2, P * s:P * s + P], kI[r:r + 64, k0:k0 + w],
                           start=True, stop=True).then_inc(S["idx_done"], 1)
                        i += 1
                for i in range(10):
                    w = chunk(l, ch + 6 + i)
                    for e in range(2 if i < 9 else 1):
                        name = TILES[11 + 2 * i + e]
                        tile(name, u_steps(w, e * 1024))
                        if name in ("ql1", "ql2", "kv0"):
                            square_sum(l, "q", ("ql1", "ql2", "kv0").index(name))
                for k in range(KKV):
                    square_sum(l, "kv", k)
                pe.wait_ge(S["lat_ready"], l * 7 + 3)
                for i in range(8):
                    w = chunk(l, ch + 16 + i // 4)
                    at = (i % 4) * KQ * P
                    tile(TILES[30 + i], [(w[:, at + k * P:at + k * P + P], ql[:, k, :]) for k in range(KQ)])
                pe.wait_ge(S["lat_ready"], l * 7 + 7)
                w = chunk(l, ch + 18)
                for i in range(4):
                    tile(f"kA{i}", [(w[:, (i * KKV + k) * P:(i * KKV + k + 1) * P], ckv[:, k, :]) for k in range(KKV)],
                         n=(0, NKEY // 2, NKEY))
                w = chunk(l, ch + 19)
                for i in range(4):
                    t = TILE[f"vA{i}"]
                    u = t % 2
                    open_tile(l, u, T_M + t // 2)
                    for b in range(2 if i < 3 else 1):
                        kt = 2 * i + b
                        m = P if kt < 6 else NEW
                        for k in range(KKV):
                            ins = mm(PS[0:m, 2 * u + b, :], ckv[:, k, P * kt:P * kt + m], w[:, k * 512:k * 512 + 512],
                                     start=k == 0, stop=k == KKV - 1)
                    ins.then_inc(done[u], 1)
                for name in ("vA2", "vA3"):
                    pe.wait_ge(vacated[TILE[name] % 2], l * T_LAYER + turn_of(name) + 3)
                pe.wait_ge(S["qr_ready"], l * 2 + 2)
                pe.wait_ge(S["rows_out"], 16 * (l * 14 + 14))
                branch_b(l)
                attend(l, 0)
                attend(l, 1)
                pe.wait_ge(S["branch_out"], l * N_PAIR + N_PAIR + 2)
                alone(pe)
                with pe.Fori(0, 2) as i:
                    for j in range(4):
                        for b in range(3):
                            c = 3 * j + b
                            w = chunk(l, ch + 20 + c, i * 3)
                            turn = turn_of("g0_0") + 3 * j + b + i * 12
                            open_tile(l, 0, turn)
                            product(0, u_steps(w, 0))
                            open_tile(l, 1, turn)
                            o = (qAn, qB, qC)[b]
                            product(1, [(w[:, 1024 + k * P:1024 + k * P + P], o[:, k, :]) for k in range(4)])
                pe.wait_ge(S["merge_ready"], l * KD + KD)
                for n in range(KD):
                    w = chunk(l, ch + 44 + n // 2)
                    at = (n % 2) * 1024
                    tile(f"wo{n}", [(w[:, at + k * P:at + k * P + P], merged[:, k, :]) for k in range(KD)])
                    if n:
                        square_sum(l, "mix_post", n - 1)
                square_sum(l, "mix_post", KD - 1)

            def branch_b(l):
                def scores(t):
                    h, j = t // 4, 3 - t % 4
                    r, w = 64 * (h % 2), SEQ - P * j
                    pe.wait_ge(S["sb_a_ready"], l * (N_B + 3) + t + 1)
                    mm(PS[:, t % 4, 0:w], kB[r:r + 64, h // 2, P * j:P * j + P], qB[r:r + 64, h // 2, P * j:SEQ],
                       start=True, stop=False, skip_group_check=True)
                    mm(PS[:, t % 4, 0:P], ident, sb_mask, start=False, stop=True,
                       skip_group_check=True).then_inc(S["sb_done"], 1)

                def cumulate(t):
                    h, j = t // 4, 3 - t % 4
                    w = SEQ - P * j
                    pe.wait_ge(S["sb_sp_ready"], l * (N_B + 3) + t + 1)
                    for i in range(3, j, -1):
                        at = 128 * ((3 - i) * (4 - i) // 2)
                        wi = SEQ - P * i
                        mm(PS[:, t % 4, (i - j) * P:w], neg_ones, sb_sp[:, h % 2, at:at + wi], start=False, stop=False,
                           skip_group_check=True)
                    at = 128 * ((3 - j) * (4 - j) // 2)
                    mm(PS[:, t % 4, 0:w], neg_tri, sb_sp[:, h % 2, at:at + w], start=False, stop=True,
                       skip_group_check=True).then_inc(S["sb_cum"], 1)

                def values(h):
                    r = 64 * (h % 2)
                    pe.wait_ge(S["sb_a_ready"], l * (N_B + 3) + 4 * h + 8)
                    alone(pe)
                    if h % 2 == 0 and h >= 4:
                        pe.wait_ge(S["sb_out"], l * 5 + h // 2 - 1)
                    for j in range(4):
                        at = 128 * ((3 - j) * (4 - j) // 2)
                        ins = mm(PS[r:r + 64, 4 + (h // 2) % 2, P * j:SEQ], VB[:, j, DH * h:DH * h + DH],
                                 sb_a[:, h % 2, at:at + SEQ - P * j], start=j == 0, stop=j == 3, skip_group_check=True)
                    ins.then_inc(S["sb_pv"], 1)

                for t in range(N_B):
                    scores(t)
                    if t >= 2:
                        cumulate(t - 2)
                    if t >= 6 and (t - 6) % 4 == 0:
                        values((t - 6) // 4)
                cumulate(N_B - 2)
                cumulate(N_B - 1)
                values(H - 1)
                pe.wait_ge(S["sb_a_ready"], l * (N_B + 3) + N_B + 4)
                pe.wait_ge(S["sb_out"], l * 5 + 4)
                alone(pe)
                tiles = [(2, KEY_NEW, NEW), (1, SEQ + P, P), (0, SEQ, P)]
                for kt, k0, m in tiles:
                    for h in range(H):
                        r = 64 * (h % 2)
                        ins = mm(PS[0:m, 2 * kt + h % 2, 32 * (h // 2):32 * (h // 2) + 32], kB[r:r + 64, h // 2, k0:k0 + m],
                                 qB[r:r + 64, h // 2, SEQ:TOK], start=h < 2, stop=kt != 2, skip_group_check=True)
                    if kt == 2:
                        for b in range(2):
                            for j in range(4):
                                ins = mm(PS[0:m, 4 + b, 32 * j:32 * j + 32], ident[0:NEW, 0:NEW], sb_mask[0:NEW, 0:NEW],
                                         start=False, stop=True, skip_group_check=True)
                    ins.then_inc(S["sb_done"], 1)
                for n, (kt, k0, m) in enumerate(tiles):
                    pe.wait_ge(S["sb_sp_ready"], l * (N_B + 3) + N_B + n + 1)
                    alone(pe)
                    for b in range(2):
                        for n2 in range(n):
                            m2 = tiles[n2][2]
                            mm(PS[0:m, 2 * kt + b, 0:P], neg_ones[0:m2, 0:m], sb_sp[0:m2, 0, 256 * n2 + P * b:256 * n2 + P * b + P],
                               start=False, stop=False, skip_group_check=True)
                        ins = mm(PS[0:m, 2 * kt + b, 0:P], neg_tri[0:m, 0:m], sb_sp[0:m, 0, 256 * n + P * b:256 * n + P * b + P],
                                 start=False, stop=True, skip_group_check=True)
                    ins.then_inc(S["sb_cum"], 1)
                pe.wait_ge(S["sb_a_ready"], l * (N_B + 3) + N_B + 3 + 4)
                alone(pe)
                for h in range(H):
                    r = 64 * (h % 2)
                    for n in (2, 1, 0):
                        kt, k0, m = tiles[n]
                        ins = mm(PS[r:r + 64, 6, 32 * (h // 2):32 * (h // 2) + 32], VB[0:m, 4 + kt, DH * h:DH * h + DH],
                                 sb_a[0:m, 0, 256 * n + P * (h % 2) + 32 * (h // 2):256 * n + P * (h % 2) + 32 * (h // 2) + 32],
                                 start=n == 2, stop=n == 0, skip_group_check=True)
                ins.then_inc(S["sb_pv"], 1)
                pe.wait_ge(S["sb_out"], l * 5 + 5)

            def attend(l, c):
                V = (VA, VC)[c]
                n0, q0 = l * N_UNIT + c * 34, l * N_PAIR + 5 * c

                def scores(i):
                    p, s, e = UNITS[i]
                    k0, w = keys(s)
                    pe.wait_ge(S["probs_ready"], n0 + i + 1)
                    if s == 4:
                        alone(pe)
                    bank = i % 2
                    if s < 4:
                        h = 2 * p + e
                        r, r4 = 64 * e, 32 * (h % 4)
                        out = PS[:, bank, 0:w]
                        if c == 0:
                            mm(out, qAr[r4:r4 + 32, h // 4, P * s:P * s + P], kr[r4:r4 + 32, 0:w], start=True, stop=False,
                               skip_group_check=True)
                            mm(out, qAn[r:r + 64, p, P * s:P * s + P], kA[r:r + 64, p, 0:w], start=False, stop=False,
                               skip_group_check=True)
                            mm(PS[:, bank, w - P:w], ident, chunk_mask, start=False, stop=True,
                               skip_group_check=True).then_inc(S["s_done"], 1)
                        else:
                            mm(out, qC[r:r + 64, p, P * s:P * s + P], kC[r:r + 64, 0:w], start=True,
                               stop=True).then_inc(S["s_done"], 1)
                        return
                    for j in range(4):
                        h = 4 * e + j
                        r = 64 * (h % 2)
                        out = PS[32 * j:32 * j + 32, bank, 0:w]
                        if c == 0:
                            mm(out, qAn[r:r + 64, h // 2, SEQ:TOK], kA[r:r + 64, h // 2, k0:k0 + w], start=True, stop=False,
                               skip_group_check=True)
                        else:
                            ins = mm(out, qC[r:r + 64, h // 2, SEQ:TOK], kC[r:r + 64, k0:k0 + w], start=True, stop=True)
                    if c == 0:
                        for j in range(4):
                            out = PS[32 * j:32 * j + 32, bank, 0:w]
                            ins = mm(out, qAr[32 * j:32 * j + 32, e, SEQ:TOK], kr[32 * j:32 * j + 32, k0:k0 + w], start=False,
                                     stop=True, skip_group_check=True)
                    ins.then_inc(S["s_done"], 1)

                def transposes(i):
                    pe.wait_ge(S["probs_ready"], n0 + i + 3)
                    pe.wait_ge(S["pt_copied"], n0 + i + 1)
                    alone(pe)
                    for _, m, at, _ in key_tiles(UNITS[i][1]):
                        ins = nc.tensor.transpose(PS[0:m, 2 + i % 2, at:at + P], prob[:, i % 2, at:at + m], ident)
                    ins.then_inc(S["pt_done"], 1)

                def values(i):
                    p, s, e = UNITS[i]
                    pe.wait_ge(S["pt_copied"], n0 + i + 3)
                    if (s, e) in ((0, 0), (4, 0)):
                        pe.wait_ge(S["heads_normed"], q0 + p + 1)
                    if s == 4:
                        alone(pe)
                    bank = 4 + (5 * c + p) % 2
                    tiles = key_tiles(s)
                    for j in range(1 if s < 4 else 4):
                        h = 2 * p + e if s < 4 else 4 * e + j
                        out = PS[:, bank, P * s + DH * e:P * s + DH * e + DH] if s < 4 else PS[32 * j:32 * j + 32, bank, DH * e:DH * e + DH]
                        hv = DH * h if c == 0 else 0
                        for n, (_, m, at, vt) in enumerate(tiles):
                            pt = probT[0:m, i % 2, at:at + P] if s < 4 else probT[0:m, i % 2, at + 32 * j:at + 32 * j + 32]
                            ins = mm(out, pt, V[0:m, vt, hv:hv + DH], start=n == 0, stop=n == len(tiles) - 1)
                    ins.then_inc(S["pv_done"], 1)

                def turn_pair(p):
                    q = 5 * c + p
                    pe.wait_ge(S["heads_normed"], q0 + p + 3)
                    pe.wait_ge(S["branch_out"], q0 + p + 1)
                    alone(pe)
                    if p < 4:
                        for s in range(NBLK):
                            ins = nc.tensor.transpose(PS[:, 6 + q % 2, P * s:P * s + P], OT[:, q % 2, P * s:P * s + P], ident)
                    else:
                        for e in range(2):
                            ins = nc.tensor.transpose(PS[0:DH, 6 + q % 2, P * e:P * e + P], OT[:, q % 2, DH * e:DH * e + DH], ident)
                    ins.then_inc(S["ot_done"], 1)

                n = len(UNITS)
                ends = {7: 0, 15: 1, 23: 2, 31: 3, 33: 4}
                if c == 0:
                    pe.wait_ge(S["sb_out"], l * 5 + 5)
                for i in range(n + 3):
                    if i < n:
                        scores(i)
                    if 1 <= i <= n:
                        transposes(i - 1)
                    if 2 <= i <= n + 1:
                        values(i - 2)
                    if i - 3 in ends:
                        turn_pair(ends[i - 3])

            with pe.Fori(0, DEPTH) as l:
                ffn(l, T_A, CH_A, PC_A, "pre_a", "post_a", 0)
                mixer(l)
                ffn(l, T_B, CH_B, PC_B, "pre_b", "post_b", 17)

        N_ACT = 70

        @blk.scalar
        def _(act):
            A = nc.scalar.activation
            act.dma_start(onehot[0:32, :], d["onehot"]).then_inc(S["table_in"], 16)
            act.dma_start(relb[0:32, :], d["rel_bias"]).then_inc(S["table_in"], 16)
            act.wait_ge(S["tab_ps"], 1)
            A(topw_tab[0:H, :].rearrange("p (a b) -> p a b", a=2), PS[0:H, 0:2, 0:320], ACT.Copy).then_inc(S["tab_sb"], 1)
            act.wait_ge(S["init_ready"], 1)
            act.wait_ge(S["table_out"], 16)

            step = [0]

            def square(l, norm, k, src):
                act.wait_ge(S["sq_used"], l * N_SQ + NORMS[norm][1] + k + 1)
                A(sq[:, k % 2, :] if len(src.shape) == 2 else sq[:, k % 2, :].rearrange("p (a b) -> p a b", a=2),
                  src, ACT.Square).then_inc(S["sq_ready"], 1)

            def root(l, norm):
                j, q0, K = NORMS[norm]
                act.wait_ge(S["sq_used"], l * N_SQ + q0 + K + 2)
                A(rstd[:].rearrange("p (a b) -> p a b", a=2), unit(2)[:, :, 0:HALF], ACT.Sqrt, scale=1.0 / (K * P),
                  bias=eps_c[:]).then_inc(S["root"], 1)

            def pre_norm(l, norm, v):
                for k in range(KD):
                    act.wait_ge(S["xnew"], l * 24 + v * 8 + k + 1)
                    square(l, norm, k, xT[:, k, :])
                root(l, norm)

            def filled(l, u, turn):
                act.wait_ge(done[u], l * T_LAYER + turn + 1)

            def high(ch, i, hs, at, n, l):
                act.wait_ge(loaded[ch % NSLOT], (l * (CH_LAYER // NSLOT) + ch // NSLOT + i + 1) * 16)
                A(piece_h[:, hs, 0:n], ring[:, ch % NSLOT, at:at + n], ACT.Copy).then_inc(S["w_high"], 1)

            def ffn(l, t0, c0, pre, post, v):
                ab = v // 2
                high(c0, 0, 0, 0, 1024, l)
                high(c0, 0, 1, 1024, 1024, l)
                pre_norm(l, pre, v)
                q = l * 2 + ab
                for k in range(KD):
                    act.wait_ge(S["u_norm"], q * KD + k + 1)
                    A(uT_r[:, k, 0:TOK], y_f[:, k, :], ACT.Copy).then_inc(S["u_high"], 1)

                def silu(f, j):
                    act.wait_ge(vacated[1], l * T_LAYER + t0 + f + 1)
                    A(gate_s[:, j % 2, :].rearrange("p (a b) -> p a b", a=2), unit(0)[:, :, 0:HALF],
                      ACT.Silu).then_inc(vacated[0], 1)

                with act.Fori(0, 5) as i:
                    for j in range(4):
                        filled(l, 0, t0 + i * 4 + j)
                        high(c0 + j + 1, i, 0, 0, 1024, l)
                        silu(i * 4 + j, j)
                        filled(l, 1, t0 + i * 4 + j)
                        high(c0 + j + 1, i, 1, 1024, 1024, l)
                for f in (KF - 2, KF - 1):
                    filled(l, 0, t0 + f)
                    if f == KF - 2:
                        high(c0 + KF - 1, 0, 0, 0, 1024, l)
                    else:
                        high(c0 + KF, 0, 0, 0, PIECE, l)
                    silu(f, f)
                    filled(l, 1, t0 + f)
                    if f == KF - 2:
                        high(c0 + KF - 1, 0, 1, 1024, 1024, l)
                    else:
                        high(c0 + KF + 1, 0, 1, 0, PIECE, l)
                for n in range(KD):
                    u = n % 2
                    if n < KD - 1:
                        act.wait_ge(S["half_read"], q * KD + n + 1)
                        high(c0 + KF + 2 * n + 2, 0, 0, 0, PIECE, l)
                    filled(l, u, t0 + KF + n // 2)
                    if n < KD - 1:
                        high(c0 + KF + 2 * n + 3, 0, 1, 0, PIECE, l)
                    square(l, post, n, unit(u)[:, :, 0:HALF])
                    A(y_f[:, n, :].rearrange("p (a b) -> p a b", a=2), unit(u)[:, :, 0:HALF], ACT.Copy).then_inc(vacated[u], 1)
                root(l, post)

            def mixer(l):
                pre_norm(l, "mix", 1)

                def evac(name):
                    t = TILE[name]
                    u = t % 2
                    filled(l, u, T_M + t // 2)
                    return u

                def to_keys(name, dst):
                    u = evac(name)
                    A(dst[:, 0:HALF], PS[:, 2 * u, 0:HALF], ACT.Copy)
                    A(dst[:, HALF:SEQ], PS[:, 2 * u + 1, 0:SEQ - HALF], ACT.Copy)
                    A(dst[:, KEY_NEW:NKEY], PS[:, 2 * u + 1, SEQ - HALF:HALF], ACT.Copy).then_inc(vacated[u], 1)

                def to_queries(name, dst, scale=1.0):
                    u = evac(name)
                    A(dst.rearrange("p (a b) -> p a b", a=2), unit(u)[:, :, 0:HALF], ACT.Copy, scale=scale).then_inc(vacated[u], 1)

                to_keys("kI", kI)
                for i in range(4):
                    u = evac(f"qI{i}")
                    A(qI[:, i, 0:HALF], PS[:, 2 * u, 0:HALF], ACT.Copy)
                    A(qI[:, i, HALF:SEQ], PS[:, 2 * u + 1, 0:SEQ - HALF], ACT.Copy)
                    A(qI[:, i, SEQ:SEQ + P].rearrange("p (a b) -> p a b", a=4),
                      PS[:, 2 * u + 1, SEQ - HALF:HALF].unsqueeze(1).broadcast_to([P, 4, NEW]), ACT.Copy).then_inc(vacated[u], 1)
                to_keys("kC", kC)
                for s in range(5):
                    u = evac(f"v{s}")
                    kt = s if s < 4 else 6
                    A(VB[:, kt, :], PS[:, 2 * u, :], ACT.Copy)
                    A(VC[:, kt, :], PS[:, 2 * u + 1, 0:DH], ACT.Copy)
                    A(wI[:, s, :], PS[:, 2 * u + 1, DH:DH + H], ACT.Copy).then_inc(vacated[u], 1)
                i = 0
                for s in range(1, 5):
                    _, w = keys(s)
                    for h in range(H):
                        act.wait_ge(S["idx_done"], l * 32 + i + 1)
                        act.wait_ge(S["idx_acc"], l * 32 + i + 1)
                        A(rel[:, i % 2, 0:w], PS[:, 6 + i % 2, 0:w], ACT.Relu, scale=SCALE_I).then_inc(S["idx_rel"], 1)
                        i += 1
                for i in range(4):
                    to_queries(f"qC{i}", qC[:, i, :])
                for i in range(4):
                    to_queries(f"qB{i}", qB[:, i, :], scale=DH ** -0.5)
                for i in range(4):
                    to_keys(f"kB{i}", kB[:, i, :])
                to_queries("kr", kr_raw[:, 0, :])
                to_queries("krs", kr_raw[:, 1, :])
                for i in range(KQ):
                    u = evac(f"ql{i}")
                    square(l, "q", i, unit(u)[:, :, 0:HALF])
                    to_queries(f"ql{i}", ql[:, i, :])
                root(l, "q")
                for i in range(KKV):
                    u = evac(f"kv{i}")
                    square(l, "kv", i, unit(u)[:, :, 0:HALF])
                    to_keys(f"kv{i}", ckv[:, i, :])
                act.wait_ge(S["lat_ready"], l * 7 + 3)
                root(l, "kv")
                act.wait_ge(S["sel_ready"], l * 4 + 4)
                act.wait_ge(S["idx_done"], l * 32 + 32)
                for i in range(4):
                    to_queries(f"uq{i}", qAn[:, i, :])
                for i in range(4):
                    u = evac(f"kA{i}")
                    A(kA[:, i, :].rearrange("p (a b) -> p a b", a=2), unit(u)[:, :, 0:NKEY // 2], ACT.Copy).then_inc(vacated[u], 1)
                for i in range(4):
                    u = evac(f"vA{i}")
                    if i < 3:
                        A(VA[:, 2 * i:2 * i + 2, :], unit(u), ACT.Copy).then_inc(vacated[u], 1)
                    else:
                        A(VA[0:NEW, 6, :], PS[0:NEW, 2 * u, :], ACT.Copy).then_inc(vacated[u], 1)
                act.wait_ge(S["rows_out"], 16 * (l * 14 + 14))
                branch_b(l)
                attend(l, 0)
                attend(l, 1)
                with act.Fori(0, 2) as i:
                    for j in range(12):
                        turn = turn_of("g0_0") + j + i * 12
                        filled(l, 0, turn)
                        act.wait_ge(vacated[1], l * T_LAYER + turn + 1)
                        A(sig[:, j % 2, :].rearrange("p (a b) -> p a b", a=2), unit(0)[:, :, 0:HALF],
                          ACT.Sigmoid).then_inc(vacated[0], 1)
                for n in range(KD):
                    u = evac(f"wo{n}")
                    square(l, "mix_post", n, unit(u)[:, :, 0:HALF])
                    to_queries(f"wo{n}", y_m[:, n, :])
                root(l, "mix_post")

            def branch_b(l):
                nb = l * (N_B + 3)
                st = l * 70
                alone(act)
                act.preload_act_table_set("natural_log_exp_and_others")

                def soft(n, rows, src, e):
                    act.wait_ge(S["sb_done"], nb + n + 1)
                    if n >= 2:
                        act.wait_ge(S["sb_sp_ready"], nb + n - 1)
                    A(e, src, ACT.Abs).then_inc(S["act_step"], 1)
                    act.wait_ge(S["act_step"], st + 2 * n + 1)
                    A(e, e, ACT.Exp, scale=-1.0).then_inc(S["act_step"], 1)
                    act.wait_ge(S["act_step"], st + 2 * n + 2)
                    A(e, e, ACT.Ln, bias=1.0).then_inc(S["sb_soft"], 1)

                def weights(t):
                    h, j = t // 4, 3 - t % 4
                    w, at = SEQ - P * j, 128 * ((3 - j) * (4 - j) // 2)
                    act.wait_ge(S["sb_cum"], nb + t + 1)
                    if t % 4 == 0:
                        act.wait_ge(S["sb_pv"], l * 9 + h + 1)
                    A(sb_a[:, h % 2, at:at + w], PS[:, t % 4, 0:w], ACT.Exp).then_inc(S["sb_a_ready"], 1)

                def out_pair(p):
                    act.wait_ge(S["sb_pv"], l * 9 + 2 * p + 4)
                    A(qB[:, p, 0:SEQ], PS[:, 4 + p % 2, :], ACT.Copy).then_inc(S["sb_out"], 1)

                for t in range(N_B + 2):
                    if t < N_B:
                        w = P * (t % 4 + 1)
                        soft(t, P, PS[:, t % 4, 0:w], sb_e[:, t % 2, 0:w])
                    if t >= 2:
                        weights(t - 2)
                    if t % 8 == 7 and t >= 15:
                        out_pair(t // 8 - 1)
                out_pair(3)
                rows = [NEW, P, P]
                for n in range(3):
                    m = rows[n]
                    kt = 2 - n
                    soft(N_B + n, m, PS[0:m, 2 * kt:2 * kt + 2, 0:P],
                         sb_e[0:m, (N_B + n) % 2, 0:2 * P].rearrange("p (a b) -> p a b", a=2))
                for n in range(3):
                    m = rows[n]
                    kt = 2 - n
                    act.wait_ge(S["sb_cum"], nb + N_B + n + 1)
                    A(sb_a[0:m, 0, 256 * n:256 * n + 256].rearrange("p (a b) -> p a b", a=2), PS[0:m, 2 * kt:2 * kt + 2, 0:P],
                      ACT.Exp).then_inc(S["sb_a_ready"], 1)
                act.wait_ge(S["sb_pv"], l * 9 + 8 + 3)
                A(qB[:, :, SEQ:TOK], PS[:, 6, 0:P].rearrange("p (a b) -> p a b", a=4), ACT.Copy).then_inc(S["sb_out"], 1)

            def attend(l, c):
                n0, q0 = l * N_UNIT + c * 34, l * N_PAIR + 5 * c
                dst = (qAn, qC)[c]

                def softmax(i):
                    p, s, e = UNITS[i]
                    w = keys(s)[1]
                    q = 5 * c + p
                    act.wait_ge(S["bias_ready"], n0 + i + 1)
                    if (s, e) in ((0, 0), (4, 0)):
                        act.wait_ge(S["heads_normed"], q0 + p + 1)
                    if c == 0:
                        act.wait_ge(S["pt_done"], n0 + i + 1)
                        src = PS[:, i % 2, 0:w]
                    else:
                        src = prob[:, i % 2, 0:w]
                    col = 2 * s + e if s < 4 else e
                    A(prob[:, i % 2, 0:w], src, ACT.Exp, scale=SCALE_A if c == 0 else 1.0, bias=nbias[:, i % 2:i % 2 + 1],
                      accum_out=sums[:, q % 2, col:col + 1]).then_inc(S["probs_ready"], 1)

                def copy_t(i):
                    copy_probs(act, lambda o, x: A(o, x, ACT.Copy), n0, i)

                def out_pair(p):
                    q = 5 * c + p
                    act.wait_ge(S["ot_done"], q0 + p + 3)
                    if p < 4:
                        A(dst[:, p, 0:SEQ], PS[:, 6 + q % 2, :], ACT.Copy).then_inc(S["branch_out"], 1)
                        return
                    for e in range(2):
                        ins = A(dst[DH * e:DH * e + DH, :, SEQ:TOK],
                                PS[0:DH, 6 + q % 2, 0:2 * P].rearrange("p (a e b) -> p e a b", a=4, e=2)[:, e], ACT.Copy)
                    ins.then_inc(S["branch_out"], 1)

                n = len(UNITS)
                ends = {7: 0, 15: 1, 23: 2, 31: 3, 33: 4}
                for i in range(n + 3):
                    if i < n:
                        softmax(i)
                    if c == 1 and 1 <= i <= n:
                        copy_t(i - 1)
                    if i - 3 in ends:
                        out_pair(ends[i - 3])

            act.wait_ge(S["x_in"], 16)
            with act.Fori(0, DEPTH) as l:
                ffn(l, T_A, CH_A, "pre_a", "post_a", 0)
                mixer(l)
                ffn(l, T_B, CH_B, "pre_b", "post_b", 2)

        N_DVE = [None]

        @blk.vector
        def _(dve):
            V = nc.vector
            V.memset(eps_c[:], EPS).then_inc(S["init_ready"], 1)
            dve.wait_ge(S["x_in"], 16)
            dve.sem_inc(S["xnew"], 8)
            dve.wait_ge(S["gain_in"], 16)
            dve.wait_ge(S["consts_in"], 32)

            per = DVE_STEPS
            count = [0]

            def link(l, ins):
                count[0] += 1
                ins.then_inc(S["dve_step"], 1)
                dve.wait_ge(S["dve_step"], l * per + count[0])
                alone(dve)

            def invert(l, norm):
                j = NORMS[norm][0]
                dve.wait_ge(S["root"], l * N_NORM + j + 2)
                V.reciprocal(rstd[:], rstd[:]).then_inc(S["inv"], 1)
                dve.wait_ge(S["inv"], l * N_NORM + j + 1)

            def pre_norm(l, norm, dst_done):
                invert(l, norm)
                c0 = NORMS[norm][1]
                for k in range(KD):
                    V.scalar_tensor_tensor(out=uT[:, k, 0:TOK], in0=xT[:, k, :], scalar=g_now[:, c0 + k:c0 + k + 1], in1=rstd[:],
                                           op0=ALU.mult, op1=ALU.mult).then_inc(S["hready"], 1)

            def post_norm(l, norm, y, half, n_y):
                invert(l, norm)
                c0 = NORMS[norm][1]
                for k in range(KD):
                    V.scalar_tensor_tensor(out=y[:, k, :], in0=y[:, k, :], scalar=g_now[:, c0 + k:c0 + k + 1], in1=rstd[:],
                                           op0=ALU.mult, op1=ALU.mult).then_inc(S["yscaled"], 1)
                for k in range(KD):
                    dve.wait_ge(S["yscaled"], l * 24 + n_y * 8 + k + 1)
                    V.scalar_tensor_tensor(out=xT[:, k, :], in0=y[:, k, :], scalar=0.5 if half else 1.0, in1=xT[:, k, :],
                                           op0=ALU.mult, op1=ALU.add).then_inc(S["xnew"], 1)

            def filled(l, u, turn):
                dve.wait_ge(done[u], l * T_LAYER + turn + 1)

            def ffn(l, t0, pre, post, n_y):
                invert(l, pre)
                c0, q = NORMS[pre][1], l * 2 + n_y // 2

                def rest(k):
                    dve.wait_ge(S["u_high"], q * KD + k + 1)
                    V.tensor_tensor(u_l[:, k, :], y_f[:, k, :], uT_r[:, k, 0:TOK].bitcast(F32), ALU.subtract).then_inc(S["hready"], 1)

                for k in range(KD):
                    V.scalar_tensor_tensor(out=y_f[:, k, :], in0=xT[:, k, :], scalar=g_now[:, c0 + k:c0 + k + 1], in1=rstd[:],
                                           op0=ALU.mult, op1=ALU.mult).then_inc(S["u_norm"], 1)
                    if k:
                        rest(k - 1)
                rest(KD - 1)

                def gated(f, j):
                    filled(l, 1, t0 + f)
                    dve.wait_ge(vacated[0], l * T_LAYER + t0 + f + 3)
                    g, up = gate_s[:, j, :].rearrange("p (a b) -> p a b", a=2), unit(1)[:, :, 0:HALF]
                    hi = act_h[:, bass.ds(f, 1)].rearrange("p o n -> p (o n)")
                    lo = act_l[:, bass.ds(f, 1)].rearrange("p o n -> p (o n)")
                    V.tensor_tensor(hi.rearrange("p (a b) -> p a b", a=2), g, up, ALU.mult).then_inc(S["gate_step"], 1)
                    V.tensor_tensor(g, g, up, ALU.mult).then_inc(S["gate_step"], 1)
                    dve.wait_ge(S["gate_step"], q * 2 * KF + f * 2 + 2)
                    V.tensor_tensor(lo, gate_s[:, j, :], hi.bitcast(F32), ALU.subtract).then_inc(vacated[1], 1)

                with dve.Fori(0, KF // 2) as i:
                    gated(i * 2, 0)
                    gated(i * 2 + 1, 1)
                post_norm(l, post, y_f, True, n_y)

            def mixer(l):
                pre_norm(l, "mix", None)
                dve.wait_ge(S["hready"], l * 25 + 16)
                V.tensor_copy(uT[:, :, TOK:SEQ + P].rearrange("p k (a b) -> p k a b", a=3),
                              uT[:, :, SEQ:TOK].unsqueeze(2).broadcast_to([P, KD, 3, NEW])).then_inc(S["hready"], 1)
                i = 0
                for s in range(1, 5):
                    w = MASK_W[s]
                    a = acc[:, ACC_AT[s]:ACC_AT[s] + w]
                    for h in range(H):
                        dve.wait_ge(S["idx_rel"], l * 32 + i + 3)
                        if h == 0:
                            V.tensor_scalar(a, rel[:, i % 2, 0:w], wI[:, s, h:h + 1], None, ALU.mult).then_inc(S["idx_acc"], 1)
                        else:
                            dve.wait_ge(S["idx_acc"], l * 32 + i + 2)
                            V.scalar_tensor_tensor(out=a, in0=rel[:, i % 2, 0:w], scalar=wI[:, s, h:h + 1], in1=a, op0=ALU.mult,
                                                   op1=ALU.add).then_inc(S["idx_acc"], 1)
                        i += 1
                dve.wait_ge(S["idx_acc"], l * 32 + 34)
                for s in range(1, 4):
                    w = MASK_W[s]
                    ins = V.memset(acc[0:CHUNK, ACC_AT[s] + w - CHUNK:ACC_AT[s] + w], LOWEST)
                link(l, ins)
                link(l, V.memset(msk[:, 0:P], 0.0))
                link(l, V.memset(msk[0:CHUNK, CHUNK:P], -BIG))
                for s in range(1, 5):
                    select(l, s)
                rotate_keys(l)
                invert(l, "q")
                for k in range(KQ):
                    V.scalar_tensor_tensor(out=ql[:, k, :], in0=ql[:, k, :], scalar=g_now[:, 24 + k:25 + k], in1=rstd[:],
                                           op0=ALU.mult, op1=ALU.mult).then_inc(S["lat_ready"], 1)
                invert(l, "kv")
                for k in range(KKV):
                    for a, b, c in ((0, SEQ, 0), (KEY_NEW, NKEY, SEQ)):
                        V.scalar_tensor_tensor(out=ckv[:, k, a:b], in0=ckv[:, k, a:b], scalar=g_now[:, 27 + k:28 + k],
                                               in1=rstd[:, c:c + b - a], op0=ALU.mult, op1=ALU.mult).then_inc(S["lat_ready"], 1)
                for g in range(2):
                    a2 = lambda v: v.rearrange("p (a b) -> p a b", a=2)
                    for e, (name, dst) in enumerate(((f"qr{g}", qAr[:, g, :]), (f"qs{g}", rope_t))):
                        u = TILE[name] % 2
                        filled(l, u, turn_of(name))
                        V.tensor_tensor(a2(dst), unit(u)[:, :, 0:HALF], a2(ropes[:, e, :]), ALU.mult).then_inc(vacated[u], 1)
                    for name in (f"qr{g}", f"qs{g}"):
                        dve.wait_ge(vacated[TILE[name] % 2], l * T_LAYER + turn_of(name) + 3)
                    V.tensor_tensor(qAr[:, g, :], qAr[:, g, :], rope_t, ALU.add).then_inc(S["qr_ready"], 1)
                    dve.wait_ge(S["qr_ready"], l * 2 + g + 1)
                dve.wait_ge(S["rows_out"], 16 * (l * 14 + 14))
                branch_b(l)
                attend(l, 0)
                attend(l, 1)
                mg = merged.rearrange("p f (a b) -> p f a b", a=2)
                with dve.Fori(0, 2) as i:
                    for j in range(4):
                        for b in range(3):
                            turn = turn_of("g0_0") + 3 * j + b + i * 12
                            filled(l, 1, turn)
                            dve.wait_ge(vacated[0], l * T_LAYER + turn + 3)
                            m = mg[:, bass.ds(i * 4 + j, 1)].rearrange("p o a b -> p (o a) b")
                            o = m if b == 0 else mt[:, b - 1, :].rearrange("p (a b) -> p a b", a=2)
                            V.tensor_tensor(o, sig[:, (3 * j + b) % 2, :].rearrange("p (a b) -> p a b", a=2), unit(1)[:, :, 0:HALF],
                                            ALU.mult).then_inc(vacated[1], 1)
                            if b:
                                dve.wait_ge(vacated[1], l * T_LAYER + turn + 3)
                                if b == 2:
                                    dve.wait_ge(S["merge_step"], l * KD + i * 4 + j + 1)
                                V.tensor_tensor(m, m, o, ALU.add).then_inc(S["merge_step" if b == 1 else "merge_ready"], 1)
                post_norm(l, "mix_post", y_m, False, 1)

            def select(l, s):
                w, k = MASK_W[s], (TOPK if s < 4 else TOPK_S)
                a = acc[:, ACC_AT[s]:ACC_AT[s] + w]
                wk, eq, cu = topw[:, 0:w], eqv[:, 0:w], cum[:, 0:w]
                src = a
                for r in range(k // 8):
                    link(l, V.max(m8[:], src))
                    if r < k // 8 - 1:
                        link(l, V.match_replace(wk, m8[:], src, LOWEST))
                        src = wk
                link(l, V.tensor_scalar(wk, a, m8[:, 7:8], None, ALU.is_gt))
                link(l, V.tensor_reduce(cnt[:, 0:1], wk, AX_X, ALU.add))
                link(l, V.tensor_scalar(cnt[:, 1:2], cnt[:, 0:1], -1.0, float(k), ALU.mult, ALU.add))
                link(l, V.tensor_scalar(eq, a, m8[:, 7:8], None, ALU.is_equal))
                link(l, V.tensor_tensor_scan(cu, eq, eq, 0.0, ALU.add, ALU.max))
                link(l, V.scalar_tensor_tensor(out=cu, in0=cu, scalar=cnt[:, 1:2], in1=eq, op0=ALU.is_le, op1=ALU.mult))
                link(l, V.tensor_tensor(wk, wk, cu, ALU.add))
                V.tensor_scalar(msk[:, MASK_AT[s]:MASK_AT[s] + w], wk, -1.0, BIG, ALU.add, ALU.mult).then_inc(S["sel_ready"], 1)
                dve.wait_ge(S["sel_ready"], l * 4 + s)
                alone(dve)

            def rotate_keys(l):
                for name in ("kr", "krs"):
                    dve.wait_ge(vacated[TILE[name] % 2], l * T_LAYER + turn_of(name) + 3)
                link(l, V.tensor_tensor(kr_raw[:, 1, :], kr_raw[:, 1, :], ropes[:, 1, :], ALU.mult))
                V.tensor_tensor(rope_t, kr_raw[:, 0, :], ropes[:, 0, :], ALU.mult).then_inc(S["rope_step"], 1)
                dve.wait_ge(S["rope_step"], l * 3 + 1)
                for a, b, c in ((0, SEQ, 0), (KEY_NEW, NKEY, SEQ)):
                    V.tensor_tensor(kr[:, a:b], rope_t[:, c:c + b - a], kr_raw[:, 1, c:c + b - a], ALU.add).then_inc(S["rope_step"], 1)
                dve.wait_ge(S["rope_step"], l * 3 + 3)

            def branch_b(l):
                nb = l * (N_B + 3)
                for t in range(N_B + 3):
                    dve.wait_ge(S["sb_soft"], nb + t + 1)
                    if t < N_B:
                        h, j = t // 4, 3 - t % 4
                        w, at = SEQ - P * j, 128 * ((3 - j) * (4 - j) // 2)
                        if t % 4 == 0 and h >= 2:
                            dve.wait_ge(S["sb_cum"], nb + t - 4)
                        V.scalar_tensor_tensor(out=sb_sp[:, h % 2, at:at + w], in0=PS[:, t % 4, 0:w], scalar=0.0,
                                               in1=sb_e[:, t % 2, 0:w], op0=ALU.max, op1=ALU.add).then_inc(S["sb_sp_ready"], 1)
                    else:
                        n = t - N_B
                        kt, m = 2 - n, (NEW, P, P)[n]
                        if n == 0:
                            dve.wait_ge(S["sb_cum"], nb + N_B)
                        V.scalar_tensor_tensor(out=sb_sp[0:m, 0, 256 * n:256 * n + 256].rearrange("p (a b) -> p a b", a=2),
                                               in0=PS[0:m, 2 * kt:2 * kt + 2, 0:P], scalar=0.0,
                                               in1=sb_e[0:m, t % 2, 0:2 * P].rearrange("p (a b) -> p a b", a=2),
                                               op0=ALU.max, op1=ALU.add).then_inc(S["sb_sp_ready"], 1)
                dve.wait_ge(S["sb_out"], l * 5 + 5)

            def attend(l, c):
                n0, q0 = l * N_UNIT + c * 34, l * N_PAIR + 5 * c

                def bias(i):
                    p, s, e = UNITS[i]
                    w = keys(s)[1]
                    x = PS[:, i % 2, 0:w]
                    dve.wait_ge(S["s_done"], n0 + i + 1)
                    dve.wait_ge(S["probs_ready"], n0 + i + 1)
                    if c == 1:
                        h = 2 * p + e
                        if s == 0:
                            if h < 4:
                                dve.wait_ge(S["t5_in01"], (l * 4 + 4) * 16)
                            else:
                                dve.wait_ge(S[f"t5_in{h // 2}"], (l * 2 + 2) * 16)
                        if s == 4 and e == 0:
                            dve.wait_ge(S["t5s_in"], (l * 8 + 8) * 16)
                        t5 = T5[:, h % 4, 384 - P * s:384 - P * s + w] if s < 4 else T5s[:, e, :]
                        dve.wait_ge(S["pt_done"], n0 + i + 1)
                        x = prob[:, i % 2, 0:w]
                        link(l, V.scalar_tensor_tensor(out=x, in0=PS[:, i % 2, 0:w], scalar=SCALE_C, in1=t5, op0=ALU.mult,
                                                       op1=ALU.add))
                        link(l, V.tensor_tensor(x, x, msk[:, MASK_AT[s]:MASK_AT[s] + w], ALU.add))
                    link(l, V.tensor_reduce(mx[:, i % 2:i % 2 + 1], x, AX_X, ALU.max))
                    V.tensor_scalar(nbias[:, i % 2:i % 2 + 1], mx[:, i % 2:i % 2 + 1], -SCALE_A if c == 0 else -1.0, None,
                                    ALU.mult).then_inc(S["bias_ready"], 1)

                def normalise(p, i):
                    q = 5 * c + p
                    n = 8 if p < 4 else 2
                    dve.wait_ge(S["pv_done"], n0 + i + 3)
                    dve.wait_ge(S["probs_ready"], n0 + i + 3)
                    dve.wait_ge(S["ot_done"], q0 + p + 1)
                    link(l, V.reciprocal(rinv[:, q % 2, 0:n], sums[:, q % 2, 0:n]))
                    V.tensor_tensor(OT[:, q % 2, 0:n * DH].rearrange("p (a b) -> p a b", a=n),
                                    PS[:, 4 + q % 2, 0:n * DH].rearrange("p (a b) -> p a b", a=n),
                                    rinv[:, q % 2, 0:n].unsqueeze(2).broadcast_to([P, n, DH]), ALU.mult).then_inc(S["heads_normed"], 1)

                n = len(UNITS)
                ends = {7: 0, 15: 1, 23: 2, 31: 3, 33: 4}
                for i in range(n + 2):
                    if i < n:
                        bias(i)
                    if c == 0 and 1 <= i <= n:
                        copy_probs(dve, V.tensor_copy, n0, i - 1)
                    if i - 2 in ends:
                        normalise(ends[i - 2], i - 2)

            with dve.Fori(0, DEPTH) as l:
                count[0] = 0
                link(l, V.tensor_copy(g_now[:], gain[:, bass.ds(l, 1), :].rearrange("p o n -> p (o n)")))
                ffn(l, T_A, "pre_a", "post_a", 0)
                mixer(l)
                ffn(l, T_B, "pre_b", "post_b", 2)
                assert count[0] == per, count[0]


DVE_STEPS = (1 + 1 + 2 + sum(2 * (k // 8) - 1 + 7 for k in (TOPK, TOPK, TOPK, TOPK_S)) + 1
             + len(UNITS) * (1 + 3) + N_PAIR)


def t5_buckets():
    rel = np.arange(NREL) - (SEQ - 1)
    nb, max_exact = 16, 8
    n = np.abs(rel)
    large = max_exact + (np.log(np.maximum(n, 1).astype(np.float32) / np.float32(max_exact)) / np.float32(math.log(256 / max_exact))
                         * np.float32(nb - max_exact)).astype(np.int32)
    return np.where(rel > 0, nb, 0) + np.where(n < max_exact, n, np.minimum(large, nb - 1))


def shape_constants():
    onehot = np.zeros((32, NREL), np.float32)
    onehot[t5_buckets(), np.arange(NREL)] = 1
    k, q = np.arange(P)[:, None], np.arange(P)[None, :]
    cst = np.zeros((P, 6, P), np.float32)
    cst[:, 0] = 1
    cst[:, 1] = -1
    cst[:, 2] = np.where(k >= q, -1, 0)
    cst[:, 3] = np.eye(P)
    cst[:, 4] = np.where(k >= q, -BIG, 0)
    cst[:, 5] = np.where((k < CHUNK) & (q >= CHUNK), -BIG, 0)
    pos = np.concatenate([np.arange(SEQ), PAST + np.arange(NEW)]).astype(np.float32)
    half = ROPE // 2
    inv = np.float32(10000.0) ** (-np.arange(half, dtype=np.float32) / np.float32(half))
    ang = pos[None, :] * inv[:, None]
    c, s = np.cos(ang), np.sin(ang)
    ropes = np.stack([np.tile(np.concatenate([c, c]), (4, 1)), np.tile(np.concatenate([-s, s]), (4, 1))], axis=1)
    return onehot, cst, np.ascontiguousarray(ropes.astype(np.float32))


def kernel(**inputs):
    from concourse import bacc as _bacc
    from concourse.bass_utils import run_bass_kernel_spmd as _run

    a = {k: np.asarray(v) for k, v in inputs.items()}
    L = DEPTH
    onehot, cst, ropes = shape_constants()

    at = np.concatenate([[0], np.cumsum([384, 256, 32, 512, 512, 512, 512, 64, 64, 512, 64, 8, 1024, 1024, 1024])])
    part = {n: np.arange(at[i], at[i + 1]) for i, n in enumerate(
        ["ql", "kv", "kr", "qb", "kb", "vb", "qc", "kc", "vc", "qi", "ki", "wi", "ga", "gb", "gc"])}
    swap = np.concatenate([np.arange(16, 32), np.arange(16)])
    krs = part["kr"][swap]
    cols = np.concatenate([part["ki"], part["ki"], part["qi"], part["kc"], part["kc"], part["qc"], part["qb"], part["kb"],
                           part["kr"], part["kr"], part["kr"], part["kr"], krs, krs, krs, krs, part["ql"], part["kv"], part["kv"][:128]])
    w_in = a["w_in"].reshape(L, KD, P, -1)

    def tiles(w, n):
        k = w.shape[1]
        return w.reshape(L, k, P, n, P).transpose(0, 3, 2, 1, 4).reshape(L, n, P, k * P)

    def groups(w, g):
        n, f = w.shape[1], w.shape[3]
        return w.reshape(L, n // g, g, P, f).transpose(0, 1, 3, 2, 4).reshape(L, n // g, P, g * f)

    uq = a["w_mla_uq"].reshape(L, KQ, P, H * 96)
    h = np.arange(H)[:, None]
    nope = (h * 96 + np.arange(64)).reshape(-1)
    rp = h * 96 + 64 + np.arange(32)
    rs = h * 96 + 64 + swap
    uq_cols = np.concatenate([nope, rp[:4].reshape(-1), rs[:4].reshape(-1), rp[4:].reshape(-1), rs[4:].reshape(-1)])
    ukv = a["w_mla_ukv"].reshape(L, KKV, P, H * 128)
    un = (h * 128 + np.arange(64)).reshape(-1)
    uv = (h * 128 + 64 + np.arange(64)).reshape(-1)
    gates = np.stack([tiles(w_in[..., part[g]], KD) for g in ("ga", "gb", "gc")], axis=2)
    br = a["w_branch"].reshape(L, 3, 4, P, KD, P).transpose(0, 4, 1, 3, 2, 5).reshape(L, KD, 3, P, 4 * P)
    vcwi = np.concatenate([part["vc"], part["wi"]])

    def gcols(g):
        return g.reshape(L, -1, P).transpose(2, 0, 1)

    def feat(x):
        return x.reshape(L, PAST, -1).transpose(0, 2, 1)

    def tokm(x):
        return x.reshape(L, 2, P, -1).transpose(0, 2, 1, 3)

    f = a["ffn_pre_gain"]
    g = a["ffn_post_gain"]
    arrays = {
        "x": np.concatenate([a["x_prompt"][0], a["x_sample"][0]]).T.reshape(KD, P, TOK).transpose(1, 0, 2),
        "cst": cst, "ropes": ropes, "onehot": onehot, "rel_bias": a["rel_bias"],
        "gains": np.concatenate([gcols(v) for v in (f[:, 0], g[:, 0], a["mix_pre_gain"], a["mla_q_norm"], a["mla_kv_norm"],
                                                    a["mix_post_gain"], f[:, 1], g[:, 1])], axis=2),
        "w_up": a["w_ffn_up"].reshape(L, 2, KD, P, 2, KF, P).transpose(0, 1, 5, 3, 4, 2, 6).reshape(L, 2 * KF, P, 2048),
        "w_dn": a["w_ffn_down"].reshape(L, 2, 2, 11, P, KD, P).transpose(0, 1, 5, 2, 4, 3, 6).reshape(L, 32, P, 1408),
        "w_in": groups(tiles(w_in[..., cols], 26), 2),
        "w_vb": w_in[..., part["vb"]].reshape(L, 2, 4, P, 512).transpose(0, 1, 3, 2, 4).reshape(L, 2, P, 2048),
        "w_vc": w_in[..., vcwi].transpose(0, 2, 1, 3).reshape(L, 1, P, 576),
        "w_uq": groups(tiles(uq[..., uq_cols], 8), 4),
        "w_ukn": groups(tiles(ukv[..., un], 4), 4),
        "w_ukv": ukv[..., uv].transpose(0, 2, 1, 3).reshape(L, 1, P, 1024),
        "w_mg": np.concatenate([gates, br], axis=4).reshape(L, 3 * KD, P, 1536),
        "w_out": groups(tiles(a["w_o"].reshape(L, KD, P, D), KD), 2),
        "c_kidx": np.concatenate([feat(a["cache_dsa_kidx"])] * 2, axis=1)[:, :, None],
        "c_dsk": np.concatenate([feat(a["cache_dsa_k"])] * 2, axis=1)[:, :, None],
        "c_dsv": tokm(a["cache_dsa_v"]),
        "c_sbk": feat(a["cache_sb_k"]).reshape(L, 4, P, PAST).transpose(0, 2, 1, 3),
        "c_sbv": tokm(a["cache_sb_v"]),
        "c_kr": np.concatenate([feat(a["cache_mla_krope"])] * 4, axis=1)[:, :, None],
        "c_ckv": feat(a["cache_mla_ckv"]).reshape(L, KKV, P, PAST).transpose(0, 2, 1, 3),
    }
    outs = {"y": (P, KD, TOK), "o_kr": (L, ROPE, TOK),
            "p_ki": (L, DH, 1, SEQ), "s_ki": (L, DH, 1, NEW), "p_kc": (L, DH, 1, SEQ), "s_kc": (L, DH, 1, NEW),
            "p_vb": (L, P, 4, 512), "s_vb": (L, NEW, 1, 512), "p_vc": (L, P, 4, DH), "s_vc": (L, NEW, 1, DH),
            "p_kb": (L, P, 4, SEQ), "s_kb": (L, P, 4, NEW), "p_ckv": (L, P, 2, SEQ), "s_ckv": (L, P, 2, NEW)}

    nc = _bacc.Bacc("TRN2", target_bir_lowering=False, num_devices=1)
    arrays = {f"in_{k}": np.ascontiguousarray(v) for k, v in arrays.items()}
    dram = {k[3:]: nc.dram_tensor(k, v.shape, F32, kind="ExternalInput").ap() for k, v in arrays.items()}
    dram |= {k: nc.dram_tensor(f"out_{k}", v, F32, kind="ExternalOutput").ap() for k, v in outs.items()}
    dram["t5"] = nc.dram_tensor("t5_by_distance", (H, P, NREL), F32, kind="Internal").ap()
    build(nc, dram)
    r = {k: _run_out for k, _run_out in _run(nc, [arrays], core_ids=[0]).results[0].items()}
    o = {k: r[f"out_{k}"] for k in outs}
    y = o["y"].transpose(2, 1, 0).reshape(TOK, D)

    def rows(v, width):
        return v.transpose(0, 3, 2, 1).reshape(L, 1, v.shape[3], width)

    def token_rows(v, width):
        return v.transpose(0, 2, 1, 3).reshape(L, 1, -1, width)

    def group(c, sl):
        return (rows(o[f"{c}_ckv"], KV_LORA), o["o_kr"][:, :, sl].transpose(0, 2, 1)[:, None],
                rows(o[f"{c}_kb"], MIX).reshape(L, 1, -1, H, DH), token_rows(o[f"{c}_vb"], MIX).reshape(L, 1, -1, H, DH),
                rows(o[f"{c}_kc"], DH), token_rows(o[f"{c}_vc"], DH), rows(o[f"{c}_ki"], DH))

    return tuple(np.ascontiguousarray(v) for v in (
        y[None, :SEQ], y[None, SEQ:], *group("p", slice(0, SEQ)), *group("s", slice(SEQ, TOK))))
```

```python
import math
from contextlib import ExitStack

import numpy as np

import concourse.bass as bass
from concourse import mybir

F32 = mybir.dt.float32
F32R = mybir.dt.float32r
BF16 = mybir.dt.bfloat16
ALU = mybir.AluOpType
ACT = mybir.ActivationFunctionType
AX_X = mybir.AxisListType.X

P = 128
DEPTH, D, D_FF = 2, 1024, 2816
SEQ, NEW, PAST = 512, 32, 256
TOK = SEQ + NEW
HALF = TOK // 2
NKEY = SEQ + PAST + NEW
KEY_NEW = SEQ + PAST
CHUNK, QB = 64, 128
NBLK = SEQ // QB
H, DH, ROPE = 8, 64, 32
Q_LORA, KV_LORA = 384, 256
MIX = H * DH
KD, KF = D // P, D_FF // P
KQ, KKV = Q_LORA // P, KV_LORA // P
EPS = 1e-6
TOPK = min(256, SEQ // 4)
TOPK_S = min(256, (PAST + NEW) // 4)
BIG = 1.0e30
LOWEST = -3.0e38
SCALE_A = (64 + 32) ** -0.5
SCALE_C = DH ** -0.5
SCALE_I = DH ** -0.5 * H ** -0.5
NREL = 640
W_S = PAST + NEW

SLOT = 2048
NSLOT = 4
CH_FFN = KF + 2 * KD
CH_MIX = 48
CH_LAYER = 2 * CH_FFN + CH_MIX
assert CH_LAYER % NSLOT == 0
CH_A, CH_M, CH_B = 0, CH_FFN, CH_FFN + CH_MIX

PC_FFN = 2 * KF + 2 * KD
PC_MIX = 30 + 48 + 8
PC_A, PC_M, PC_B = 0, PC_FFN, PC_FFN + PC_MIX
PC_LAYER = 2 * PC_FFN + PC_MIX
PIECE = 1408

T_FFN = (2 * KF + KD) // 2
T_MIX = 50
T_LAYER = 2 * T_FFN + T_MIX
T_A, T_M, T_B = 0, T_FFN, T_FFN + T_MIX

NORMS = {"pre_a": (0, 0, 8), "post_a": (1, 8, 8), "mix": (2, 16, 8), "q": (3, 24, 3), "kv": (4, 27, 2),
         "mix_post": (5, 29, 8), "pre_b": (6, 37, 8), "post_b": (7, 45, 8)}
N_NORM, N_SQ = 8, 53

UNITS = [(p, s, e) for p in range(4) for s in range(NBLK) for e in range(2)] + [(4, 4, 0), (4, 4, 1)]
N_UNIT = 2 * len(UNITS)
N_PAIR = 10
N_B = H * NBLK
MASK_AT = [0, 128, 384, 768, 1280]
MASK_W = [128, 256, 384, 512, W_S]
ACC_AT = {1: 0, 2: 256, 3: 640, 4: 1152}


def mixer_tiles():
    t = ["kI"] + [f"qI{i}" for i in range(4)] + ["kC"] + ["v0", "v1"]
    t += [f"qC{i}" for i in range(4)] + [f"qB{i}" for i in range(4)] + [f"kB{i}" for i in range(4)]
    t += ["kr", "krs"] + [f"ql{i}" for i in range(KQ)] + [f"kv{i}" for i in range(KKV)]
    t += [f"uq{i}" for i in range(4)] + ["qr0", "qs0", "qr1", "qs1"]
    t += [f"kA{i}" for i in range(4)] + [f"vA{i}" for i in range(5)]
    for n in range(KD):
        t += [f"g0_{n}", f"b0_{n}", f"g1_{n}", f"b1_{n}", f"g2_{n}", f"b2_{n}"]
    return t + [f"wo{n}" for n in range(KD)]


TILES = mixer_tiles()
assert len(TILES) == 2 * T_MIX
TILE = {name: i for i, name in enumerate(TILES)}
MIX_CHUNKS = ([("w_in", i, 2048, TILES[2 * i + 1]) for i in range(3)]
              + [("w_vb", 0, 2048, "v0"), ("w_vb", 1, 2048, "v0"), ("w_vc", 0, 576, "v1")]
              + [("w_in", 3 + i, 2048 if i < 9 else 1024, TILES[min(9 + 2 * i, 26)]) for i in range(10)]
              + [("w_uq", 0, 1536, "uq3"), ("w_uq", 1, 1536, "qs1"), ("w_ukn", 0, 1024, "kA3"), ("w_ukv", 0, 1024, "vA4")]
              + [("w_mg", 3 * n + b, 1536, f"b{b}_{n}") for n in range(KD) for b in range(3)]
              + [("w_out", i, 2048, f"wo{2 * i + 1}") for i in range(4)])
assert len(MIX_CHUNKS) == CH_MIX
IN_PIECES = ([(i // 2, (i % 2) * 1024, 1024) for i in range(6)]
             + [(3 + i // 2, (i % 2) * 1024, 1024) for i in range(4)] + [(5, 0, 576)]
             + [(6 + i // 2, (i % 2) * 1024, 1024) for i in range(19)])
OUT_PIECES = [(44 + i // 2, (i % 2) * 1024, 1024) for i in range(KD)]
PIECE_OF = {t: i for i, t in enumerate(TILES[:6])} | {t: 11 + i for i, t in enumerate(TILES[8:27])} | {f"wo{n}": 78 + n for n in range(KD)}
VA_KEYS = [(0, 1), (2, 3), (4,), (5,), (6,)]


def build(nc, d):
    with ExitStack() as ctx:
        def sb(name, shape, dt=F32):
            return ctx.enter_context(nc.sbuf_tensor(name, shape, dt))

        def sem(name):
            return ctx.enter_context(nc.semaphore(name))

        PS = ctx.enter_context(nc.psum_tensor("PS", [P, 8, 512], F32))
        xT = sb("xT", [P, KD, TOK])
        uT_at = nc.sbuf_base
        uT = sb("uT", [P, KD, SEQ + P])
        uT_r = nc.alloc_sbuf_tensor_at("uT_r", [P, KD, SEQ + P], F32R, offset=uT_at)
        ring_at = nc.sbuf_base
        ring = sb("ring", [P, NSLOT, SLOT])
        ring_r = nc.alloc_sbuf_tensor_at("ring_r", [P, NSLOT, SLOT], F32R, offset=ring_at)
        cst = sb("cst", [P, 6, P])
        ropes = sb("ropes", [P, 2, TOK])
        gain = sb("gain", [P, DEPTH, N_SQ])
        g_now = sb("g_now", [P, N_SQ])
        sq = sb("sq", [P, 2, TOK])
        rstd = sb("rstd", [P, TOK])
        eps_c = sb("eps_c", [P, 1])
        m8 = sb("m8", [P, 8])
        cnt = sb("cnt", [P, 4])
        mx = sb("mx", [P, 2])
        nbias = sb("nbias", [P, 2])
        sums = sb("sums", [P, 2, 8])
        rinv = sb("rinv", [P, 2, 8])
        ARENA = 28472 + 3100
        arena_at = nc.sbuf_base
        arena = sb("arena", [P, ARENA])

        ones, neg_ones, neg_tri, ident, sb_mask, chunk_mask = (cst[:, i, :] for i in range(6))

        def region_r(name, at, *shape):
            return nc.alloc_sbuf_tensor_at(name, [P, *shape], F32R, offset=arena_at + 4 * at)

        def region(at, *shape):
            n = int(np.prod(shape))
            v = arena[:, at:at + n]
            if len(shape) == 2:
                v = v.rearrange("p (a b) -> p a b", a=shape[0])
            return v

        act_h = region_r("act_h", 0, KF, TOK)
        act_l = region_r("act_l", KF * TOK, KF, TOK)
        y_f = region(2 * KF * TOK, KD, TOK)
        u_l = region_r("u_l", 2 * KF * TOK, KD, TOK)
        piece_h = region_r("piece_h", (ARENA - 2 * PIECE) // 8 * 8, 2, PIECE)
        gate_s = sq
        u_norm_m = region(23448, KD, SEQ + P)
        u_lm = region_r("u_lm", 23448, KD, SEQ + P)
        VB = region(0, 7, 512)
        VC = region(3584, 7, DH)
        kC = region(4032, NKEY)
        qC = region(4832, 4, TOK)
        qB = region(7008, 4, TOK)
        kB = region(9184, 4, NKEY)
        kr = region(12384, NKEY)
        msk = arena[:, 13536:13536 + 784].bitcast(BF16)
        ckv = region(14320, KKV, NKEY)
        qI = region(15920, 4, SEQ + P)
        ql = region(15920, KQ, TOK)
        rope_t = region(17552, TOK)
        kI = region(18480, NKEY)
        wI = region(19280, 5, H)
        acc = region(19320, 1440)
        topw = region(20760, 512)
        eqv = region(21272, 512)
        cum = region(21784, 512)
        rel = region(22296, 2, 512)
        kr_raw = region(22296, 2, TOK)
        sb_sp = region(17552, 2, 1280)
        sb_a = region(20112, 2, 1280)
        sb_e = sq[:, :, 0:512]
        VA = region(0, 7, 512)
        kA = region(9184, 4, NKEY)
        qAr = region(20184, 2, TOK)
        qAn = region(21272, 4, TOK)
        prob = region(14320, 2, 512)
        probT = region(15344, 2, 512)
        OT = region(16368, 2, 512)
        T5 = region(17552, 4, 512)
        T5s = region(19600, 2, W_S)
        topw_tab = region(0, NREL)
        onehot = region(NREL, NREL)
        relb = region(2 * NREL, H)
        o_l = [region_r(f"o_l{b}", at, 4, TOK) for b, at in enumerate((21272, 7008, 4832))]
        o_h = [region_r(f"o_h{b}", at, 4, TOK) for b, at in enumerate((11360, 9184, 13536))]
        merged_l = region_r("merged_l", 0, KD, TOK)
        merged_h = region_r("merged_h", 15712, KD, TOK)
        mt = region(20064, 2, TOK)
        y_m = region(4832, KD, TOK)
        sig = sq

        S = {n: sem(n) for n in (
            "consts_in", "x_in", "gain_in", "table_out", "table_in", "gain_now", "xnew", "hready", "sq_ready", "sq_used",
            "root", "inv", "yscaled", "cache_in", "rows_out", "y_out", "idx_done", "idx_rel", "idx_acc",
            "sel_ready", "lat_ready", "rope_step", "qr_ready", "dve_step", "act_step", "sb_done", "sb_soft",
            "sb_sp_ready", "sb_cum", "sb_a_ready", "sb_pv", "sb_out", "s_done", "bias_ready", "probs_ready",
            "pt_done", "pt_copied", "pv_done", "heads_normed", "ot_done", "branch_out", "t5_in01", "t5_in2", "t5_in3", "t5s_in",
            "merge_ready", "merge_step", "init_ready", "tab_ps", "tab_sb", "u_norm", "u_high",
            "w_high", "w_low", "half_read", "gate_step", "v_step", "split", "split_c")}
        done = [sem("tile_done0"), sem("tile_done1")]
        vacated = [sem("tile_vacated0"), sem("tile_vacated1")]
        loaded = [sem(f"slot_loaded{i}") for i in range(NSLOT)]
        blk = ctx.enter_context(nc.Block())

        def alone(eng):
            eng.nop(nofuse=True)

        def unit(u):
            return PS[:, 2 * u:2 * u + 2, :]

        def turn_of(name):
            return T_M + TILE[name] // 2

        def keys(s):
            return (SEQ, W_S) if s == 4 else (0, QB * (s + 1))

        def key_tiles(s):
            k0, w = keys(s)
            return [(k0 + 128 * t, min(128, w - 128 * t), 128 * t, (4 + t) if s == 4 else t)
                    for t in range((w + 127) // 128)]

        def copy_probs(eng, copy, n0, i):
            eng.wait_ge(S["pt_done"], n0 + i + 3)
            eng.wait_ge(S["pv_done"], n0 + i + 1)
            tiles = key_tiles(UNITS[i][1])
            full = [t for t in tiles if t[1] == P]
            ins = copy(probT[:, i % 2, 0:P * len(full)], PS[:, 2 + i % 2, 0:P * len(full)])
            for _, m, at, _ in tiles[len(full):]:
                ins = copy(probT[0:m, i % 2, at:at + P], PS[0:m, 2 + i % 2, at:at + P])
            ins.then_inc(S["pt_copied"], 1)

        @blk.sync
        def _(sp):
            sp.dma_start(xT[:], d["x"]).then_inc(S["x_in"], 16)
            sp.dma_start(cst[:], d["cst"]).then_inc(S["consts_in"], 16)
            sp.dma_start(gain[:], d["gains"]).then_inc(S["gain_in"], 16)

            def load(src, n, ch):
                slot = ch % NSLOT
                sp.dma_start(ring[:, slot, 0:n], src).then_inc(loaded[slot], 16)

            def one(name, l, i):
                return d[name][bass.ds(l, 1), bass.ds(i, 1)].rearrange("l c p n -> p (l c n)")

            def consumed(l, u, turn):
                sp.wait_ge(done[u], l * T_LAYER + turn + 1)

            for f in range(NSLOT):
                load(one("w_up", 0, f), 2048, f)
            sp.dma_start(ropes[:], d["ropes"]).then_inc(S["consts_in"], 16)

            def ffn(l, ab, t0, c0, after):
                w0 = ab * KF
                with sp.Fori(0, 4) as i:
                    for j in range(4):
                        consumed(l, 1, t0 + i * 4 + j)
                        load(one("w_up", l, w0 + i * 4 + j + 4), 2048, c0 + j)
                for f in range(16, KF - 4):
                    consumed(l, 1, t0 + f)
                    load(one("w_up", l, w0 + f + 4), 2048, c0 + f)
                for f in range(KF - 4, KF):
                    consumed(l, 1, t0 + f)
                    load(one("w_dn", l, ab * 16 + f - KF + 4), 1408, c0 + f)
                with sp.Fori(0, 3) as i:
                    for j in range(4):
                        if j % 2 == 0:
                            consumed(l, j // 2, t0 + KF + i)
                        load(one("w_dn", l, ab * 16 + i * 4 + j + 4), 1408, c0 + KF + j)
                for j in range(4):
                    if j % 2 == 0:
                        consumed(l, j // 2, t0 + KF + 3)
                    after(j, c0 + KF + 12 + j)

            def mixer(l):
                for k in range(CH_MIX):
                    u, turn = TILE[MIX_CHUNKS[k][3]] % 2, turn_of(MIX_CHUNKS[k][3])
                    consumed(l, u, turn)
                    if k + NSLOT < CH_MIX:
                        name, i, n, _ = MIX_CHUNKS[k + NSLOT]
                        load(one(name, l, i)[:, 0:n], n, CH_M + k)
                    else:
                        load(one("w_up", l, KF + k + NSLOT - CH_MIX), 2048, CH_M + k)

            with sp.Fori(0, DEPTH) as l:
                ffn(l, 0, T_A, CH_A, lambda j, ch: load(one(MIX_CHUNKS[j][0], l, MIX_CHUNKS[j][1]), 2048, ch))
                mixer(l)
                ffn(l, 1, T_B, CH_B, lambda j, ch: load(one("w_up", l * -1 + (DEPTH - 1), j), 2048, ch))
            sp.wait_ge(S["xnew"], 8 + DEPTH * 24)
            sp.dma_start(d["y"], xT[:]).then_inc(S["y_out"], 16)
            sp.wait_ge(S["y_out"], 16)
            for i in range(NSLOT):
                sp.wait_ge(loaded[i], 16 * (DEPTH * CH_LAYER // NSLOT + 1))

        N_ROWS = 12
        N_CACHE = 7

        @blk.gpsimd
        def _(pool):
            pool.wait_ge(S["tab_sb"], 1)
            pool.dma_start(d["t5"], topw_tab[0:H, :].unsqueeze(1).broadcast_to([H, P, NREL])).then_inc(S["table_out"], 16)
            pool.wait_ge(S["table_out"], 16)

            def t5_sem(h):
                return "t5_in01" if h < 4 else f"t5_in{h // 2}"

            def toeplitz(h, rows, c0, n):
                return bass.AP(d["t5"].tensor, h * P * NREL + c0 + P - 1, [[NREL - 1, rows], [1, n]])

            def low(l, p0, i, ch, at, n, t=0):
                pool.wait_ge(S["w_high"], l * PC_LAYER + p0 + i + 1)
                hi, w = piece_h[:, ch[1], 0:n].bitcast(F32), ring[:, ch[0] % NSLOT, at:at + n]
                nc.gpsimd.tensor_tensor(ring_r[:, ch[0] % NSLOT, at:at + n], w, hi, ALU.subtract).then_inc(S["w_low"], 1)

            def ffn(l, p0, c0):
                with pool.Fori(0, 5) as i:
                    for j in range(8):
                        low(l, p0, i * 8 + j, (c0 + j // 2, j % 2), (j % 2) * 1024, 1024)
                for j in range(40, 2 * KF):
                    low(l, p0, j, (c0 + j // 2, j % 2), (j % 2) * 1024, 1024)
                for j in range(2 * KD):
                    low(l, p0, 2 * KF + j, (c0 + KF + j, j % 2), 0, PIECE)

            with pool.Fori(0, DEPTH) as l:
                ffn(l, PC_A, CH_A)
                def cached(dst, name):
                    pool.dma_start(dst, d[name][bass.ds(l, 1)].rearrange(
                        "l p a b -> p (l a) b" if len(dst.shape) == 3 else "l p a b -> p (l a b)")).then_inc(S["cache_in"], 16)

                pool.wait_ge(S["xnew"], l * 24 + 16)
                alone(pool)
                cached(kI[:, SEQ:KEY_NEW], "c_kidx")
                cached(kC[:, SEQ:KEY_NEW], "c_dsk")
                cached(VC[:, 4:6, :], "c_dsv")
                cached(kB[:, :, SEQ:KEY_NEW], "c_sbk")
                cached(VB[:, 4:6, :], "c_sbv")
                cached(kr[:, SEQ:KEY_NEW], "c_kr")
                cached(ckv[:, :, SEQ:KEY_NEW], "c_ckv")

                def lows(a, b):
                    for i in range(a, b):
                        ch, at, n = IN_PIECES[i]
                        low(l, PC_M, i, (CH_M + ch, i % 2), at, n)

                def row(name, src):
                    dst = d[name][bass.ds(l, 1)]
                    dst = dst.rearrange("l p a b -> p (l a) b" if len(src.shape) == 3 else "l p a b -> p (l a b)")
                    pool.dma_start(dst, src).then_inc(S["rows_out"], 16)

                def evacuated(name):
                    pool.wait_ge(vacated[TILE[name] % 2], l * T_LAYER + turn_of(name) + 3)
                    alone(pool)

                lows(0, 4)
                evacuated("kI")
                row("p_ki", kI[0:DH, 0:SEQ])
                row("s_ki", kI[0:DH, KEY_NEW:NKEY])
                lows(4, 13)
                evacuated("v0")
                evacuated("v1")
                evacuated("kC")
                row("p_kc", kC[0:DH, 0:SEQ])
                row("s_kc", kC[0:DH, KEY_NEW:NKEY])
                row("p_vb", VB[:, 0:4, :])
                row("s_vb", VB[0:NEW, 6, :])
                row("p_vc", VC[:, 0:4, :])
                row("s_vc", VC[0:NEW, 6, :])
                lows(13, 26)
                evacuated("kB3")
                evacuated("kB2")
                row("p_kb", kB[:, :, 0:SEQ])
                row("s_kb", kB[:, :, KEY_NEW:NKEY])
                lows(26, 30)
                pool.wait_ge(S["rope_step"], l * 3 + 3)
                alone(pool)
                pool.dma_start(d["o_kr"][bass.ds(l, 1)].rearrange("l p b -> p (l b)")[:, 0:SEQ], kr[0:ROPE, 0:SEQ]).then_inc(S["rows_out"], 16)
                pool.dma_start(d["o_kr"][bass.ds(l, 1)].rearrange("l p b -> p (l b)")[:, SEQ:TOK], kr[0:ROPE, KEY_NEW:NKEY]).then_inc(S["rows_out"], 16)
                pool.wait_ge(S["lat_ready"], l * 7 + 7)
                alone(pool)
                row("p_ckv", ckv[:, :, 0:SEQ])
                row("s_ckv", ckv[:, :, KEY_NEW:NKEY])
                pool.wait_ge(S["qr_ready"], l * 2 + 2)
                alone(pool)
                for h in range(4):
                    pool.dma_start(T5[:, h, :], toeplitz(h, P, 0, 512)).then_inc(S[t5_sem(h)], 16)
                for h in range(H):
                    j, g = h % 4, h // 4
                    pool.dma_start(T5s[32 * j:32 * j + 32, g, :], toeplitz(h, NEW, 128, W_S)).then_inc(S["t5s_in"], 16)
                pool.wait_ge(S["branch_out"], l * N_PAIR + 5 + 2)
                for b, o, n in ((1, qB, 0), (0, qAn, 2)):
                    alone(pool)
                    nc.gpsimd.tensor_copy(o_h[b][:], o).then_inc(S["split"], 1)
                    pool.wait_ge(S["split"], l * 4 + n + 1)
                    nc.gpsimd.tensor_tensor(o_l[b][:], o, o_h[b][:].bitcast(F32), ALU.subtract).then_inc(S["split"], 1)
                    for h in range(4 + n, 6 + n):
                        pool.wait_ge(S["bias_ready"], l * N_UNIT + 34 + 8 * ((h - 4) // 2 + 1))
                        alone(pool)
                        pool.dma_start(T5[:, h % 4, :], toeplitz(h, P, 0, 512)).then_inc(S[t5_sem(h)], 16)
                with pool.Fori(0, 5) as i:
                    for j in range(8):
                        low(l, PC_M, i * 8 + 30 + j, (CH_M + 20 + j // 2, j % 2), (j % 2) * 1024, (1024, 512)[j % 2])
                for j in range(40, 48):
                    low(l, PC_M, 30 + j, (CH_M + 20 + j // 2, j % 2), (j % 2) * 1024, (1024, 512)[j % 2])
                for n, (ch, at, m) in enumerate(OUT_PIECES):
                    low(l, PC_M, 78 + n, (CH_M + ch, n % 2), at, m)
                ffn(l, PC_B, CH_B)
            pool.wait_ge(S["rows_out"], 16 * 14 * DEPTH)

        @blk.tensor
        def _(pe):
            mm = nc.tensor.matmul
            pe.sem_inc(vacated[0], 2)
            pe.sem_inc(vacated[1], 2)
            pe.sem_inc(S["sq_used"], 2)
            pe.sem_inc(S["root"], 1)
            for n in ("idx_rel", "idx_acc", "probs_ready", "pt_done", "pt_copied", "pv_done", "heads_normed",
                      "ot_done", "branch_out"):
                pe.sem_inc(S[n], 2)
            pe.sem_inc(S["sb_a_ready"], 4)
            pe.sem_inc(S["sb_pv"], 2)

            pe.wait_ge(S["table_in"], 32)
            for c in range(2):
                last = mm(PS[0:H, c, 0:320], relb[0:32, :], onehot[0:32, 320 * c:320 * c + 320], start=True, stop=True)
            last.then_inc(S["tab_ps"], 1)
            pe.wait_ge(S["tab_sb"], 1)
            pe.wait_ge(S["consts_in"], 32)

            def chunk(l, ch, i=0):
                pe.wait_ge(loaded[ch % NSLOT], (l * (CH_LAYER // NSLOT) + ch // NSLOT + i + 1) * 16)
                return ring[:, ch % NSLOT, :]

            def open_tile(l, u, turn):
                pe.wait_ge(vacated[u], l * T_LAYER + turn + 2)

            def product(u, steps, n=(0, HALF, TOK), first=True, last=True, m=P):
                ins = None
                for s, (w, x) in enumerate(steps):
                    for b in range(2):
                        ins = mm(PS[0:m, 2 * u + b, 0:n[b + 1] - n[b]], w, x[:, n[b]:n[b + 1]],
                                 start=first and s == 0, stop=last and s == len(steps) - 1)
                if last:
                    ins.then_inc(done[u], 1)

            def square_sum(l, norm, k):
                j, q0, K = NORMS[norm]
                if k == 0:
                    pe.wait_ge(S["root"], l * N_NORM + j + 1)
                pe.wait_ge(S["sq_ready"], l * N_SQ + q0 + k + 1)
                for b in range(2):
                    ins = mm(PS[:, 4 + b, 0:HALF], ones, sq[:, k % 2, HALF * b:HALF * b + HALF],
                             start=k == 0, stop=k == K - 1)
                ins.then_inc(S["sq_used"], 1)

            def square_sum_at(l, q0, expr, k2):
                pe.wait_ge(S["sq_ready"], l * N_SQ + q0 + expr + 1)
                for b in range(2):
                    ins = mm(PS[:, 4 + b, 0:HALF], ones, sq[:, k2, HALF * b:HALF * b + HALF], start=False, stop=False)
                ins.then_inc(S["sq_used"], 1)

            def split_product(l, u, piece, hs, w_l, x_h, x_l, first=True, last=True, step=None):
                K = len(x_h)
                pe.wait_ge(S["w_high"], piece + 1)
                for k in range(K):
                    if step:
                        step(k)
                    w = piece_h[:, hs, k * P:(k + 1) * P]
                    for n, x in enumerate((x_h, x_l)):
                        for b in range(2):
                            mm(PS[:, 2 * u + b, 0:HALF], w, x[k][:, HALF * b:HALF * b + HALF],
                               start=first and k == 0 and n == 0, stop=False)
                pe.wait_ge(S["w_low"], piece + 1)
                for k in range(K):
                    for b in range(2):
                        ins = mm(PS[:, 2 * u + b, 0:HALF], w_l[:, k * P:(k + 1) * P], x_h[k][:, HALF * b:HALF * b + HALF],
                                 start=False, stop=last and k == K - 1)
                ins.then_inc(done[u] if last else S["half_read"], 1)

            def ffn(l, t0, c0, p0, pre, post, h0):
                for k in range(KD):
                    square_sum(l, pre, k)
                u_h, u_lo = [uT_r[:, k, 0:TOK] for k in range(KD)], [u_l[:, k, :] for k in range(KD)]

                def up(f, ch, step=None):
                    for g in range(2):
                        open_tile(l, g, t0 + f)
                        split_product(l, g, l * PC_LAYER + p0 + f * 2 + g, g, ring_r[:, ch % NSLOT, g * 1024:g * 1024 + 1024],
                                      u_h, u_lo, step=step if g == 0 else None)

                def input_ready(k):
                    pe.wait_ge(S["hready"], l * 26 + h0 + k + 1)

                up(0, c0, input_ready)
                alone(pe)
                with pe.Fori(0, 5) as i:
                    for j in range(4):
                        up(i * 4 + j + 1, c0 + j + 1)
                up(KF - 1, c0 + KF - 1)
                pe.wait_ge(vacated[1], l * T_LAYER + t0 + KF + 2)

                def down(u, turn, n, ch):
                    open_tile(l, u, turn)
                    for kh in range(2):
                        split_product(l, u, l * PC_LAYER + p0 + 2 * KF + n * 2 + kh, kh, ring_r[:, (ch + kh) % NSLOT, :],
                                      [act_h[:, 11 * kh + k, :] for k in range(11)], [act_l[:, 11 * kh + k, :] for k in range(11)],
                                      first=kh == 0, last=kh == 1)

                q0 = NORMS[post][1]
                down(0, t0 + KF, 0, c0 + KF)
                down(1, t0 + KF, 1, c0 + KF + 2)
                square_sum(l, post, 0)
                down(0, t0 + KF + 1, 2, c0 + KF + 4)
                square_sum(l, post, 1)
                alone(pe)
                with pe.Fori(0, 2) as i:
                    down(1, t0 + KF + 1 + i, i * 2 + 3, c0 + KF + 6)
                    square_sum_at(l, q0, 2 + i * 2, 0)
                    down(0, t0 + KF + 2 + i, i * 2 + 4, c0 + KF + 8)
                    square_sum_at(l, q0, 3 + i * 2, 1)
                down(1, t0 + KF + 3, 7, c0 + KF + 14)
                square_sum(l, post, 6)
                square_sum(l, post, 7)

            def mixer(l):
                for k in range(KD):
                    square_sum(l, "mix", k)
                ch = CH_M
                u_h, u_lo = [uT_r[:, k, 0:TOK] for k in range(KD)], [u_lm[:, k, 0:TOK] for k in range(KD)]

                def tile(name, steps, **kw):
                    t = TILE[name]
                    open_tile(l, t % 2, T_M + t // 2)
                    product(t % 2, steps, **kw)

                def split_tile(name, x_h, x_l, chunk_of, at, step=None):
                    t, piece = TILE[name], PIECE_OF[name]
                    open_tile(l, t % 2, T_M + t // 2)
                    split_product(l, t % 2, l * PC_LAYER + PC_M + piece, piece % 2, ring_r[:, (ch + chunk_of) % NSLOT, at:at + 1024],
                                  x_h, x_l, step=step)

                def input_ready(k):
                    pe.wait_ge(S["hready"], l * 26 + 8 + k + 1)

                for i in range(6):
                    split_tile(TILES[i], u_h, u_lo, IN_PIECES[i][0], IN_PIECES[i][1], input_ready if i == 0 else None)
                pe.wait_ge(S["hready"], l * 26 + 18)
                for u in range(2):
                    open_tile(l, u, T_M + TILE[f"v{u}"] // 2)
                for i in range(5):
                    piece = 6 + i
                    slot, at, _ = IN_PIECES[piece]
                    low_part = ring_r[:, (ch + slot) % NSLOT, at:at + 1024]
                    n = 512 if i < 4 else 72
                    pe.wait_ge(S["w_low"], l * PC_LAYER + PC_M + piece + 1)
                    for s in range(5):
                        ks = range(2) if i < 4 else range(KD)
                        for kk in ks:
                            k = 2 * i + kk if i < 4 else kk
                            out = PS[:, s, :] if i < 4 else PS[:, 5, 72 * s:72 * s + 72]
                            cols = slice(P * s, P * s + P)
                            w_h, w_l = piece_h[:, piece % 2, kk * n:kk * n + n], low_part[:, kk * n:kk * n + n]
                            first = k == 0 and (i < 4 or s == 0)
                            for m, (x, w) in enumerate(((uT_r[:, k, cols], w_h), (u_lm[:, k, cols], w_h), (uT_r[:, k, cols], w_l))):
                                ins = mm(out, x, w, start=first and m == 0, stop=k == KD - 1 and m == 2, skip_group_check=True)
                    ins.then_inc(S["v_step"] if i < 3 else done[i - 3], 1)
                pe.wait_ge(S["cache_in"], (l * N_CACHE + N_CACHE) * 16)
                pe.wait_ge(vacated[0], l * T_LAYER + turn_of("v0") + 3)
                pe.wait_ge(vacated[1], l * T_LAYER + turn_of("v1") + 3)
                i = 0
                for s in range(1, 5):
                    k0, w = keys(s)
                    for h in range(H):
                        r = 64 * (h % 2)
                        pe.wait_ge(S["idx_rel"], l * 32 + i + 1)
                        mm(PS[:, 6 + i % 2, 0:w], qI[r:r + 64, h // 2, P * s:P * s + P], kI[r:r + 64, k0:k0 + w],
                           start=True, stop=True).then_inc(S["idx_done"], 1)
                        i += 1
                for i in range(11, 30):
                    name = TILES[8 + i - 11]
                    split_tile(name, u_h, u_lo, IN_PIECES[i][0], IN_PIECES[i][1])
                    if name in ("ql1", "ql2", "kv0"):
                        square_sum(l, "q", ("ql1", "ql2", "kv0").index(name))
                for k in range(KKV):
                    square_sum(l, "kv", k)
                pe.wait_ge(S["lat_ready"], l * 7 + 7)
                for name in ("kv0", "kv1"):
                    pe.wait_ge(vacated[TILE[name] % 2], l * T_LAYER + turn_of(name) + 3)
                pe.wait_ge(S["rows_out"], 16 * (l * 14 + 14))
                branch_b(l)
                pe.wait_ge(S["lat_ready"], l * 7 + 3)
                for i in range(8):
                    w = chunk(l, ch + 16 + i // 4)
                    at = (i % 4) * KQ * P
                    tile(TILES[27 + i], [(w[:, at + k * P:at + k * P + P], ql[:, k, :]) for k in range(KQ)])
                pe.wait_ge(S["lat_ready"], l * 7 + 7)
                w = chunk(l, ch + 18)
                for i in range(4):
                    tile(f"kA{i}", [(w[:, (i * KKV + k) * P:(i * KKV + k + 1) * P], ckv[:, k, :]) for k in range(KKV)],
                         n=(0, NKEY // 2, NKEY))
                w = chunk(l, ch + 19)
                for i, kts in enumerate(VA_KEYS):
                    t = TILE[f"vA{i}"]
                    u = t % 2
                    open_tile(l, u, T_M + t // 2)
                    for b, kt in enumerate(kts):
                        m = P if kt < 6 else NEW
                        for k in range(KKV):
                            ins = mm(PS[0:m, 2 * u + b, :], ckv[:, k, P * kt:P * kt + m], w[:, k * 512:k * 512 + 512],
                                     start=k == 0, stop=k == KKV - 1)
                    ins.then_inc(done[u], 1)
                for name in ("vA3", "vA4"):
                    pe.wait_ge(vacated[TILE[name] % 2], l * T_LAYER + turn_of(name) + 3)
                pe.wait_ge(S["qr_ready"], l * 2 + 2)
                attend(l, 0)
                attend(l, 1)
                pe.wait_ge(S["branch_out"], l * N_PAIR + N_PAIR + 2)
                pe.wait_ge(S["split"], l * 4 + 4)
                alone(pe)
                with pe.Fori(0, 2) as i:
                    for j in range(4):
                        for b in range(3):
                            c = 3 * j + b
                            turn = turn_of("g0_0") + 3 * j + b + i * 12
                            piece = l * PC_LAYER + PC_M + 30 + 2 * c + i * 24
                            w_l = ring_r[:, (ch + 20 + c) % NSLOT, :]
                            open_tile(l, 0, turn)
                            split_product(l, 0, piece, 0, w_l, u_h, u_lo)
                            open_tile(l, 1, turn)
                            if b == 2:
                                pe.wait_ge(S["split_c"], l * 2 + 2)
                            split_product(l, 1, piece + 1, 1, w_l[:, 1024:1536], [o_h[b][:, k, :] for k in range(4)],
                                          [o_l[b][:, k, :] for k in range(4)])
                pe.wait_ge(S["merge_ready"], l * KD + KD)
                for n in range(KD):
                    split_tile(f"wo{n}", [merged_h[:, k, :] for k in range(KD)], [merged_l[:, k, :] for k in range(KD)], *OUT_PIECES[n][:2])
                    if n:
                        square_sum(l, "mix_post", n - 1)
                square_sum(l, "mix_post", KD - 1)

            def branch_b(l):
                def scores(t):
                    h, j = t // 4, 3 - t % 4
                    r, w = 64 * (h % 2), SEQ - P * j
                    pe.wait_ge(S["sb_a_ready"], l * (N_B + 3) + t + 1)
                    mm(PS[:, t % 4, 0:w], kB[r:r + 64, h // 2, P * j:P * j + P], qB[r:r + 64, h // 2, P * j:SEQ],
                       start=True, stop=False, skip_group_check=True)
                    mm(PS[:, t % 4, 0:P], ident, sb_mask, start=False, stop=True,
                       skip_group_check=True).then_inc(S["sb_done"], 1)

                def cumulate(t):
                    h, j = t // 4, 3 - t % 4
                    w = SEQ - P * j
                    pe.wait_ge(S["sb_sp_ready"], l * (N_B + 3) + t + 1)
                    for i in range(3, j, -1):
                        at = 128 * ((3 - i) * (4 - i) // 2)
                        wi = SEQ - P * i
                        mm(PS[:, t % 4, (i - j) * P:w], neg_ones, sb_sp[:, h % 2, at:at + wi], start=False, stop=False,
                           skip_group_check=True)
                    at = 128 * ((3 - j) * (4 - j) // 2)
                    mm(PS[:, t % 4, 0:w], neg_tri, sb_sp[:, h % 2, at:at + w], start=False, stop=True,
                       skip_group_check=True).then_inc(S["sb_cum"], 1)

                def values(h):
                    r = 64 * (h % 2)
                    pe.wait_ge(S["sb_a_ready"], l * (N_B + 3) + 4 * h + 8)
                    alone(pe)
                    if h % 2 == 0 and h >= 4:
                        pe.wait_ge(S["sb_out"], l * 5 + h // 2 - 1)
                    for j in range(4):
                        at = 128 * ((3 - j) * (4 - j) // 2)
                        ins = mm(PS[r:r + 64, 4 + (h // 2) % 2, P * j:SEQ], VB[:, j, DH * h:DH * h + DH],
                                 sb_a[:, h % 2, at:at + SEQ - P * j], start=j == 0, stop=j == 3, skip_group_check=True)
                    ins.then_inc(S["sb_pv"], 1)

                for t in range(N_B):
                    scores(t)
                    if t >= 2:
                        cumulate(t - 2)
                    if t >= 6 and (t - 6) % 4 == 0:
                        values((t - 6) // 4)
                cumulate(N_B - 2)
                cumulate(N_B - 1)
                values(H - 1)
                pe.wait_ge(S["sb_a_ready"], l * (N_B + 3) + N_B + 4)
                pe.wait_ge(S["sb_out"], l * 5 + 4)
                alone(pe)
                tiles = [(2, KEY_NEW, NEW), (1, SEQ + P, P), (0, SEQ, P)]
                for kt, k0, m in tiles:
                    for h in range(H):
                        r = 64 * (h % 2)
                        ins = mm(PS[0:m, 2 * kt + h % 2, 32 * (h // 2):32 * (h // 2) + 32], kB[r:r + 64, h // 2, k0:k0 + m],
                                 qB[r:r + 64, h // 2, SEQ:TOK], start=h < 2, stop=kt != 2, skip_group_check=True)
                    if kt == 2:
                        for b in range(2):
                            for j in range(4):
                                ins = mm(PS[0:m, 4 + b, 32 * j:32 * j + 32], ident[0:NEW, 0:NEW], sb_mask[0:NEW, 0:NEW],
                                         start=False, stop=True, skip_group_check=True)
                    ins.then_inc(S["sb_done"], 1)
                for n, (kt, k0, m) in enumerate(tiles):
                    pe.wait_ge(S["sb_sp_ready"], l * (N_B + 3) + N_B + n + 1)
                    alone(pe)
                    for b in range(2):
                        for n2 in range(n):
                            m2 = tiles[n2][2]
                            mm(PS[0:m, 2 * kt + b, 0:P], neg_ones[0:m2, 0:m], sb_sp[0:m2, 0, 256 * n2 + P * b:256 * n2 + P * b + P],
                               start=False, stop=False, skip_group_check=True)
                        ins = mm(PS[0:m, 2 * kt + b, 0:P], neg_tri[0:m, 0:m], sb_sp[0:m, 0, 256 * n + P * b:256 * n + P * b + P],
                                 start=False, stop=True, skip_group_check=True)
                    ins.then_inc(S["sb_cum"], 1)
                pe.wait_ge(S["sb_a_ready"], l * (N_B + 3) + N_B + 3 + 4)
                alone(pe)
                for h in range(H):
                    r = 64 * (h % 2)
                    for n in (2, 1, 0):
                        kt, k0, m = tiles[n]
                        ins = mm(PS[r:r + 64, 6, 32 * (h // 2):32 * (h // 2) + 32], VB[0:m, 4 + kt, DH * h:DH * h + DH],
                                 sb_a[0:m, 0, 256 * n + P * (h % 2) + 32 * (h // 2):256 * n + P * (h % 2) + 32 * (h // 2) + 32],
                                 start=n == 2, stop=n == 0, skip_group_check=True)
                ins.then_inc(S["sb_pv"], 1)
                pe.wait_ge(S["sb_out"], l * 5 + 5)

            def attend(l, c):
                V = (VA, VC)[c]
                n0, q0 = l * N_UNIT + c * 34, l * N_PAIR + 5 * c

                def scores(i):
                    p, s, e = UNITS[i]
                    k0, w = keys(s)
                    pe.wait_ge(S["probs_ready"], n0 + i + 1)
                    if s == 4:
                        alone(pe)
                    bank = i % 2
                    if s < 4:
                        h = 2 * p + e
                        r, r4 = 64 * e, 32 * (h % 4)
                        out = PS[:, bank, 0:w]
                        if c == 0:
                            mm(out, qAr[r4:r4 + 32, h // 4, P * s:P * s + P], kr[r4:r4 + 32, 0:w], start=True, stop=False,
                               skip_group_check=True)
                            mm(out, qAn[r:r + 64, p, P * s:P * s + P], kA[r:r + 64, p, 0:w], start=False, stop=False,
                               skip_group_check=True)
                            mm(PS[:, bank, w - P:w], ident, chunk_mask, start=False, stop=True,
                               skip_group_check=True).then_inc(S["s_done"], 1)
                        else:
                            mm(out, qC[r:r + 64, p, P * s:P * s + P], kC[r:r + 64, 0:w], start=True,
                               stop=True).then_inc(S["s_done"], 1)
                        return
                    for j in range(4):
                        h = 4 * e + j
                        r = 64 * (h % 2)
                        out = PS[32 * j:32 * j + 32, bank, 0:w]
                        if c == 0:
                            mm(out, qAn[r:r + 64, h // 2, SEQ:TOK], kA[r:r + 64, h // 2, k0:k0 + w], start=True, stop=False,
                               skip_group_check=True)
                        else:
                            ins = mm(out, qC[r:r + 64, h // 2, SEQ:TOK], kC[r:r + 64, k0:k0 + w], start=True, stop=True)
                    if c == 0:
                        for j in range(4):
                            out = PS[32 * j:32 * j + 32, bank, 0:w]
                            ins = mm(out, qAr[32 * j:32 * j + 32, e, SEQ:TOK], kr[32 * j:32 * j + 32, k0:k0 + w], start=False,
                                     stop=True, skip_group_check=True)
                    ins.then_inc(S["s_done"], 1)

                def transposes(i):
                    pe.wait_ge(S["probs_ready"], n0 + i + 3)
                    pe.wait_ge(S["pt_copied"], n0 + i + 1)
                    alone(pe)
                    for _, m, at, _ in key_tiles(UNITS[i][1]):
                        ins = nc.tensor.transpose(PS[0:m, 2 + i % 2, at:at + P], prob[:, i % 2, at:at + m], ident)
                    ins.then_inc(S["pt_done"], 1)

                def values(i):
                    p, s, e = UNITS[i]
                    pe.wait_ge(S["pt_copied"], n0 + i + 3)
                    if (s, e) in ((0, 0), (4, 0)):
                        pe.wait_ge(S["heads_normed"], q0 + p + 1)
                    if s == 4:
                        alone(pe)
                    bank = 4 + (5 * c + p) % 2
                    tiles = key_tiles(s)
                    for j in range(1 if s < 4 else 4):
                        h = 2 * p + e if s < 4 else 4 * e + j
                        out = PS[:, bank, P * s + DH * e:P * s + DH * e + DH] if s < 4 else PS[32 * j:32 * j + 32, bank, DH * e:DH * e + DH]
                        hv = DH * h if c == 0 else 0
                        for n, (_, m, at, vt) in enumerate(tiles):
                            pt = probT[0:m, i % 2, at:at + P] if s < 4 else probT[0:m, i % 2, at + 32 * j:at + 32 * j + 32]
                            ins = mm(out, pt, V[0:m, vt, hv:hv + DH], start=n == 0, stop=n == len(tiles) - 1)
                    ins.then_inc(S["pv_done"], 1)

                def turn_pair(p):
                    q = 5 * c + p
                    pe.wait_ge(S["heads_normed"], q0 + p + 3)
                    pe.wait_ge(S["branch_out"], q0 + p + 1)
                    alone(pe)
                    if p < 4:
                        for s in range(NBLK):
                            ins = nc.tensor.transpose(PS[:, 6 + q % 2, P * s:P * s + P], OT[:, q % 2, P * s:P * s + P], ident)
                    else:
                        for e in range(2):
                            ins = nc.tensor.transpose(PS[0:DH, 6 + q % 2, P * e:P * e + P], OT[:, q % 2, DH * e:DH * e + DH], ident)
                    ins.then_inc(S["ot_done"], 1)

                n = len(UNITS)
                ends = {7: 0, 15: 1, 23: 2, 31: 3, 33: 4}
                if c == 0:
                    pe.wait_ge(S["sb_out"], l * 5 + 5)
                for i in range(n + 3):
                    if i < n:
                        scores(i)
                    if 1 <= i <= n:
                        transposes(i - 1)
                    if 2 <= i <= n + 1:
                        values(i - 2)
                    if i - 3 in ends:
                        turn_pair(ends[i - 3])

            with pe.Fori(0, DEPTH) as l:
                ffn(l, T_A, CH_A, PC_A, "pre_a", "post_a", 0)
                mixer(l)
                ffn(l, T_B, CH_B, PC_B, "pre_b", "post_b", 18)

        N_ACT = 70

        @blk.scalar
        def _(act):
            A = nc.scalar.activation
            act.dma_start(onehot[0:32, :], d["onehot"]).then_inc(S["table_in"], 16)
            act.dma_start(relb[0:32, :], d["rel_bias"]).then_inc(S["table_in"], 16)
            act.wait_ge(S["tab_ps"], 1)
            A(topw_tab[0:H, :].rearrange("p (a b) -> p a b", a=2), PS[0:H, 0:2, 0:320], ACT.Copy).then_inc(S["tab_sb"], 1)
            act.wait_ge(S["init_ready"], 1)
            act.wait_ge(S["table_out"], 16)

            step = [0]

            def square(l, norm, k, src):
                act.wait_ge(S["sq_used"], l * N_SQ + NORMS[norm][1] + k + 1)
                A(sq[:, k % 2, :] if len(src.shape) == 2 else sq[:, k % 2, :].rearrange("p (a b) -> p a b", a=2),
                  src, ACT.Square).then_inc(S["sq_ready"], 1)

            def root(l, norm):
                j, q0, K = NORMS[norm]
                act.wait_ge(S["sq_used"], l * N_SQ + q0 + K + 2)
                A(rstd[:].rearrange("p (a b) -> p a b", a=2), unit(2)[:, :, 0:HALF], ACT.Sqrt, scale=1.0 / (K * P),
                  bias=eps_c[:]).then_inc(S["root"], 1)

            def pre_norm(l, norm, v):
                for k in range(KD):
                    act.wait_ge(S["xnew"], l * 24 + v * 8 + k + 1)
                    square(l, norm, k, xT[:, k, :])
                root(l, norm)

            def filled(l, u, turn):
                act.wait_ge(done[u], l * T_LAYER + turn + 1)

            def high_input(l, v, u):
                for k in range(KD):
                    act.wait_ge(S["u_norm"], (l * 3 + v) * KD + k + 1)
                    A(uT_r[:, k, 0:TOK], u[:, k, 0:TOK], ACT.Copy).then_inc(S["u_high"], 1)

            def high(ch, i, hs, at, n, l):
                act.wait_ge(loaded[ch % NSLOT], (l * (CH_LAYER // NSLOT) + ch // NSLOT + i + 1) * 16)
                A(piece_h[:, hs, 0:n], ring[:, ch % NSLOT, at:at + n], ACT.Copy).then_inc(S["w_high"], 1)

            def ffn(l, t0, c0, pre, post, v):
                ab = v // 2
                high(c0, 0, 0, 0, 1024, l)
                high(c0, 0, 1, 1024, 1024, l)
                pre_norm(l, pre, v)
                q = l * 2 + ab
                high_input(l, v, y_f)

                def silu(f, j):
                    act.wait_ge(vacated[1], l * T_LAYER + t0 + f + 1)
                    A(gate_s[:, j % 2, :].rearrange("p (a b) -> p a b", a=2), unit(0)[:, :, 0:HALF],
                      ACT.Silu).then_inc(vacated[0], 1)

                with act.Fori(0, 5) as i:
                    for j in range(4):
                        filled(l, 0, t0 + i * 4 + j)
                        high(c0 + j + 1, i, 0, 0, 1024, l)
                        silu(i * 4 + j, j)
                        filled(l, 1, t0 + i * 4 + j)
                        high(c0 + j + 1, i, 1, 1024, 1024, l)
                for f in (KF - 2, KF - 1):
                    filled(l, 0, t0 + f)
                    if f == KF - 2:
                        high(c0 + KF - 1, 0, 0, 0, 1024, l)
                    else:
                        high(c0 + KF, 0, 0, 0, PIECE, l)
                    silu(f, f)
                    filled(l, 1, t0 + f)
                    if f == KF - 2:
                        high(c0 + KF - 1, 0, 1, 1024, 1024, l)
                    else:
                        high(c0 + KF + 1, 0, 1, 0, PIECE, l)
                for n in range(KD):
                    u = n % 2
                    if n < KD - 1:
                        act.wait_ge(S["half_read"], q * KD + n + 1)
                        high(c0 + KF + 2 * n + 2, 0, 0, 0, PIECE, l)
                    filled(l, u, t0 + KF + n // 2)
                    if n < KD - 1:
                        high(c0 + KF + 2 * n + 3, 0, 1, 0, PIECE, l)
                    square(l, post, n, unit(u)[:, :, 0:HALF])
                    A(y_f[:, n, :].rearrange("p (a b) -> p a b", a=2), unit(u)[:, :, 0:HALF], ACT.Copy).then_inc(vacated[u], 1)
                root(l, post)

            def mixer(l):
                def high_in(i):
                    if i < 30:
                        ch, at, n = IN_PIECES[i]
                        high(CH_M + ch, 0, i % 2, at, n, l)
                    elif 78 <= i < 78 + KD:
                        ch, at, n = OUT_PIECES[i - 78]
                        high(CH_M + ch, 0, i % 2, at, n, l)

                high_in(0)
                high_in(1)
                pre_norm(l, "mix", 1)
                high_input(l, 1, u_norm_m)

                def unit_of(name):
                    return TILE[name] % 2

                def evac(name):
                    t = TILE[name]
                    u = t % 2
                    filled(l, u, T_M + t // 2)
                    if name in PIECE_OF:
                        high_in(PIECE_OF[name] + 2)
                    return u

                def to_keys(name, dst, at_hand=False):
                    u = unit_of(name) if at_hand else evac(name)
                    A(dst[:, 0:HALF], PS[:, 2 * u, 0:HALF], ACT.Copy)
                    A(dst[:, HALF:SEQ], PS[:, 2 * u + 1, 0:SEQ - HALF], ACT.Copy)
                    A(dst[:, KEY_NEW:NKEY], PS[:, 2 * u + 1, SEQ - HALF:HALF], ACT.Copy).then_inc(vacated[u], 1)

                def to_queries(name, dst, scale=1.0, at_hand=False):
                    u = unit_of(name) if at_hand else evac(name)
                    A(dst.rearrange("p (a b) -> p a b", a=2), unit(u)[:, :, 0:HALF], ACT.Copy, scale=scale).then_inc(vacated[u], 1)

                to_keys("kI", kI)
                for i in range(4):
                    u = evac(f"qI{i}")
                    A(qI[:, i, 0:HALF], PS[:, 2 * u, 0:HALF], ACT.Copy)
                    A(qI[:, i, HALF:SEQ], PS[:, 2 * u + 1, 0:SEQ - HALF], ACT.Copy)
                    A(qI[:, i, SEQ:SEQ + P].rearrange("p (a b) -> p a b", a=4),
                      PS[:, 2 * u + 1, SEQ - HALF:HALF].unsqueeze(1).broadcast_to([P, 4, NEW]), ACT.Copy).then_inc(vacated[u], 1)
                to_keys("kC", kC)
                for i in range(3):
                    act.wait_ge(S["v_step"], l * 3 + i + 1)
                    high_in(8 + i)
                evac("v0")
                high_in(11)
                for s in (2, 3, 4, 0, 1):
                    ins = A(VB[:, s if s < 4 else 6, :], PS[:, s, :], ACT.Copy)
                ins.then_inc(vacated[0], 1)
                evac("v1")
                high_in(12)
                vw = PS[:, 5, 0:360].rearrange("p (s n) -> p s n", s=5)
                A(VC[:, 0:4, :], vw[:, 0:4, 0:DH], ACT.Copy)
                A(VC[:, 6, :], vw[:, 4, 0:DH], ACT.Copy)
                A(wI[:], vw[:, :, DH:DH + H], ACT.Copy).then_inc(vacated[1], 1)
                i = 0
                for s in range(1, 5):
                    _, w = keys(s)
                    for h in range(H):
                        act.wait_ge(S["idx_done"], l * 32 + i + 1)
                        act.wait_ge(S["idx_acc"], l * 32 + i + 1)
                        A(rel[:, i % 2, 0:w], PS[:, 6 + i % 2, 0:w], ACT.Relu, scale=SCALE_I).then_inc(S["idx_rel"], 1)
                        i += 1
                for i in range(4):
                    to_queries(f"qC{i}", qC[:, i, :])
                for i in range(4):
                    to_queries(f"qB{i}", qB[:, i, :], scale=DH ** -0.5)
                for i in range(4):
                    to_keys(f"kB{i}", kB[:, i, :])
                act.wait_ge(S["idx_acc"], l * 32 + 34)
                to_queries("kr", kr_raw[:, 0, :])
                to_queries("krs", kr_raw[:, 1, :])
                for i in range(KQ):
                    u = evac(f"ql{i}")
                    square(l, "q", i, unit(u)[:, :, 0:HALF])
                    to_queries(f"ql{i}", ql[:, i, :], at_hand=True)
                root(l, "q")
                for i in range(KKV):
                    u = evac(f"kv{i}")
                    square(l, "kv", i, unit(u)[:, :, 0:HALF])
                    to_keys(f"kv{i}", ckv[:, i, :], at_hand=True)
                act.wait_ge(S["lat_ready"], l * 7 + 3)
                root(l, "kv")
                act.wait_ge(S["sel_ready"], l * 4 + 4)
                act.wait_ge(S["idx_done"], l * 32 + 32)
                act.wait_ge(S["rows_out"], 16 * (l * 14 + 14))
                branch_b(l)
                for i in range(4):
                    to_queries(f"uq{i}", qAn[:, i, :])
                for i in range(4):
                    u = evac(f"kA{i}")
                    A(kA[:, i, :].rearrange("p (a b) -> p a b", a=2), unit(u)[:, :, 0:NKEY // 2], ACT.Copy).then_inc(vacated[u], 1)
                for i, kts in enumerate(VA_KEYS):
                    u = evac(f"vA{i}")
                    if len(kts) == 2:
                        A(VA[:, kts[0]:kts[0] + 2, :], unit(u), ACT.Copy).then_inc(vacated[u], 1)
                    else:
                        m = P if kts[0] < 6 else NEW
                        A(VA[0:m, kts[0], :], PS[0:m, 2 * u, :], ACT.Copy).then_inc(vacated[u], 1)
                high(CH_M + 20, 0, 0, 0, 1024, l)
                high(CH_M + 20, 0, 1, 1024, 512, l)
                attend(l, 0)
                attend(l, 1)
                def gate(turn, j, next_high):
                    filled(l, 0, turn)
                    next_high(0)
                    act.wait_ge(vacated[1], l * T_LAYER + turn + 1)
                    A(sig[:, j % 2, :].rearrange("p (a b) -> p a b", a=2), unit(0)[:, :, 0:HALF],
                      ACT.Sigmoid).then_inc(vacated[0], 1)
                    filled(l, 1, turn)
                    next_high(1)

                with act.Fori(0, 5) as i:
                    for j in range(4):
                        gate(turn_of("g0_0") + j + i * 4, j,
                             lambda g: high(CH_M + 21 + j, i, g, g * 1024, (1024, 512)[g], l))
                for c in range(20, 24):
                    gate(turn_of("g0_0") + c, c,
                         lambda g: high(CH_M + 21 + c, 0, g, g * 1024, (1024, 512)[g] if c < 23 else 1024, l))
                for n in range(KD):
                    u = evac(f"wo{n}")
                    square(l, "mix_post", n, unit(u)[:, :, 0:HALF])
                    to_queries(f"wo{n}", y_m[:, n, :], at_hand=True)
                root(l, "mix_post")

            def branch_b(l):
                nb = l * (N_B + 3)
                st = l * 70
                alone(act)
                act.preload_act_table_set("natural_log_exp_and_others")

                def soft(n, rows, src, e):
                    act.wait_ge(S["sb_done"], nb + n + 1)
                    if n >= 2:
                        act.wait_ge(S["sb_sp_ready"], nb + n - 1)
                    A(e, src, ACT.Abs).then_inc(S["act_step"], 1)
                    act.wait_ge(S["act_step"], st + 2 * n + 1)
                    A(e, e, ACT.Exp, scale=-1.0).then_inc(S["act_step"], 1)
                    act.wait_ge(S["act_step"], st + 2 * n + 2)
                    A(e, e, ACT.Ln, bias=1.0).then_inc(S["sb_soft"], 1)

                def weights(t):
                    h, j = t // 4, 3 - t % 4
                    w, at = SEQ - P * j, 128 * ((3 - j) * (4 - j) // 2)
                    act.wait_ge(S["sb_cum"], nb + t + 1)
                    if t % 4 == 0:
                        act.wait_ge(S["sb_pv"], l * 9 + h + 1)
                    A(sb_a[:, h % 2, at:at + w], PS[:, t % 4, 0:w], ACT.Exp).then_inc(S["sb_a_ready"], 1)

                def out_pair(p):
                    act.wait_ge(S["sb_pv"], l * 9 + 2 * p + 4)
                    A(qB[:, p, 0:SEQ], PS[:, 4 + p % 2, :], ACT.Copy).then_inc(S["sb_out"], 1)

                for t in range(N_B + 2):
                    if t < N_B:
                        w = P * (t % 4 + 1)
                        soft(t, P, PS[:, t % 4, 0:w], sb_e[:, t % 2, 0:w])
                    if t >= 2:
                        weights(t - 2)
                    if t % 8 == 7 and t >= 15:
                        out_pair(t // 8 - 1)
                out_pair(3)
                rows = [NEW, P, P]
                for n in range(3):
                    m = rows[n]
                    kt = 2 - n
                    soft(N_B + n, m, PS[0:m, 2 * kt:2 * kt + 2, 0:P],
                         sb_e[0:m, (N_B + n) % 2, 0:2 * P].rearrange("p (a b) -> p a b", a=2))
                for n in range(3):
                    m = rows[n]
                    kt = 2 - n
                    act.wait_ge(S["sb_cum"], nb + N_B + n + 1)
                    A(sb_a[0:m, 0, 256 * n:256 * n + 256].rearrange("p (a b) -> p a b", a=2), PS[0:m, 2 * kt:2 * kt + 2, 0:P],
                      ACT.Exp).then_inc(S["sb_a_ready"], 1)
                act.wait_ge(S["sb_pv"], l * 9 + 8 + 3)
                A(qB[:, :, SEQ:TOK], PS[:, 6, 0:P].rearrange("p (a b) -> p a b", a=4), ACT.Copy).then_inc(S["sb_out"], 1)

            def attend(l, c):
                n0, q0 = l * N_UNIT + c * 34, l * N_PAIR + 5 * c
                dst = (qAn, qC)[c]

                def softmax(i):
                    p, s, e = UNITS[i]
                    w = keys(s)[1]
                    q = 5 * c + p
                    act.wait_ge(S["bias_ready"], n0 + i + 1)
                    if (s, e) in ((0, 0), (4, 0)):
                        act.wait_ge(S["heads_normed"], q0 + p + 1)
                    if c == 0:
                        act.wait_ge(S["pt_done"], n0 + i + 1)
                        src = PS[:, i % 2, 0:w]
                    else:
                        src = prob[:, i % 2, 0:w]
                    col = 2 * s + e if s < 4 else e
                    A(prob[:, i % 2, 0:w], src, ACT.Exp, scale=SCALE_A if c == 0 else 1.0, bias=nbias[:, i % 2:i % 2 + 1],
                      accum_out=sums[:, q % 2, col:col + 1]).then_inc(S["probs_ready"], 1)

                def copy_t(i):
                    copy_probs(act, lambda o, x: A(o, x, ACT.Copy), n0, i)

                def out_pair(p):
                    q = 5 * c + p
                    act.wait_ge(S["ot_done"], q0 + p + 3)
                    if p < 4:
                        A(dst[:, p, 0:SEQ], PS[:, 6 + q % 2, :], ACT.Copy).then_inc(S["branch_out"], 1)
                        return
                    for e in range(2):
                        ins = A(dst[DH * e:DH * e + DH, :, SEQ:TOK],
                                PS[0:DH, 6 + q % 2, 0:2 * P].rearrange("p (a e b) -> p e a b", a=4, e=2)[:, e], ACT.Copy)
                    ins.then_inc(S["branch_out"], 1)

                n = len(UNITS)
                ends = {7: 0, 15: 1, 23: 2, 31: 3, 33: 4}
                for i in range(n + 3):
                    if i < n:
                        softmax(i)
                    if c == 1 and 1 <= i <= n:
                        copy_t(i - 1)
                    if i - 3 in ends:
                        out_pair(ends[i - 3])

            act.wait_ge(S["x_in"], 16)
            with act.Fori(0, DEPTH) as l:
                ffn(l, T_A, CH_A, "pre_a", "post_a", 0)
                mixer(l)
                ffn(l, T_B, CH_B, "pre_b", "post_b", 2)

        N_DVE = [None]

        @blk.vector
        def _(dve):
            V = nc.vector
            V.memset(eps_c[:], EPS).then_inc(S["init_ready"], 1)
            dve.wait_ge(S["x_in"], 16)
            dve.sem_inc(S["xnew"], 8)
            dve.wait_ge(S["gain_in"], 16)
            dve.wait_ge(S["consts_in"], 32)

            per = DVE_STEPS
            count = [0]

            def link(l, ins):
                count[0] += 1
                ins.then_inc(S["dve_step"], 1)
                dve.wait_ge(S["dve_step"], l * per + count[0])
                alone(dve)

            def invert(l, norm):
                j = NORMS[norm][0]
                dve.wait_ge(S["root"], l * N_NORM + j + 2)
                V.reciprocal(rstd[:], rstd[:]).then_inc(S["inv"], 1)
                dve.wait_ge(S["inv"], l * N_NORM + j + 1)

            def pre_norm(l, norm, v, u_f, u_lo):
                invert(l, norm)
                c0 = NORMS[norm][1]

                def rest(k):
                    dve.wait_ge(S["u_high"], (l * 3 + v) * KD + k + 1)
                    V.tensor_tensor(u_lo[:, k, 0:TOK], u_f[:, k, 0:TOK], uT_r[:, k, 0:TOK].bitcast(F32), ALU.subtract).then_inc(S["hready"], 1)

                for k in range(KD):
                    V.scalar_tensor_tensor(out=u_f[:, k, 0:TOK], in0=xT[:, k, :], scalar=g_now[:, c0 + k:c0 + k + 1], in1=rstd[:],
                                           op0=ALU.mult, op1=ALU.mult).then_inc(S["u_norm"], 1)
                    if k:
                        rest(k - 1)
                rest(KD - 1)

            def post_norm(l, norm, y, half, n_y):
                invert(l, norm)
                c0 = NORMS[norm][1]
                for k in range(KD):
                    V.scalar_tensor_tensor(out=y[:, k, :], in0=y[:, k, :], scalar=g_now[:, c0 + k:c0 + k + 1], in1=rstd[:],
                                           op0=ALU.mult, op1=ALU.mult).then_inc(S["yscaled"], 1)
                for k in range(KD):
                    dve.wait_ge(S["yscaled"], l * 24 + n_y * 8 + k + 1)
                    V.scalar_tensor_tensor(out=xT[:, k, :], in0=y[:, k, :], scalar=0.5 if half else 1.0, in1=xT[:, k, :],
                                           op0=ALU.mult, op1=ALU.add).then_inc(S["xnew"], 1)

            def filled(l, u, turn):
                dve.wait_ge(done[u], l * T_LAYER + turn + 1)

            def ffn(l, t0, pre, post, n_y):
                pre_norm(l, pre, n_y, y_f, u_l)
                q = l * 2 + n_y // 2

                def gated(f, j):
                    filled(l, 1, t0 + f)
                    dve.wait_ge(vacated[0], l * T_LAYER + t0 + f + 3)
                    g, up = gate_s[:, j, :].rearrange("p (a b) -> p a b", a=2), unit(1)[:, :, 0:HALF]
                    hi = act_h[:, bass.ds(f, 1)].rearrange("p o n -> p (o n)")
                    lo = act_l[:, bass.ds(f, 1)].rearrange("p o n -> p (o n)")
                    V.tensor_tensor(hi.rearrange("p (a b) -> p a b", a=2), g, up, ALU.mult).then_inc(S["gate_step"], 1)
                    V.tensor_tensor(g, g, up, ALU.mult).then_inc(S["gate_step"], 1)
                    dve.wait_ge(S["gate_step"], q * 2 * KF + f * 2 + 2)
                    V.tensor_tensor(lo, gate_s[:, j, :], hi.bitcast(F32), ALU.subtract).then_inc(vacated[1], 1)

                with dve.Fori(0, KF // 2) as i:
                    gated(i * 2, 0)
                    gated(i * 2 + 1, 1)
                post_norm(l, post, y_f, True, n_y)

            def mixer(l):
                pre_norm(l, "mix", 1, u_norm_m, u_lm)
                dve.wait_ge(S["hready"], l * 26 + 16)
                for part in (uT_r, u_lm):
                    V.tensor_copy(part[:, :, TOK:SEQ + P].rearrange("p k (a b) -> p k a b", a=3),
                                  part[:, :, SEQ:TOK].bitcast(F32).unsqueeze(2).broadcast_to([P, KD, 3, NEW])).then_inc(S["hready"], 1)
                i = 0
                for s in range(1, 5):
                    w = MASK_W[s]
                    a = acc[:, ACC_AT[s]:ACC_AT[s] + w]
                    for h in range(H):
                        dve.wait_ge(S["idx_rel"], l * 32 + i + 3)
                        if h == 0:
                            V.tensor_scalar(a, rel[:, i % 2, 0:w], wI[:, s, h:h + 1], None, ALU.mult).then_inc(S["idx_acc"], 1)
                        else:
                            dve.wait_ge(S["idx_acc"], l * 32 + i + 2)
                            V.scalar_tensor_tensor(out=a, in0=rel[:, i % 2, 0:w], scalar=wI[:, s, h:h + 1], in1=a, op0=ALU.mult,
                                                   op1=ALU.add).then_inc(S["idx_acc"], 1)
                        i += 1
                dve.wait_ge(S["idx_acc"], l * 32 + 34)
                for s in range(1, 4):
                    w = MASK_W[s]
                    ins = V.memset(acc[0:CHUNK, ACC_AT[s] + w - CHUNK:ACC_AT[s] + w], LOWEST)
                link(l, ins)
                link(l, V.memset(msk[:, 0:P], 0.0))
                link(l, V.memset(msk[0:CHUNK, CHUNK:P], -BIG))
                for s in range(1, 5):
                    select(l, s)
                rotate_keys(l)
                invert(l, "q")
                for k in range(KQ):
                    V.scalar_tensor_tensor(out=ql[:, k, :], in0=ql[:, k, :], scalar=g_now[:, 24 + k:25 + k], in1=rstd[:],
                                           op0=ALU.mult, op1=ALU.mult).then_inc(S["lat_ready"], 1)
                invert(l, "kv")
                for k in range(KKV):
                    for a, b, c in ((0, SEQ, 0), (KEY_NEW, NKEY, SEQ)):
                        V.scalar_tensor_tensor(out=ckv[:, k, a:b], in0=ckv[:, k, a:b], scalar=g_now[:, 27 + k:28 + k],
                                               in1=rstd[:, c:c + b - a], op0=ALU.mult, op1=ALU.mult).then_inc(S["lat_ready"], 1)
                dve.wait_ge(S["rows_out"], 16 * (l * 14 + 14))
                branch_b(l)
                for g in range(2):
                    a2 = lambda v: v.rearrange("p (a b) -> p a b", a=2)
                    for e, (name, dst) in enumerate(((f"qr{g}", qAr[:, g, :]), (f"qs{g}", rope_t))):
                        u = TILE[name] % 2
                        filled(l, u, turn_of(name))
                        V.tensor_tensor(a2(dst), unit(u)[:, :, 0:HALF], a2(ropes[:, e, :]), ALU.mult).then_inc(vacated[u], 1)
                    for name in (f"qr{g}", f"qs{g}"):
                        dve.wait_ge(vacated[TILE[name] % 2], l * T_LAYER + turn_of(name) + 3)
                    V.tensor_tensor(qAr[:, g, :], qAr[:, g, :], rope_t, ALU.add).then_inc(S["qr_ready"], 1)
                    dve.wait_ge(S["qr_ready"], l * 2 + g + 1)
                attend(l, 0)
                attend(l, 1)
                dve.wait_ge(S["branch_out"], l * N_PAIR + N_PAIR + 2)
                V.tensor_copy(o_h[2][:], qC).then_inc(S["split_c"], 1)
                dve.wait_ge(S["split_c"], l * 2 + 1)
                V.tensor_tensor(o_l[2][:], qC, o_h[2][:].bitcast(F32), ALU.subtract).then_inc(S["split_c"], 1)
                halves = lambda v: v.rearrange("p (a b) -> p a b", a=2)
                with dve.Fori(0, 2) as i:
                    for j in range(4):
                        for b in range(3):
                            turn = turn_of("g0_0") + 3 * j + b + i * 12
                            filled(l, 1, turn)
                            dve.wait_ge(vacated[0], l * T_LAYER + turn + 3)
                            V.tensor_tensor(halves(mt[:, min(b, 1), :]), halves(sig[:, (3 * j + b) % 2, :]), unit(1)[:, :, 0:HALF],
                                            ALU.mult).then_inc(vacated[1], 1)
                            if b == 0:
                                continue
                            dve.wait_ge(vacated[1], l * T_LAYER + turn + 3)
                            if b == 2:
                                hi = merged_h[:, bass.ds(i * 4 + j, 1)].rearrange("p o n -> p (o n)")
                                lo = merged_l[:, bass.ds(i * 4 + j, 1)].rearrange("p o n -> p (o n)")
                                V.tensor_tensor(hi, mt[:, 0, :], mt[:, 1, :], ALU.add).then_inc(S["merge_step"], 1)
                            V.tensor_tensor(mt[:, 0, :], mt[:, 0, :], mt[:, 1, :], ALU.add).then_inc(S["merge_step"], 1)
                            dve.wait_ge(S["merge_step"], l * 3 * KD + i * 12 + 3 * j + (1 if b == 1 else 3))
                        V.tensor_tensor(lo, mt[:, 0, :], hi.bitcast(F32), ALU.subtract).then_inc(S["merge_ready"], 1)
                        dve.wait_ge(S["merge_ready"], l * KD + i * 4 + j + 1)
                post_norm(l, "mix_post", y_m, False, 1)

            def select(l, s):
                w, k = MASK_W[s], (TOPK if s < 4 else TOPK_S)
                a = acc[:, ACC_AT[s]:ACC_AT[s] + w]
                wk, eq, cu = topw[:, 0:w], eqv[:, 0:w], cum[:, 0:w]
                src = a
                for r in range(k // 8):
                    link(l, V.max(m8[:], src))
                    if r < k // 8 - 1:
                        link(l, V.match_replace(wk, m8[:], src, LOWEST))
                        src = wk
                link(l, V.tensor_scalar(wk, a, m8[:, 7:8], None, ALU.is_gt))
                link(l, V.tensor_reduce(cnt[:, 0:1], wk, AX_X, ALU.add))
                link(l, V.tensor_scalar(cnt[:, 1:2], cnt[:, 0:1], -1.0, float(k), ALU.mult, ALU.add))
                link(l, V.tensor_scalar(eq, a, m8[:, 7:8], None, ALU.is_equal))
                link(l, V.tensor_tensor_scan(cu, eq, eq, 0.0, ALU.add, ALU.max))
                link(l, V.scalar_tensor_tensor(out=cu, in0=cu, scalar=cnt[:, 1:2], in1=eq, op0=ALU.is_le, op1=ALU.mult))
                link(l, V.tensor_tensor(wk, wk, cu, ALU.add))
                V.tensor_scalar(msk[:, MASK_AT[s]:MASK_AT[s] + w], wk, -1.0, BIG, ALU.add, ALU.mult).then_inc(S["sel_ready"], 1)
                dve.wait_ge(S["sel_ready"], l * 4 + s)
                alone(dve)

            def rotate_keys(l):
                for name in ("kr", "krs"):
                    dve.wait_ge(vacated[TILE[name] % 2], l * T_LAYER + turn_of(name) + 3)
                link(l, V.tensor_tensor(kr_raw[:, 1, :], kr_raw[:, 1, :], ropes[:, 1, :], ALU.mult))
                V.tensor_tensor(rope_t, kr_raw[:, 0, :], ropes[:, 0, :], ALU.mult).then_inc(S["rope_step"], 1)
                dve.wait_ge(S["rope_step"], l * 3 + 1)
                for a, b, c in ((0, SEQ, 0), (KEY_NEW, NKEY, SEQ)):
                    V.tensor_tensor(kr[:, a:b], rope_t[:, c:c + b - a], kr_raw[:, 1, c:c + b - a], ALU.add).then_inc(S["rope_step"], 1)
                dve.wait_ge(S["rope_step"], l * 3 + 3)

            def branch_b(l):
                nb = l * (N_B + 3)
                for t in range(N_B + 3):
                    dve.wait_ge(S["sb_soft"], nb + t + 1)
                    if t < N_B:
                        h, j = t // 4, 3 - t % 4
                        w, at = SEQ - P * j, 128 * ((3 - j) * (4 - j) // 2)
                        if t % 4 == 0 and h >= 2:
                            dve.wait_ge(S["sb_cum"], nb + t - 4)
                        V.scalar_tensor_tensor(out=sb_sp[:, h % 2, at:at + w], in0=PS[:, t % 4, 0:w], scalar=0.0,
                                               in1=sb_e[:, t % 2, 0:w], op0=ALU.max, op1=ALU.add).then_inc(S["sb_sp_ready"], 1)
                    else:
                        n = t - N_B
                        kt, m = 2 - n, (NEW, P, P)[n]
                        if n == 0:
                            dve.wait_ge(S["sb_cum"], nb + N_B)
                        V.scalar_tensor_tensor(out=sb_sp[0:m, 0, 256 * n:256 * n + 256].rearrange("p (a b) -> p a b", a=2),
                                               in0=PS[0:m, 2 * kt:2 * kt + 2, 0:P], scalar=0.0,
                                               in1=sb_e[0:m, t % 2, 0:2 * P].rearrange("p (a b) -> p a b", a=2),
                                               op0=ALU.max, op1=ALU.add).then_inc(S["sb_sp_ready"], 1)
                dve.wait_ge(S["sb_out"], l * 5 + 5)

            def attend(l, c):
                n0, q0 = l * N_UNIT + c * 34, l * N_PAIR + 5 * c

                def bias(i):
                    p, s, e = UNITS[i]
                    w = keys(s)[1]
                    x = PS[:, i % 2, 0:w]
                    dve.wait_ge(S["s_done"], n0 + i + 1)
                    dve.wait_ge(S["probs_ready"], n0 + i + 1)
                    if c == 1:
                        h = 2 * p + e
                        if s == 0:
                            if h < 4:
                                dve.wait_ge(S["t5_in01"], (l * 4 + 4) * 16)
                            else:
                                dve.wait_ge(S[f"t5_in{h // 2}"], (l * 2 + 2) * 16)
                        if s == 4 and e == 0:
                            dve.wait_ge(S["t5s_in"], (l * 8 + 8) * 16)
                        t5 = T5[:, h % 4, 384 - P * s:384 - P * s + w] if s < 4 else T5s[:, e, :]
                        dve.wait_ge(S["pt_done"], n0 + i + 1)
                        x = prob[:, i % 2, 0:w]
                        link(l, V.scalar_tensor_tensor(out=x, in0=PS[:, i % 2, 0:w], scalar=SCALE_C, in1=t5, op0=ALU.mult,
                                                       op1=ALU.add))
                        link(l, V.tensor_tensor(x, x, msk[:, MASK_AT[s]:MASK_AT[s] + w], ALU.add))
                    link(l, V.tensor_reduce(mx[:, i % 2:i % 2 + 1], x, AX_X, ALU.max))
                    V.tensor_scalar(nbias[:, i % 2:i % 2 + 1], mx[:, i % 2:i % 2 + 1], -SCALE_A if c == 0 else -1.0, None,
                                    ALU.mult).then_inc(S["bias_ready"], 1)

                def normalise(p, i):
                    q = 5 * c + p
                    n = 8 if p < 4 else 2
                    dve.wait_ge(S["pv_done"], n0 + i + 3)
                    dve.wait_ge(S["probs_ready"], n0 + i + 3)
                    dve.wait_ge(S["ot_done"], q0 + p + 1)
                    link(l, V.reciprocal(rinv[:, q % 2, 0:n], sums[:, q % 2, 0:n]))
                    V.tensor_tensor(OT[:, q % 2, 0:n * DH].rearrange("p (a b) -> p a b", a=n),
                                    PS[:, 4 + q % 2, 0:n * DH].rearrange("p (a b) -> p a b", a=n),
                                    rinv[:, q % 2, 0:n].unsqueeze(2).broadcast_to([P, n, DH]), ALU.mult).then_inc(S["heads_normed"], 1)

                n = len(UNITS)
                ends = {7: 0, 15: 1, 23: 2, 31: 3, 33: 4}
                for i in range(n + 2):
                    if i < n:
                        bias(i)
                    if c == 0 and 1 <= i <= n:
                        copy_probs(dve, V.tensor_copy, n0, i - 1)
                    if i - 2 in ends:
                        normalise(ends[i - 2], i - 2)

            with dve.Fori(0, DEPTH) as l:
                count[0] = 0
                link(l, V.tensor_copy(g_now[:], gain[:, bass.ds(l, 1), :].rearrange("p o n -> p (o n)")))
                ffn(l, T_A, "pre_a", "post_a", 0)
                mixer(l)
                ffn(l, T_B, "pre_b", "post_b", 2)
                assert count[0] == per, count[0]


DVE_STEPS = (1 + 1 + 2 + sum(2 * (k // 8) - 1 + 7 for k in (TOPK, TOPK, TOPK, TOPK_S)) + 1
             + len(UNITS) * (1 + 3) + N_PAIR)


def t5_buckets():
    rel = np.arange(NREL) - (SEQ - 1)
    nb, max_exact = 16, 8
    n = np.abs(rel)
    large = max_exact + (np.log(np.maximum(n, 1).astype(np.float32) / np.float32(max_exact)) / np.float32(math.log(256 / max_exact))
                         * np.float32(nb - max_exact)).astype(np.int32)
    return np.where(rel > 0, nb, 0) + np.where(n < max_exact, n, np.minimum(large, nb - 1))


def shape_constants():
    onehot = np.zeros((32, NREL), np.float32)
    onehot[t5_buckets(), np.arange(NREL)] = 1
    k, q = np.arange(P)[:, None], np.arange(P)[None, :]
    cst = np.zeros((P, 6, P), np.float32)
    cst[:, 0] = 1
    cst[:, 1] = -1
    cst[:, 2] = np.where(k >= q, -1, 0)
    cst[:, 3] = np.eye(P)
    cst[:, 4] = np.where(k >= q, -BIG, 0)
    cst[:, 5] = np.where((k < CHUNK) & (q >= CHUNK), -BIG, 0)
    pos = np.concatenate([np.arange(SEQ), PAST + np.arange(NEW)]).astype(np.float32)
    half = ROPE // 2
    inv = np.float32(10000.0) ** (-np.arange(half, dtype=np.float32) / np.float32(half))
    ang = pos[None, :] * inv[:, None]
    c, s = np.cos(ang), np.sin(ang)
    ropes = np.stack([np.tile(np.concatenate([c, c]), (4, 1)), np.tile(np.concatenate([-s, s]), (4, 1))], axis=1)
    return onehot, cst, np.ascontiguousarray(ropes.astype(np.float32))


def kernel(**inputs):
    from concourse import bacc as _bacc
    from concourse.bass_utils import run_bass_kernel_spmd as _run

    a = {k: np.asarray(v) for k, v in inputs.items()}
    L = DEPTH
    onehot, cst, ropes = shape_constants()

    at = np.concatenate([[0], np.cumsum([384, 256, 32, 512, 512, 512, 512, 64, 64, 512, 64, 8, 1024, 1024, 1024])])
    part = {n: np.arange(at[i], at[i + 1]) for i, n in enumerate(
        ["ql", "kv", "kr", "qb", "kb", "vb", "qc", "kc", "vc", "qi", "ki", "wi", "ga", "gb", "gc"])}
    swap = np.concatenate([np.arange(16, 32), np.arange(16)])
    krs = part["kr"][swap]
    cols = np.concatenate([part["ki"], part["ki"], part["qi"], part["kc"], part["kc"], part["qc"], part["qb"], part["kb"],
                           part["kr"], part["kr"], part["kr"], part["kr"], krs, krs, krs, krs, part["ql"], part["kv"], part["kv"][:128]])
    w_in = a["w_in"].reshape(L, KD, P, -1)

    def tiles(w, n):
        k = w.shape[1]
        return w.reshape(L, k, P, n, P).transpose(0, 3, 2, 1, 4).reshape(L, n, P, k * P)

    def groups(w, g):
        n, f = w.shape[1], w.shape[3]
        return w.reshape(L, n // g, g, P, f).transpose(0, 1, 3, 2, 4).reshape(L, n // g, P, g * f)

    uq = a["w_mla_uq"].reshape(L, KQ, P, H * 96)
    h = np.arange(H)[:, None]
    nope = (h * 96 + np.arange(64)).reshape(-1)
    rp = h * 96 + 64 + np.arange(32)
    rs = h * 96 + 64 + swap
    uq_cols = np.concatenate([nope, rp[:4].reshape(-1), rs[:4].reshape(-1), rp[4:].reshape(-1), rs[4:].reshape(-1)])
    ukv = a["w_mla_ukv"].reshape(L, KKV, P, H * 128)
    un = (h * 128 + np.arange(64)).reshape(-1)
    uv = (h * 128 + 64 + np.arange(64)).reshape(-1)
    gates = np.stack([tiles(w_in[..., part[g]], KD) for g in ("ga", "gb", "gc")], axis=2)
    br = a["w_branch"].reshape(L, 3, 4, P, KD, P).transpose(0, 4, 1, 3, 2, 5).reshape(L, KD, 3, P, 4 * P)
    vcwi = np.concatenate([part["vc"], part["wi"]])

    def gcols(g):
        return g.reshape(L, -1, P).transpose(2, 0, 1)

    def feat(x):
        return x.reshape(L, PAST, -1).transpose(0, 2, 1)

    def tokm(x):
        return x.reshape(L, 2, P, -1).transpose(0, 2, 1, 3)

    f = a["ffn_pre_gain"]
    g = a["ffn_post_gain"]
    arrays = {
        "x": np.concatenate([a["x_prompt"][0], a["x_sample"][0]]).T.reshape(KD, P, TOK).transpose(1, 0, 2),
        "cst": cst, "ropes": ropes, "onehot": onehot, "rel_bias": a["rel_bias"],
        "gains": np.concatenate([gcols(v) for v in (f[:, 0], g[:, 0], a["mix_pre_gain"], a["mla_q_norm"], a["mla_kv_norm"],
                                                    a["mix_post_gain"], f[:, 1], g[:, 1])], axis=2),
        "w_up": a["w_ffn_up"].reshape(L, 2, KD, P, 2, KF, P).transpose(0, 1, 5, 3, 4, 2, 6).reshape(L, 2 * KF, P, 2048),
        "w_dn": a["w_ffn_down"].reshape(L, 2, 2, 11, P, KD, P).transpose(0, 1, 5, 2, 4, 3, 6).reshape(L, 32, P, 1408),
        "w_in": groups(tiles(w_in[..., cols], 26), 2),
        "w_vb": w_in[..., part["vb"]].reshape(L, 2, 4, P, 512).transpose(0, 1, 3, 2, 4).reshape(L, 2, P, 2048),
        "w_vc": w_in[..., vcwi].transpose(0, 2, 1, 3).reshape(L, 1, P, 576),
        "w_uq": groups(tiles(uq[..., uq_cols], 8), 4),
        "w_ukn": groups(tiles(ukv[..., un], 4), 4),
        "w_ukv": ukv[..., uv].transpose(0, 2, 1, 3).reshape(L, 1, P, 1024),
        "w_mg": np.concatenate([gates, br], axis=4).reshape(L, 3 * KD, P, 1536),
        "w_out": groups(tiles(a["w_o"].reshape(L, KD, P, D), KD), 2),
        "c_kidx": np.concatenate([feat(a["cache_dsa_kidx"])] * 2, axis=1)[:, :, None],
        "c_dsk": np.concatenate([feat(a["cache_dsa_k"])] * 2, axis=1)[:, :, None],
        "c_dsv": tokm(a["cache_dsa_v"]),
        "c_sbk": feat(a["cache_sb_k"]).reshape(L, 4, P, PAST).transpose(0, 2, 1, 3),
        "c_sbv": tokm(a["cache_sb_v"]),
        "c_kr": np.concatenate([feat(a["cache_mla_krope"])] * 4, axis=1)[:, :, None],
        "c_ckv": feat(a["cache_mla_ckv"]).reshape(L, KKV, P, PAST).transpose(0, 2, 1, 3),
    }
    outs = {"y": (P, KD, TOK), "o_kr": (L, ROPE, TOK),
            "p_ki": (L, DH, 1, SEQ), "s_ki": (L, DH, 1, NEW), "p_kc": (L, DH, 1, SEQ), "s_kc": (L, DH, 1, NEW),
            "p_vb": (L, P, 4, 512), "s_vb": (L, NEW, 1, 512), "p_vc": (L, P, 4, DH), "s_vc": (L, NEW, 1, DH),
            "p_kb": (L, P, 4, SEQ), "s_kb": (L, P, 4, NEW), "p_ckv": (L, P, 2, SEQ), "s_ckv": (L, P, 2, NEW)}

    nc = _bacc.Bacc("TRN2", target_bir_lowering=False, num_devices=1)
    arrays = {f"in_{k}": np.ascontiguousarray(v) for k, v in arrays.items()}
    dram = {k[3:]: nc.dram_tensor(k, v.shape, F32, kind="ExternalInput").ap() for k, v in arrays.items()}
    dram |= {k: nc.dram_tensor(f"out_{k}", v, F32, kind="ExternalOutput").ap() for k, v in outs.items()}
    dram["t5"] = nc.dram_tensor("t5_by_distance", (H, P, NREL), F32, kind="Internal").ap()
    build(nc, dram)
    r = {k: _run_out for k, _run_out in _run(nc, [arrays], core_ids=[0]).results[0].items()}
    o = {k: r[f"out_{k}"] for k in outs}
    y = o["y"].transpose(2, 1, 0).reshape(TOK, D)

    def rows(v, width):
        return v.transpose(0, 3, 2, 1).reshape(L, 1, v.shape[3], width)

    def token_rows(v, width):
        return v.transpose(0, 2, 1, 3).reshape(L, 1, -1, width)

    def group(c, sl):
        return (rows(o[f"{c}_ckv"], KV_LORA), o["o_kr"][:, :, sl].transpose(0, 2, 1)[:, None],
                rows(o[f"{c}_kb"], MIX).reshape(L, 1, -1, H, DH), token_rows(o[f"{c}_vb"], MIX).reshape(L, 1, -1, H, DH),
                rows(o[f"{c}_kc"], DH), token_rows(o[f"{c}_vc"], DH), rows(o[f"{c}_ki"], DH))

    return tuple(np.ascontiguousarray(v) for v in (
        y[None, :SEQ], y[None, SEQ:], *group("p", slice(0, SEQ)), *group("s", slice(SEQ, TOK))))
```

```python
import math
from contextlib import ExitStack

import numpy as np

import concourse.bass as bass
from concourse import mybir

F32 = mybir.dt.float32
F32R = mybir.dt.float32r
BF16 = mybir.dt.bfloat16
ALU = mybir.AluOpType
ACT = mybir.ActivationFunctionType
AX_X = mybir.AxisListType.X

P = 128
DEPTH, D, D_FF = 2, 1024, 2816
SEQ, NEW, PAST = 512, 32, 256
TOK = SEQ + NEW
HALF = TOK // 2
NKEY = SEQ + PAST + NEW
KEY_NEW = SEQ + PAST
CHUNK, QB = 64, 128
NBLK = SEQ // QB
H, DH, ROPE = 8, 64, 32
Q_LORA, KV_LORA = 384, 256
MIX = H * DH
KD, KF = D // P, D_FF // P
KQ, KKV = Q_LORA // P, KV_LORA // P
EPS = 1e-6
TOPK = min(256, SEQ // 4)
TOPK_S = min(256, (PAST + NEW) // 4)
BIG = 1.0e30
LOWEST = -3.0e38
SCALE_A = (64 + 32) ** -0.5
SCALE_C = DH ** -0.5
SCALE_I = DH ** -0.5 * H ** -0.5
NREL = 640
W_S = PAST + NEW

SLOT = 2048
NSLOT = 4
CH_FFN = KF + 2 * KD
CH_MIX = 48
CH_LAYER = 2 * CH_FFN + CH_MIX
assert CH_LAYER % NSLOT == 0
CH_A, CH_M, CH_B = 0, CH_FFN, CH_FFN + CH_MIX

PC_FFN = 2 * KF + 2 * KD
PC_MIX = 30 + 48 + 8
PC_A, PC_M, PC_B = 0, PC_FFN, PC_FFN + PC_MIX
PC_LAYER = 2 * PC_FFN + PC_MIX
PIECE = 1408

T_FFN = (2 * KF + KD) // 2
T_MIX = 50
T_LAYER = 2 * T_FFN + T_MIX
T_A, T_M, T_B = 0, T_FFN, T_FFN + T_MIX

NORMS = {"pre_a": (0, 0, 8), "post_a": (1, 8, 8), "mix": (2, 16, 8), "q": (3, 24, 3), "kv": (4, 27, 2),
         "mix_post": (5, 29, 8), "pre_b": (6, 37, 8), "post_b": (7, 45, 8)}
N_NORM, N_SQ = 8, 53

UNITS = [(p, s, e) for p in range(4) for s in range(NBLK) for e in range(2)] + [(4, 4, 0), (4, 4, 1)]
N_UNIT = 2 * len(UNITS)
N_PAIR = 10
N_B = H * NBLK
MASK_AT = [0, 128, 384, 768, 1280]
MASK_W = [128, 256, 384, 512, W_S]
ACC_AT = {1: 0, 2: 256, 3: 640, 4: 1152}


def mixer_tiles():
    t = ["kI"] + [f"qI{i}" for i in range(4)] + ["kC", "vw", "v0", "v1"]
    t += [f"qC{i}" for i in range(4)] + [f"qB{i}" for i in range(4)] + [f"kB{i}" for i in range(4)]
    t += ["kr", "krs"] + [f"ql{i}" for i in range(KQ)] + [f"kv{i}" for i in range(KKV)]
    t += [f"uq{i}" for i in range(4)] + ["qr0", "qs0", "qr1", "qs1"]
    t += [f"kA{i}" for i in range(4)] + [f"vA{i}" for i in range(4)]
    for n in range(KD):
        t += [f"g0_{n}", f"b0_{n}", f"g1_{n}", f"b1_{n}", f"g2_{n}", f"b2_{n}"]
    return t + [f"wo{n}" for n in range(KD)]


TILES = mixer_tiles()
assert len(TILES) == 2 * T_MIX
TILE = {name: i for i, name in enumerate(TILES)}
MIX_CHUNKS = ([("w_in", i, 2048, TILES[2 * i + 1]) for i in range(3)]
              + [("w_vw", 0, 1024, "vw"), ("w_vb", 0, 2048, "v1"), ("w_vb", 1, 2048, "v1")]
              + [("w_in", 3 + i, 2048 if i < 9 else 1024, TILES[min(10 + 2 * i, 27)]) for i in range(10)]
              + [("w_uq", 0, 1536, "uq3"), ("w_uq", 1, 1536, "qs1"), ("w_ukn", 0, 1024, "kA3"), ("w_ukv", 0, 1024, "vA3")]
              + [("w_mg", 3 * n + b, 1536, f"b{b}_{n}") for n in range(KD) for b in range(3)]
              + [("w_out", i, 2048, f"wo{2 * i + 1}") for i in range(4)])
assert len(MIX_CHUNKS) == CH_MIX
IN_PIECES = ([(i // 2, (i % 2) * 1024, 1024) for i in range(6)]
             + [(3, 0, 1024)] + [(4 + i // 2, (i % 2) * 1024, 1024) for i in range(4)]
             + [(6 + i // 2, (i % 2) * 1024, 1024) for i in range(19)])
OUT_PIECES = [(44 + i // 2, (i % 2) * 1024, 1024) for i in range(KD)]
PIECE_OF = {t: i for i, t in enumerate(TILES[:7])} | {t: 11 + i for i, t in enumerate(TILES[9:28])} | {f"wo{n}": 78 + n for n in range(KD)}
VA_KEYS = [(0, 1), (2, 3), (4, 5), (6,)]


def build(nc, d):
    with ExitStack() as ctx:
        def sb(name, shape, dt=F32):
            return ctx.enter_context(nc.sbuf_tensor(name, shape, dt))

        def sem(name):
            return ctx.enter_context(nc.semaphore(name))

        PS = ctx.enter_context(nc.psum_tensor("PS", [P, 8, 512], F32))
        xT = sb("xT", [P, KD, TOK])
        uT_at = nc.sbuf_base
        uT = sb("uT", [P, KD, SEQ + P])
        uT_r = nc.alloc_sbuf_tensor_at("uT_r", [P, KD, SEQ + P], F32R, offset=uT_at)
        ring_at = nc.sbuf_base
        ring = sb("ring", [P, NSLOT, SLOT])
        ring_r = nc.alloc_sbuf_tensor_at("ring_r", [P, NSLOT, SLOT], F32R, offset=ring_at)
        cst = sb("cst", [P, 6, P])
        ropes = sb("ropes", [P, 2, TOK])
        gain = sb("gain", [P, DEPTH, N_SQ])
        g_now = sb("g_now", [P, N_SQ])
        sq = sb("sq", [P, 2, TOK])
        rstd = sb("rstd", [P, TOK])
        eps_c = sb("eps_c", [P, 1])
        m8 = sb("m8", [P, 8])
        cnt = sb("cnt", [P, 4])
        mx = sb("mx", [P, 2])
        nbias = sb("nbias", [P, 2])
        sums = sb("sums", [P, 2, 8])
        rinv = sb("rinv", [P, 2, 8])
        ARENA = 31560
        arena_at = nc.sbuf_base
        arena = sb("arena", [P, ARENA])

        ones, neg_ones, neg_tri, ident, sb_mask, chunk_mask = (cst[:, i, :] for i in range(6))

        def region_r(name, at, *shape):
            return nc.alloc_sbuf_tensor_at(name, [P, *shape], F32R, offset=arena_at + 4 * at)

        def region(at, *shape):
            n = int(np.prod(shape))
            v = arena[:, at:at + n]
            if len(shape) == 2:
                v = v.rearrange("p (a b) -> p a b", a=shape[0])
            return v

        act_h = region_r("act_h", 0, KF, TOK)
        act_l = region_r("act_l", KF * TOK, KF, TOK)
        y_f = region(2 * KF * TOK, KD, TOK)
        u_l = region_r("u_l", 2 * KF * TOK, KD, TOK)
        piece_h = region_r("piece_h", (ARENA - 2 * PIECE) // 8 * 8, 2, PIECE)
        gate_s = sq
        u_norm_m = region(23448, KD, SEQ + P)
        u_lm = region_r("u_lm", 23448, KD, SEQ + P)
        VB = region(0, 7, 512)
        VC = region(3584, 7, DH)
        kC = region(4032, NKEY)
        qC = region(4832, 4, TOK)
        qB = region(7008, 4, TOK)
        kB = region(9184, 4, NKEY)
        kr = region(12384, NKEY)
        msk = arena[:, 13536:13536 + 784].bitcast(BF16)
        ckv = region(14320, KKV, NKEY)
        qI = region(15920, 4, SEQ + P)
        ql = region(15920, KQ, TOK)
        rope_t = region(17552, TOK)
        kI = region(18480, NKEY)
        wI = region(19280, 5, H)
        acc = region(19320, 1440)
        topw = region(20760, 512)
        eqv = region(21272, 512)
        cum = region(21784, 512)
        rel = region(22296, 2, 512)
        vw_f = region(22296, SEQ + P)
        kr_raw = region(22296, 2, TOK)
        sb_sp = region(17552, 2, 1280)
        sb_a = region(20112, 2, 1280)
        sb_e = sq[:, :, 0:512]
        VA = region(0, 7, 512)
        kA = region(9184, 4, NKEY)
        qAr = region(20184, 2, TOK)
        qAn = region(21272, 4, TOK)
        prob = region(14320, 2, 512)
        probT = region(15344, 2, 512)
        OT = region(16368, 2, 512)
        T5 = region(17552, 4, 512)
        T5s = region(19600, 2, W_S)
        topw_tab = region(0, NREL)
        onehot = region(NREL, NREL)
        relb = region(2 * NREL, H)
        ident_r = region_r("ident_r", 13184, P)
        sb_mask_r = region_r("sb_mask_r", 13312, P)
        chunk_mask_r = region_r("chunk_mask_r", 28568, P)
        o_l = [region_r(f"o_l{b}", at, 4, TOK) for b, at in enumerate((21272, 7008, 4832))]
        o_h = [region_r(f"o_h{b}", at, 4, TOK) for b, at in enumerate((11360, 9184, 13536))]
        merged_l = region_r("merged_l", 0, KD, TOK)
        merged_h = region_r("merged_h", 15712, KD, TOK)
        mt = region(20064, 2, TOK)
        y_m = region(4832, KD, TOK)
        sig = sq

        S = {n: sem(n) for n in (
            "consts_in", "x_in", "gain_in", "table_out", "table_in", "gain_now", "xnew", "hready", "sq_ready", "sq_used",
            "root", "inv", "yscaled", "cache_in", "rows_out", "y_out", "idx_done", "idx_rel", "idx_acc",
            "sel_ready", "lat_ready", "rope_step", "qr_ready", "dve_step", "act_step", "sb_done", "sb_soft",
            "sb_sp_ready", "sb_cum", "sb_a_ready", "sb_pv", "sb_out", "s_done", "bias_ready", "probs_ready",
            "pt_done", "pt_copied", "pv_done", "heads_normed", "ot_done", "branch_out", "t5_in01", "t5_in2", "t5_in3", "t5s_in",
            "merge_ready", "merge_step", "init_ready", "tab_ps", "tab_sb", "u_norm", "u_high",
            "w_high", "w_low", "half_read", "gate_step", "v_step", "split", "split_c", "vw_turned", "rows_ki", "silu_done", "ropes_in", "masks_ready")}
        done = [sem("tile_done0"), sem("tile_done1")]
        vacated = [sem("tile_vacated0"), sem("tile_vacated1")]
        loaded = [sem(f"slot_loaded{i}") for i in range(NSLOT)]
        blk = ctx.enter_context(nc.Block())

        def alone(eng):
            eng.nop(nofuse=True)

        def unit(u):
            return PS[:, 2 * u:2 * u + 2, :]

        def turn_of(name):
            return T_M + TILE[name] // 2

        def keys(s):
            return (SEQ, W_S) if s == 4 else (0, QB * (s + 1))

        def score_bank(c, i):
            return (0, 1, 6)[(len(UNITS) * c + i) % 3]

        def probs(c, i):
            j = (len(UNITS) * c + i) % 3
            return prob[:, j, :] if j < 2 else sq[:, 0, 0:512]

        def key_tiles(s):
            k0, w = keys(s)
            return [(k0 + 128 * t, min(128, w - 128 * t), 128 * t, (4 + t) if s == 4 else t)
                    for t in range((w + 127) // 128)]

        def copy_probs(eng, copy, n0, i):
            eng.wait_ge(S["pt_done"], n0 + i + 4)
            eng.wait_ge(S["pv_done"], n0 + i + 1)
            tiles = key_tiles(UNITS[i][1])
            full = [t for t in tiles if t[1] == P]
            ins = copy(probT[:, i % 2, 0:P * len(full)], PS[:, 2 + i % 2, 0:P * len(full)])
            for _, m, at, _ in tiles[len(full):]:
                ins = copy(probT[0:m, i % 2, at:at + P], PS[0:m, 2 + i % 2, at:at + P])
            ins.then_inc(S["pt_copied"], 1)

        @blk.sync
        def _(sp):
            sp.dma_start(xT[:], d["x"]).then_inc(S["x_in"], 16)
            sp.dma_start(cst[:], d["cst"]).then_inc(S["consts_in"], 16)
            sp.dma_start(gain[:], d["gains"]).then_inc(S["gain_in"], 16)

            def load(src, n, ch):
                slot = ch % NSLOT
                sp.dma_start(ring[:, slot, 0:n], src).then_inc(loaded[slot], 16)

            def one(name, l, i):
                return d[name][bass.ds(l, 1), bass.ds(i, 1)].rearrange("l c p n -> p (l c n)")

            def consumed(l, u, turn):
                sp.wait_ge(done[u], l * T_LAYER + turn + 1)

            for f in range(NSLOT):
                load(one("w_up", 0, f), 2048, f)
            sp.dma_start(ropes[:], d["ropes"]).then_inc(S["ropes_in"], 16)

            def ffn(l, ab, t0, c0, after):
                w0 = ab * KF
                with sp.Fori(0, 4) as i:
                    for j in range(4):
                        consumed(l, 1, t0 + i * 4 + j)
                        load(one("w_up", l, w0 + i * 4 + j + 4), 2048, c0 + j)
                for f in range(16, KF - 4):
                    consumed(l, 1, t0 + f)
                    load(one("w_up", l, w0 + f + 4), 2048, c0 + f)
                for f in range(KF - 4, KF):
                    consumed(l, 1, t0 + f)
                    load(one("w_dn", l, ab * 16 + f - KF + 4), 1408, c0 + f)
                with sp.Fori(0, 3) as i:
                    for j in range(4):
                        if j % 2 == 0:
                            consumed(l, j // 2, t0 + KF + i)
                        load(one("w_dn", l, ab * 16 + i * 4 + j + 4), 1408, c0 + KF + j)
                for j in range(4):
                    if j % 2 == 0:
                        consumed(l, j // 2, t0 + KF + 3)
                    after(j, c0 + KF + 12 + j)

            def mixer(l):
                for k in range(CH_MIX):
                    u, turn = TILE[MIX_CHUNKS[k][3]] % 2, turn_of(MIX_CHUNKS[k][3])
                    consumed(l, u, turn)
                    if k + NSLOT < CH_MIX:
                        name, i, n, _ = MIX_CHUNKS[k + NSLOT]
                        load(one(name, l, i)[:, 0:n], n, CH_M + k)
                    else:
                        load(one("w_up", l, KF + k + NSLOT - CH_MIX), 2048, CH_M + k)

            with sp.Fori(0, DEPTH) as l:
                ffn(l, 0, T_A, CH_A, lambda j, ch: load(one(MIX_CHUNKS[j][0], l, MIX_CHUNKS[j][1]), MIX_CHUNKS[j][2], ch))
                mixer(l)
                ffn(l, 1, T_B, CH_B, lambda j, ch: load(one("w_up", l * -1 + (DEPTH - 1), j), 2048, ch))
            sp.wait_ge(S["xnew"], 8 + DEPTH * 24)
            sp.dma_start(d["y"], xT[:]).then_inc(S["y_out"], 16)
            sp.wait_ge(S["y_out"], 16)
            for i in range(NSLOT):
                sp.wait_ge(loaded[i], 16 * (DEPTH * CH_LAYER // NSLOT + 1))

        N_CACHE = 7

        @blk.gpsimd
        def _(pool):
            pool.wait_ge(S["tab_sb"], 1)
            pool.dma_start(d["t5"], topw_tab[0:H, :].unsqueeze(1).broadcast_to([H, P, NREL])).then_inc(S["table_out"], 16)
            pool.wait_ge(S["table_out"], 16)

            def t5_sem(h):
                return "t5_in01" if h < 4 else f"t5_in{h // 2}"

            def toeplitz(h, rows, c0, n):
                return bass.AP(d["t5"].tensor, h * P * NREL + c0 + P - 1, [[NREL - 1, rows], [1, n]])

            def low(l, p0, i, ch, at, n):
                pool.wait_ge(S["w_high"], l * PC_LAYER + p0 + i + 1)
                hi, w = piece_h[:, ch[1], 0:n].bitcast(F32), ring[:, ch[0] % NSLOT, at:at + n]
                nc.gpsimd.tensor_tensor(ring_r[:, ch[0] % NSLOT, at:at + n], w, hi, ALU.subtract).then_inc(S["w_low"], 1)

            def ffn(l, p0, c0):
                with pool.Fori(0, 5) as i:
                    for j in range(8):
                        low(l, p0, i * 8 + j, (c0 + j // 2, j % 2), (j % 2) * 1024, 1024)
                for j in range(40, 2 * KF):
                    low(l, p0, j, (c0 + j // 2, j % 2), (j % 2) * 1024, 1024)
                for j in range(2 * KD):
                    low(l, p0, 2 * KF + j, (c0 + KF + j, j % 2), 0, PIECE)

            with pool.Fori(0, DEPTH) as l:
                ffn(l, PC_A, CH_A)

                def lows(a, b):
                    for i in range(a, b):
                        ch, at, n = IN_PIECES[i]
                        low(l, PC_M, i, (CH_M + ch, i % 2), at, n)

                lows(0, 2)

                def cached(dst, name):
                    pool.dma_start(dst, d[name][bass.ds(l, 1)].rearrange(
                        "l p a b -> p (l a) b" if len(dst.shape) == 3 else "l p a b -> p (l a b)")).then_inc(S["cache_in"], 16)

                pool.wait_ge(S["xnew"], l * 24 + 16)
                alone(pool)
                cached(kI[:, SEQ:KEY_NEW], "c_kidx")
                cached(kC[:, SEQ:KEY_NEW], "c_dsk")
                cached(VC[:, 4:6, :], "c_dsv")
                cached(kB[:, :, SEQ:KEY_NEW], "c_sbk")
                cached(VB[:, 4:6, :], "c_sbv")
                cached(kr[:, SEQ:KEY_NEW], "c_kr")
                cached(ckv[:, :, SEQ:KEY_NEW], "c_ckv")

                def row(name, src, out="rows_out"):
                    dst = d[name][bass.ds(l, 1)]
                    dst = dst.rearrange("l p a b -> p (l a) b" if len(src.shape) == 3 else "l p a b -> p (l a b)")
                    pool.dma_start(dst, src).then_inc(S[out], 16)

                def evacuated(name):
                    pool.wait_ge(vacated[TILE[name] % 2], l * T_LAYER + turn_of(name) + 3)
                    alone(pool)

                lows(2, 4)
                evacuated("kI")
                row("p_ki", kI[0:DH, 0:SEQ], "rows_ki")
                row("s_ki", kI[0:DH, KEY_NEW:NKEY], "rows_ki")
                lows(4, 13)
                evacuated("v0")
                evacuated("v1")
                evacuated("kC")
                row("p_kc", kC[0:DH, 0:SEQ])
                row("s_kc", kC[0:DH, KEY_NEW:NKEY])
                row("p_vb", VB[:, 0:4, :])
                row("s_vb", VB[0:NEW, 6, :])
                row("p_vc", VC[:, 0:4, :])
                row("s_vc", VC[0:NEW, 6, :])
                lows(13, 26)
                evacuated("kB3")
                evacuated("kB2")
                row("p_kb", kB[:, :, 0:SEQ])
                row("s_kb", kB[:, :, KEY_NEW:NKEY])
                lows(26, 30)
                pool.wait_ge(S["rope_step"], l * 3 + 3)
                alone(pool)
                pool.dma_start(d["o_kr"][bass.ds(l, 1)].rearrange("l p b -> p (l b)")[:, 0:SEQ], kr[0:ROPE, 0:SEQ]).then_inc(S["rows_out"], 16)
                pool.dma_start(d["o_kr"][bass.ds(l, 1)].rearrange("l p b -> p (l b)")[:, SEQ:TOK], kr[0:ROPE, KEY_NEW:NKEY]).then_inc(S["rows_out"], 16)
                pool.wait_ge(S["lat_ready"], l * 7 + 7)
                alone(pool)
                row("p_ckv", ckv[:, :, 0:SEQ])
                row("s_ckv", ckv[:, :, KEY_NEW:NKEY])
                pool.wait_ge(S["qr_ready"], l * 2 + 2)
                alone(pool)
                for h in range(4):
                    pool.dma_start(T5[:, h, :], toeplitz(h, P, 0, 512)).then_inc(S[t5_sem(h)], 16)
                for h in range(H):
                    j, g = h % 4, h // 4
                    pool.dma_start(T5s[32 * j:32 * j + 32, g, :], toeplitz(h, NEW, 128, W_S)).then_inc(S["t5s_in"], 16)
                pool.wait_ge(S["branch_out"], l * N_PAIR + 5 + 2)
                for b, o, n in ((1, qB, 0), (0, qAn, 2)):
                    alone(pool)
                    nc.gpsimd.tensor_copy(o_h[b][:], o).then_inc(S["split"], 1)
                    pool.wait_ge(S["split"], l * 4 + n + 1)
                    nc.gpsimd.tensor_tensor(o_l[b][:], o, o_h[b][:].bitcast(F32), ALU.subtract).then_inc(S["split"], 1)
                    for h in range(4 + n, 6 + n):
                        pool.wait_ge(S["bias_ready"], l * N_UNIT + 34 + 8 * ((h - 4) // 2 + 1))
                        alone(pool)
                        pool.dma_start(T5[:, h % 4, :], toeplitz(h, P, 0, 512)).then_inc(S[t5_sem(h)], 16)
                with pool.Fori(0, 5) as i:
                    for j in range(8):
                        low(l, PC_M, i * 8 + 30 + j, (CH_M + 20 + j // 2, j % 2), (j % 2) * 1024, (1024, 512)[j % 2])
                for j in range(40, 48):
                    low(l, PC_M, 30 + j, (CH_M + 20 + j // 2, j % 2), (j % 2) * 1024, (1024, 512)[j % 2])
                for n, (ch, at, m) in enumerate(OUT_PIECES):
                    low(l, PC_M, 78 + n, (CH_M + ch, n % 2), at, m)
                ffn(l, PC_B, CH_B)
            pool.wait_ge(S["rows_out"], 16 * 12 * DEPTH)
            pool.wait_ge(S["rows_ki"], 16 * 2 * DEPTH)

        @blk.tensor
        def _(pe):
            mm = nc.tensor.matmul
            pe.sem_inc(vacated[0], 2)
            pe.sem_inc(vacated[1], 2)
            pe.sem_inc(S["sq_used"], 2)
            pe.sem_inc(S["root"], 1)
            for n in ("idx_rel", "idx_acc", "probs_ready", "pt_done", "pt_copied", "pv_done", "heads_normed",
                      "ot_done", "branch_out"):
                pe.sem_inc(S[n], 3 if n in ("probs_ready", "pt_done") else 2)
            pe.sem_inc(S["sb_a_ready"], 4)
            pe.sem_inc(S["sb_pv"], 2)

            pe.wait_ge(S["table_in"], 32)
            for c in range(2):
                last = mm(PS[0:H, c, 0:320], relb[0:32, :], onehot[0:32, 320 * c:320 * c + 320], start=True, stop=True)
            last.then_inc(S["tab_ps"], 1)
            pe.wait_ge(S["tab_sb"], 1)
            pe.wait_ge(S["consts_in"], 16)

            def chunk(l, ch, i=0):
                pe.wait_ge(loaded[ch % NSLOT], (l * (CH_LAYER // NSLOT) + ch // NSLOT + i + 1) * 16)
                return ring[:, ch % NSLOT, :]

            def open_tile(l, u, turn):
                pe.wait_ge(vacated[u], l * T_LAYER + turn + 2)

            def product(u, steps, n=(0, HALF, TOK), first=True, last=True, m=P):
                ins = None
                for s, (w, x) in enumerate(steps):
                    for b in range(2):
                        ins = mm(PS[0:m, 2 * u + b, 0:n[b + 1] - n[b]], w, x[:, n[b]:n[b + 1]],
                                 start=first and s == 0, stop=last and s == len(steps) - 1)
                if last:
                    ins.then_inc(done[u], 1)

            def square_sum(l, norm, k):
                j, q0, K = NORMS[norm]
                if k == 0:
                    pe.wait_ge(S["root"], l * N_NORM + j + 1)
                pe.wait_ge(S["sq_ready"], l * N_SQ + q0 + k + 1)
                for b in range(2):
                    ins = mm(PS[:, 4 + b, 0:HALF], ones, sq[:, k % 2, HALF * b:HALF * b + HALF],
                             start=k == 0, stop=k == K - 1)
                ins.then_inc(S["sq_used"], 1)

            def sum_partitions(l, norm):
                j, q0, K = NORMS[norm]
                pe.wait_ge(S["root"], l * N_NORM + j + 1)
                pe.wait_ge(S["sq_used"], l * N_SQ + q0 + K + 1)
                for b in range(2):
                    mm(PS[:, 4 + b, 0:HALF], ones, rstd[:, HALF * b:HALF * b + HALF], start=True, stop=False)
                pe.wait_ge(S["sq_ready"], l * N_SQ + q0 + K)
                for b in range(2):
                    ins = mm(PS[:, 4 + b, 0:HALF], ones, sq[:, (K - 1) % 2, HALF * b:HALF * b + HALF], start=False, stop=True)
                ins.then_inc(S["sq_used"], 1)

            def split_product(l, u, piece, hs, w_l, x_h, x_l, first=True, last=True, step=None):
                K = len(x_h)
                pe.wait_ge(S["w_high"], piece + 1)
                for k in range(K):
                    if step:
                        step(k)
                    w = piece_h[:, hs, k * P:(k + 1) * P]
                    for n, x in enumerate((x_h, x_l)):
                        for b in range(2):
                            mm(PS[:, 2 * u + b, 0:HALF], w, x[k][:, HALF * b:HALF * b + HALF],
                               start=first and k == 0 and n == 0, stop=False)
                pe.wait_ge(S["w_low"], piece + 1)
                for k in range(K):
                    for b in range(2):
                        ins = mm(PS[:, 2 * u + b, 0:HALF], w_l[:, k * P:(k + 1) * P], x_h[k][:, HALF * b:HALF * b + HALF],
                                 start=False, stop=last and k == K - 1)
                ins.then_inc(done[u] if last else S["half_read"], 1)

            def ffn(l, t0, c0, p0, pre, post, h0):
                for k in range(KD):
                    square_sum(l, pre, k)
                u_h, u_lo = [uT_r[:, k, 0:TOK] for k in range(KD)], [u_l[:, k, :] for k in range(KD)]

                def up(f, ch, step=None):
                    for g in range(2):
                        open_tile(l, g, t0 + f)
                        split_product(l, g, l * PC_LAYER + p0 + f * 2 + g, g, ring_r[:, ch % NSLOT, g * 1024:g * 1024 + 1024],
                                      u_h, u_lo, step=step if g == 0 else None)

                def input_ready(k):
                    pe.wait_ge(S["hready"], l * 26 + h0 + k + 1)

                up(0, c0, input_ready)
                alone(pe)
                with pe.Fori(0, 5) as i:
                    for j in range(4):
                        up(i * 4 + j + 1, c0 + j + 1)
                up(KF - 1, c0 + KF - 1)
                pe.wait_ge(vacated[1], l * T_LAYER + t0 + 11 + 2)

                def down(u, turn, n, ch):
                    open_tile(l, u, turn)
                    for kh in range(2):
                        if kh and u == 0:
                            pe.wait_ge(vacated[1], l * T_LAYER + t0 + KF + 2)
                        split_product(l, u, l * PC_LAYER + p0 + 2 * KF + n * 2 + kh, kh, ring_r[:, (ch + kh) % NSLOT, :],
                                      [act_h[:, 11 * kh + k, :] for k in range(11)], [act_l[:, 11 * kh + k, :] for k in range(11)],
                                      first=kh == 0, last=kh == 1)

                alone(pe)
                with pe.Fori(0, 2) as i:
                    for j in range(4):
                        down(j % 2, t0 + KF + j // 2 + i * 2, i * 4 + j, c0 + KF + 2 * j)
                sum_partitions(l, post)

            def mixer(l):
                for k in range(KD):
                    square_sum(l, "mix", k)
                ch = CH_M
                u_h, u_lo = [uT_r[:, k, 0:TOK] for k in range(KD)], [u_lm[:, k, 0:TOK] for k in range(KD)]

                def tile(name, steps, **kw):
                    t = TILE[name]
                    open_tile(l, t % 2, T_M + t // 2)
                    product(t % 2, steps, **kw)

                def split_tile(name, x_h, x_l, chunk_of, at, step=None):
                    t, piece = TILE[name], PIECE_OF[name]
                    open_tile(l, t % 2, T_M + t // 2)
                    split_product(l, t % 2, l * PC_LAYER + PC_M + piece, piece % 2, ring_r[:, (ch + chunk_of) % NSLOT, at:at + 1024],
                                  x_h, x_l, step=step)

                def input_ready(k):
                    pe.wait_ge(S["hready"], l * 26 + 8 + k + 1)

                for i in range(7):
                    split_tile(TILES[i], u_h, u_lo, IN_PIECES[i][0], IN_PIECES[i][1], input_ready if i == 0 else None)
                banks = [2 * (TILE[f"v{s // 2}"] % 2) + s % 2 for s in range(4)] + [4]
                pe.wait_ge(S["hready"], l * 26 + 18)
                for n in range(2):
                    open_tile(l, TILE[f"v{n}"] % 2, turn_of(f"v{n}"))
                for i in range(4):
                    piece = 7 + i
                    slot, at, _ = IN_PIECES[piece]
                    w_h, w_l = piece_h[:, piece % 2, :], ring_r[:, (ch + slot) % NSLOT, at:at + 1024]
                    pe.wait_ge(S["w_low"], l * PC_LAYER + PC_M + piece + 1)
                    for s in range(5):
                        for kk in range(2):
                            k, cols, n = 2 * i + kk, slice(P * s, P * s + P), slice(512 * kk, 512 * kk + 512)
                            for m, (x, w) in enumerate(((uT_r, w_h), (u_lm, w_h), (uT_r, w_l))):
                                ins = mm(PS[:, banks[s], :], x[:, k, cols], w[:, n], start=k == 0 and m == 0, stop=k == KD - 1 and m == 2)
                        if i == 3 and s == 1:
                            ins.then_inc(done[TILE["v0"] % 2], 1)
                    ins.then_inc(S["v_step"] if i < 3 else done[TILE["v1"] % 2], 1)
                    if i == 0:
                        pe.wait_ge(vacated[TILE["vw"] % 2], l * T_LAYER + turn_of("vw") + 3)
                        alone(pe)
                        for s in range(5):
                            ins = nc.tensor.transpose(PS[:, 5 + s // 4, P * (s % 4):P * (s % 4) + P], vw_f[:, P * s:P * s + P], ident)
                        ins.then_inc(S["vw_turned"], 1)
                pe.wait_ge(S["cache_in"], (l * N_CACHE + N_CACHE) * 16)
                for name in ("v0", "v1"):
                    pe.wait_ge(vacated[TILE[name] % 2], l * T_LAYER + turn_of(name) + 3)
                i = 0
                for s in range(1, 5):
                    k0, w = keys(s)
                    for h in range(H):
                        r = 64 * (h % 2)
                        pe.wait_ge(S["idx_rel"], l * 32 + i + 1)
                        mm(PS[:, 6 + i % 2, 0:w], qI[r:r + 64, h // 2, P * s:P * s + P], kI[r:r + 64, k0:k0 + w],
                           start=True, stop=True).then_inc(S["idx_done"], 1)
                        i += 1
                for i in range(11, 30):
                    name = TILES[9 + i - 11]
                    split_tile(name, u_h, u_lo, IN_PIECES[i][0], IN_PIECES[i][1])
                    if name in ("ql1", "ql2", "kv0"):
                        square_sum(l, "q", ("ql1", "ql2", "kv0").index(name))
                for k in range(KKV):
                    square_sum(l, "kv", k)
                for name in ("kv0", "kv1"):
                    pe.wait_ge(vacated[TILE[name] % 2], l * T_LAYER + turn_of(name) + 3)
                branch_b(l)
                pe.wait_ge(S["lat_ready"], l * 7 + 3)
                for i in range(8):
                    w = chunk(l, ch + 16 + i // 4)
                    at = (i % 4) * KQ * P
                    tile(TILES[28 + i], [(w[:, at + k * P:at + k * P + P], ql[:, k, :]) for k in range(KQ)])
                pe.wait_ge(S["lat_ready"], l * 7 + 7)
                w = chunk(l, ch + 18)
                for i in range(4):
                    tile(f"kA{i}", [(w[:, (i * KKV + k) * P:(i * KKV + k + 1) * P], ckv[:, k, :]) for k in range(KKV)],
                         n=(0, NKEY // 2, NKEY))
                w = chunk(l, ch + 19)
                for i, kts in enumerate(VA_KEYS):
                    t = TILE[f"vA{i}"]
                    u = t % 2
                    open_tile(l, u, T_M + t // 2)
                    for b, kt in enumerate(kts):
                        m = P if kt < 6 else NEW
                        for k in range(KKV):
                            ins = mm(PS[0:m, 2 * u + b, :], ckv[:, k, P * kt:P * kt + m], w[:, k * 512:k * 512 + 512],
                                     start=k == 0, stop=k == KKV - 1)
                    ins.then_inc(done[u], 1)
                for name in ("vA2", "vA3"):
                    pe.wait_ge(vacated[TILE[name] % 2], l * T_LAYER + turn_of(name) + 3)
                pe.wait_ge(S["qr_ready"], l * 2 + 2)
                attend(l, 0)
                attend(l, 1)
                pe.wait_ge(S["branch_out"], l * N_PAIR + N_PAIR + 2)
                pe.wait_ge(S["split"], l * 4 + 4)
                alone(pe)
                with pe.Fori(0, 2) as i:
                    for j in range(4):
                        for b in range(3):
                            c = 3 * j + b
                            turn = turn_of("g0_0") + 3 * j + b + i * 12
                            piece = l * PC_LAYER + PC_M + 30 + 2 * c + i * 24
                            w_l = ring_r[:, (ch + 20 + c) % NSLOT, :]
                            open_tile(l, 0, turn)
                            split_product(l, 0, piece, 0, w_l, u_h, u_lo)
                            open_tile(l, 1, turn)
                            if b == 2:
                                pe.wait_ge(S["split_c"], l * 2 + 2)
                            split_product(l, 1, piece + 1, 1, w_l[:, 1024:1536], [o_h[b][:, k, :] for k in range(4)],
                                          [o_l[b][:, k, :] for k in range(4)])
                pe.wait_ge(S["merge_ready"], l * KD + KD)
                for n in range(KD):
                    split_tile(f"wo{n}", [merged_h[:, k, :] for k in range(KD)], [merged_l[:, k, :] for k in range(KD)], *OUT_PIECES[n][:2])
                sum_partitions(l, "mix_post")

            def branch_b(l):
                def scores(t):
                    h, j = t // 4, 3 - t % 4
                    r, w = 64 * (h % 2), SEQ - P * j
                    pe.wait_ge(S["sb_a_ready"], l * (N_B + 3) + t + 1)
                    mm(PS[:, t % 4, 0:w], kB[r:r + 64, h // 2, P * j:P * j + P], qB[r:r + 64, h // 2, P * j:SEQ],
                       start=True, stop=False, skip_group_check=True)
                    if t == 0:
                        pe.wait_ge(S["masks_ready"], l * 3 + 3)
                    mm(PS[:, t % 4, 0:P], ident_r[:], sb_mask_r[:], start=False, stop=True,
                       skip_group_check=True).then_inc(S["sb_done"], 1)

                def cumulate(t):
                    h, j = t // 4, 3 - t % 4
                    w = SEQ - P * j
                    pe.wait_ge(S["sb_sp_ready"], l * (N_B + 3) + t + 1)
                    for i in range(3, j, -1):
                        at = 128 * ((3 - i) * (4 - i) // 2)
                        wi = SEQ - P * i
                        mm(PS[:, t % 4, (i - j) * P:w], neg_ones, sb_sp[:, h % 2, at:at + wi], start=False, stop=False,
                           skip_group_check=True)
                    at = 128 * ((3 - j) * (4 - j) // 2)
                    mm(PS[:, t % 4, 0:w], neg_tri, sb_sp[:, h % 2, at:at + w], start=False, stop=True,
                       skip_group_check=True).then_inc(S["sb_cum"], 1)

                def values(h):
                    r = 64 * (h % 2)
                    pe.wait_ge(S["sb_a_ready"], l * (N_B + 3) + 4 * h + 8)
                    alone(pe)
                    if h == 0:
                        pe.wait_ge(S["root"], l * N_NORM + NORMS["kv"][0] + 2)
                    if h % 2 == 0 and h >= 4:
                        pe.wait_ge(S["sb_out"], l * 5 + h // 2 - 1)
                    for j in range(4):
                        at = 128 * ((3 - j) * (4 - j) // 2)
                        ins = mm(PS[r:r + 64, 4 + (h // 2) % 2, P * j:SEQ], VB[:, j, DH * h:DH * h + DH],
                                 sb_a[:, h % 2, at:at + SEQ - P * j], start=j == 0, stop=j == 3, skip_group_check=True)
                    ins.then_inc(S["sb_pv"], 1)

                for t in range(N_B):
                    scores(t)
                    if t >= 2:
                        cumulate(t - 2)
                    if t >= 6 and (t - 6) % 4 == 0:
                        values((t - 6) // 4)
                cumulate(N_B - 2)
                cumulate(N_B - 1)
                values(H - 1)
                pe.wait_ge(S["sb_a_ready"], l * (N_B + 3) + N_B + 4)
                pe.wait_ge(S["sb_out"], l * 5 + 4)
                alone(pe)
                tiles = [(2, KEY_NEW, NEW), (1, SEQ + P, P), (0, SEQ, P)]
                for kt, k0, m in tiles:
                    for h in range(H):
                        r = 64 * (h % 2)
                        ins = mm(PS[0:m, 2 * kt + h % 2, 32 * (h // 2):32 * (h // 2) + 32], kB[r:r + 64, h // 2, k0:k0 + m],
                                 qB[r:r + 64, h // 2, SEQ:TOK], start=h < 2, stop=kt != 2, skip_group_check=True)
                    if kt == 2:
                        for b in range(2):
                            for j in range(4):
                                ins = mm(PS[0:m, 4 + b, 32 * j:32 * j + 32], ident[0:NEW, 0:NEW], sb_mask[0:NEW, 0:NEW],
                                         start=False, stop=True, skip_group_check=True)
                    ins.then_inc(S["sb_done"], 1)
                for n, (kt, k0, m) in enumerate(tiles):
                    pe.wait_ge(S["sb_sp_ready"], l * (N_B + 3) + N_B + n + 1)
                    alone(pe)
                    for b in range(2):
                        for n2 in range(n):
                            m2 = tiles[n2][2]
                            mm(PS[0:m, 2 * kt + b, 0:P], neg_ones[0:m2, 0:m], sb_sp[0:m2, 0, 256 * n2 + P * b:256 * n2 + P * b + P],
                               start=False, stop=False, skip_group_check=True)
                        ins = mm(PS[0:m, 2 * kt + b, 0:P], neg_tri[0:m, 0:m], sb_sp[0:m, 0, 256 * n + P * b:256 * n + P * b + P],
                                 start=False, stop=True, skip_group_check=True)
                    ins.then_inc(S["sb_cum"], 1)
                pe.wait_ge(S["sb_a_ready"], l * (N_B + 3) + N_B + 3 + 4)
                alone(pe)
                for h in range(H):
                    r = 64 * (h % 2)
                    for n in (2, 1, 0):
                        kt, k0, m = tiles[n]
                        ins = mm(PS[r:r + 64, 6, 32 * (h // 2):32 * (h // 2) + 32], VB[0:m, 4 + kt, DH * h:DH * h + DH],
                                 sb_a[0:m, 0, 256 * n + P * (h % 2) + 32 * (h // 2):256 * n + P * (h % 2) + 32 * (h // 2) + 32],
                                 start=n == 2, stop=n == 0, skip_group_check=True)
                ins.then_inc(S["sb_pv"], 1)
                pe.wait_ge(S["sb_out"], l * 5 + 5)

            def attend(l, c):
                V = (VA, VC)[c]
                n0, q0 = l * N_UNIT + c * 34, l * N_PAIR + 5 * c

                def scores(i):
                    p, s, e = UNITS[i]
                    k0, w = keys(s)
                    pe.wait_ge(S["probs_ready"], n0 + i + 1)
                    if s == 4:
                        alone(pe)
                    bank = score_bank(c, i)
                    if s < 4:
                        h = 2 * p + e
                        r, r4 = 64 * e, 32 * (h % 4)
                        out = PS[:, bank, 0:w]
                        if c == 0:
                            mm(out, qAr[r4:r4 + 32, h // 4, P * s:P * s + P], kr[r4:r4 + 32, 0:w], start=True, stop=False,
                               skip_group_check=True)
                            mm(out, qAn[r:r + 64, p, P * s:P * s + P], kA[r:r + 64, p, 0:w], start=False, stop=False,
                               skip_group_check=True)
                            mm(PS[:, bank, w - P:w], ident_r[:], chunk_mask_r[:], start=False, stop=True,
                               skip_group_check=True).then_inc(S["s_done"], 1)
                        else:
                            mm(out, qC[r:r + 64, p, P * s:P * s + P], kC[r:r + 64, 0:w], start=True,
                               stop=True).then_inc(S["s_done"], 1)
                        return
                    for j in range(4):
                        h = 4 * e + j
                        r = 64 * (h % 2)
                        out = PS[32 * j:32 * j + 32, bank, 0:w]
                        if c == 0:
                            mm(out, qAn[r:r + 64, h // 2, SEQ:TOK], kA[r:r + 64, h // 2, k0:k0 + w], start=True, stop=False,
                               skip_group_check=True)
                        else:
                            ins = mm(out, qC[r:r + 64, h // 2, SEQ:TOK], kC[r:r + 64, k0:k0 + w], start=True, stop=True)
                    if c == 0:
                        for j in range(4):
                            out = PS[32 * j:32 * j + 32, bank, 0:w]
                            ins = mm(out, qAr[32 * j:32 * j + 32, e, SEQ:TOK], kr[32 * j:32 * j + 32, k0:k0 + w], start=False,
                                     stop=True, skip_group_check=True)
                    ins.then_inc(S["s_done"], 1)

                def transposes(i):
                    pe.wait_ge(S["probs_ready"], n0 + i + 4)
                    pe.wait_ge(S["pt_copied"], n0 + i + 1)
                    alone(pe)
                    for _, m, at, _ in key_tiles(UNITS[i][1]):
                        ins = nc.tensor.transpose(PS[0:m, 2 + i % 2, at:at + P], probs(c, i)[:, at:at + m], ident)
                    ins.then_inc(S["pt_done"], 1)

                def values(i):
                    p, s, e = UNITS[i]
                    pe.wait_ge(S["pt_copied"], n0 + i + 3)
                    if (s, e) in ((0, 0), (4, 0)):
                        pe.wait_ge(S["heads_normed"], q0 + p + 1)
                    if s == 4:
                        alone(pe)
                    bank = 4 + (5 * c + p) % 2
                    tiles = key_tiles(s)
                    for j in range(1 if s < 4 else 4):
                        h = 2 * p + e if s < 4 else 4 * e + j
                        out = PS[:, bank, P * s + DH * e:P * s + DH * e + DH] if s < 4 else PS[32 * j:32 * j + 32, bank, DH * e:DH * e + DH]
                        hv = DH * h if c == 0 else 0
                        for n, (_, m, at, vt) in enumerate(tiles):
                            pt = probT[0:m, i % 2, at:at + P] if s < 4 else probT[0:m, i % 2, at + 32 * j:at + 32 * j + 32]
                            ins = mm(out, pt, V[0:m, vt, hv:hv + DH], start=n == 0, stop=n == len(tiles) - 1)
                    ins.then_inc(S["pv_done"], 1)

                def turn_pair(p):
                    q = 5 * c + p
                    pe.wait_ge(S["heads_normed"], q0 + p + 3)
                    pe.wait_ge(S["branch_out"], q0 + p + 2)
                    alone(pe)
                    if p < 4:
                        for s in range(NBLK):
                            ins = nc.tensor.transpose(PS[:, 7, P * s:P * s + P], OT[:, q % 2, P * s:P * s + P], ident)
                    else:
                        for e in range(2):
                            ins = nc.tensor.transpose(PS[0:DH, 7, P * e:P * e + P], OT[:, q % 2, DH * e:DH * e + DH], ident)
                    ins.then_inc(S["ot_done"], 1)

                n = len(UNITS)
                ends = {7: 0, 15: 1, 23: 2, 31: 3, 33: 4}
                if c == 0:
                    pe.wait_ge(S["sb_out"], l * 5 + 5)
                for i in range(n + 4):
                    if i < n:
                        scores(i)
                    if 2 <= i <= n + 1:
                        transposes(i - 2)
                    if 3 <= i <= n + 2:
                        values(i - 3)
                    if i - 4 in ends:
                        turn_pair(ends[i - 4])

            with pe.Fori(0, DEPTH) as l:
                ffn(l, T_A, CH_A, PC_A, "pre_a", "post_a", 0)
                mixer(l)
                ffn(l, T_B, CH_B, PC_B, "pre_b", "post_b", 18)

        N_ACT = 70

        @blk.scalar
        def _(act):
            A = nc.scalar.activation
            act.dma_start(onehot[0:32, :], d["onehot"]).then_inc(S["table_in"], 16)
            act.dma_start(relb[0:32, :], d["rel_bias"]).then_inc(S["table_in"], 16)
            act.wait_ge(S["tab_ps"], 1)
            A(topw_tab[0:H, :].rearrange("p (a b) -> p a b", a=2), PS[0:H, 0:2, 0:320], ACT.Copy).then_inc(S["tab_sb"], 1)
            act.wait_ge(S["init_ready"], 1)

            def square(l, norm, k, src):
                act.wait_ge(S["sq_used"], l * N_SQ + NORMS[norm][1] + k + 1)
                A(sq[:, k % 2, :] if len(src.shape) == 2 else sq[:, k % 2, :].rearrange("p (a b) -> p a b", a=2),
                  src, ACT.Square).then_inc(S["sq_ready"], 1)

            def root(l, norm):
                j, q0, K = NORMS[norm]
                act.wait_ge(S["sq_used"], l * N_SQ + q0 + K + 2)
                A(rstd[:].rearrange("p (a b) -> p a b", a=2), unit(2)[:, :, 0:HALF], ACT.Sqrt, scale=1.0 / (K * P),
                  bias=eps_c[:]).then_inc(S["root"], 1)

            def pre_norm(l, norm, v):
                for k in range(KD):
                    act.wait_ge(S["xnew"], l * 24 + v * 8 + k + 1)
                    square(l, norm, k, xT[:, k, :])
                root(l, norm)

            def filled(l, u, turn):
                act.wait_ge(done[u], l * T_LAYER + turn + 1)

            def high_input(l, u):
                for k in range(KD):
                    act.wait_ge(S["u_norm"], l * KD + k + 1)
                    A(uT_r[:, k, 0:TOK], u[:, k, 0:TOK], ACT.Copy).then_inc(S["u_high"], 1)

            def high(ch, i, hs, at, n, l):
                act.wait_ge(loaded[ch % NSLOT], (l * (CH_LAYER // NSLOT) + ch // NSLOT + i + 1) * 16)
                A(piece_h[:, hs, 0:n], ring[:, ch % NSLOT, at:at + n], ACT.Copy).then_inc(S["w_high"], 1)

            def ffn(l, t0, c0, pre, post, v):
                high(c0, 0, 0, 0, 1024, l)
                high(c0, 0, 1, 1024, 1024, l)
                q = l * 2 + v // 2
                c = NORMS[pre][1]
                if v == 0:
                    act.wait_ge(S["gain_now"], l + 1)
                for k in range(KD):
                    act.wait_ge(S["xnew"], l * 24 + v * 8 + k + 1)
                    square(l, pre, k, xT[:, k, :])
                    A(uT_r[:, k, 0:TOK], xT[:, k, :], ACT.Copy, scale=g_now[:, c + k:c + k + 1]).then_inc(S["u_high"], 1)
                root(l, pre)

                def silu(f, j):
                    act.wait_ge(vacated[0], l * T_LAYER + t0 + f + 3)
                    A(gate_s[:, j % 2, :], gate_s[:, j % 2, :], ACT.Silu).then_inc(S["silu_done"], 1)

                with act.Fori(0, 5) as i:
                    for j in range(4):
                        filled(l, 0, t0 + i * 4 + j)
                        high(c0 + j + 1, i, 0, 0, 1024, l)
                        silu(i * 4 + j, j)
                        filled(l, 1, t0 + i * 4 + j)
                        high(c0 + j + 1, i, 1, 1024, 1024, l)
                for f in (KF - 2, KF - 1):
                    filled(l, 0, t0 + f)
                    if f == KF - 2:
                        high(c0 + KF - 1, 0, 0, 0, 1024, l)
                    else:
                        high(c0 + KF, 0, 0, 0, PIECE, l)
                    silu(f, f)
                    filled(l, 1, t0 + f)
                    if f == KF - 2:
                        high(c0 + KF - 1, 0, 1, 1024, 1024, l)
                    else:
                        high(c0 + KF + 1, 0, 1, 0, PIECE, l)
                act.preload_act_table_set("sqrt_and_others")
                for n in range(KD):
                    u = n % 2
                    if n < KD - 1:
                        act.wait_ge(S["half_read"], q * KD + n + 1)
                        high(c0 + KF + 2 * n + 2, 0, 0, 0, PIECE, l)
                    filled(l, u, t0 + KF + n // 2)
                    if n < KD - 1:
                        high(c0 + KF + 2 * n + 3, 0, 1, 0, PIECE, l)
                    square(l, post, n, unit(u)[:, :, 0:HALF])
                    A(y_f[:, n, :].rearrange("p (a b) -> p a b", a=2), unit(u)[:, :, 0:HALF], ACT.Copy).then_inc(vacated[u], 1)
                root(l, post)

            def mixer(l):
                def high_in(i):
                    if i < 30:
                        ch, at, n = IN_PIECES[i]
                        high(CH_M + ch, 0, i % 2, at, n, l)
                    elif 78 <= i < 78 + KD:
                        ch, at, n = OUT_PIECES[i - 78]
                        high(CH_M + ch, 0, i % 2, at, n, l)

                high_in(0)
                high_in(1)
                pre_norm(l, "mix", 1)
                high_input(l, u_norm_m)

                def unit_of(name):
                    return TILE[name] % 2

                def evac(name):
                    t = TILE[name]
                    u = t % 2
                    filled(l, u, T_M + t // 2)
                    if name in PIECE_OF:
                        high_in(PIECE_OF[name] + 2)
                    return u

                def to_keys(name, dst, at_hand=False):
                    u = unit_of(name) if at_hand else evac(name)
                    A(dst[:, 0:HALF], PS[:, 2 * u, 0:HALF], ACT.Copy)
                    A(dst[:, HALF:SEQ], PS[:, 2 * u + 1, 0:SEQ - HALF], ACT.Copy)
                    A(dst[:, KEY_NEW:NKEY], PS[:, 2 * u + 1, SEQ - HALF:HALF], ACT.Copy).then_inc(vacated[u], 1)

                def to_queries(name, dst, scale=1.0, at_hand=False):
                    u = unit_of(name) if at_hand else evac(name)
                    A(dst.rearrange("p (a b) -> p a b", a=2), unit(u)[:, :, 0:HALF], ACT.Copy, scale=scale).then_inc(vacated[u], 1)

                to_keys("kI", kI)

                def to_blocks(name, dst):
                    u = evac(name)
                    A(dst[:, 0:HALF], PS[:, 2 * u, 0:HALF], ACT.Copy)
                    A(dst[:, HALF:SEQ], PS[:, 2 * u + 1, 0:SEQ - HALF], ACT.Copy)
                    A(dst[:, SEQ:SEQ + P].rearrange("p (a b) -> p a b", a=4),
                      PS[:, 2 * u + 1, SEQ - HALF:HALF].unsqueeze(1).broadcast_to([P, 4, NEW]), ACT.Copy).then_inc(vacated[u], 1)

                for i in range(4):
                    to_blocks(f"qI{i}", qI[:, i, :])
                to_keys("kC", kC)
                to_blocks("vw", vw_f)
                act.wait_ge(S["v_step"], l * 3 + 1)
                high_in(9)
                act.wait_ge(S["vw_turned"], l + 1)
                vw = PS[:, 5, :].rearrange("p (s n) -> p s n", s=4)
                A(VC[:, 0:4, :], vw[:, :, 0:DH], ACT.Copy)
                A(wI[:, 0:4, :], vw[:, :, DH:DH + H], ACT.Copy)
                A(VC[:, 6, :], PS[:, 6, 0:DH], ACT.Copy)
                A(wI[:, 4, :], PS[:, 6, DH:DH + H], ACT.Copy)
                for i in range(1, 3):
                    act.wait_ge(S["v_step"], l * 3 + i + 1)
                    high_in(9 + i)
                for n in range(2):
                    u = evac(f"v{n}")
                    if n:
                        high_in(12)
                        A(VB[:, 6, :], PS[:, 4, :], ACT.Copy)
                    A(VB[:, 2 * n:2 * n + 2, :], unit(u), ACT.Copy).then_inc(vacated[u], 1)
                i = 0
                for s in range(1, 5):
                    _, w = keys(s)
                    for h in range(H):
                        act.wait_ge(S["idx_done"], l * 32 + i + 1)
                        act.wait_ge(S["idx_acc"], l * 32 + i + 1)
                        A(rel[:, i % 2, 0:w], PS[:, 6 + i % 2, 0:w], ACT.Relu, scale=SCALE_I).then_inc(S["idx_rel"], 1)
                        i += 1
                for i in range(4):
                    to_queries(f"qC{i}", qC[:, i, :])
                for i in range(4):
                    to_queries(f"qB{i}", qB[:, i, :], scale=DH ** -0.5)
                for i in range(4):
                    to_keys(f"kB{i}", kB[:, i, :])
                act.wait_ge(S["idx_acc"], l * 32 + 34)
                to_queries("kr", kr_raw[:, 0, :])
                to_queries("krs", kr_raw[:, 1, :])
                for i in range(KQ):
                    u = evac(f"ql{i}")
                    square(l, "q", i, unit(u)[:, :, 0:HALF])
                    to_queries(f"ql{i}", ql[:, i, :], at_hand=True)
                root(l, "q")
                for i in range(KKV):
                    u = evac(f"kv{i}")
                    square(l, "kv", i, unit(u)[:, :, 0:HALF])
                    to_keys(f"kv{i}", ckv[:, i, :], at_hand=True)
                act.wait_ge(S["lat_ready"], l * 7 + 3)
                root(l, "kv")
                act.wait_ge(S["sel_ready"], l * 4 + 4)
                act.wait_ge(S["idx_done"], l * 32 + 32)
                act.wait_ge(S["rows_ki"], 16 * (l * 2 + 2))
                branch_b(l)
                act.wait_ge(S["rows_out"], 16 * (l * 12 + 12))
                for i in range(4):
                    to_queries(f"uq{i}", qAn[:, i, :])
                for i in range(4):
                    u = evac(f"kA{i}")
                    A(kA[:, i, :].rearrange("p (a b) -> p a b", a=2), unit(u)[:, :, 0:NKEY // 2], ACT.Copy).then_inc(vacated[u], 1)
                for i, kts in enumerate(VA_KEYS):
                    u = evac(f"vA{i}")
                    if len(kts) == 2:
                        A(VA[:, kts[0]:kts[0] + 2, :], unit(u), ACT.Copy).then_inc(vacated[u], 1)
                    else:
                        m = P if kts[0] < 6 else NEW
                        A(VA[0:m, kts[0], :], PS[0:m, 2 * u, :], ACT.Copy).then_inc(vacated[u], 1)
                high(CH_M + 20, 0, 0, 0, 1024, l)
                high(CH_M + 20, 0, 1, 1024, 512, l)
                attend(l, 0)
                attend(l, 1)
                def gate(turn, j, next_high):
                    filled(l, 0, turn)
                    next_high(0)
                    act.wait_ge(vacated[1], l * T_LAYER + turn + 1)
                    A(sig[:, j % 2, :].rearrange("p (a b) -> p a b", a=2), unit(0)[:, :, 0:HALF],
                      ACT.Sigmoid).then_inc(vacated[0], 1)
                    filled(l, 1, turn)
                    next_high(1)

                with act.Fori(0, 5) as i:
                    for j in range(4):
                        gate(turn_of("g0_0") + j + i * 4, j,
                             lambda g: high(CH_M + 21 + j, i, g, g * 1024, (1024, 512)[g], l))
                for c in range(20, 24):
                    gate(turn_of("g0_0") + c, c,
                         lambda g: high(CH_M + 21 + c, 0, g, g * 1024, (1024, 512)[g] if c < 23 else 1024, l))
                act.preload_act_table_set("sqrt_and_others")
                for n in range(KD):
                    u = evac(f"wo{n}")
                    square(l, "mix_post", n, unit(u)[:, :, 0:HALF])
                    to_queries(f"wo{n}", y_m[:, n, :], at_hand=True)
                root(l, "mix_post")

            def branch_b(l):
                nb = l * (N_B + 3)
                st = l * 70
                alone(act)
                act.preload_act_table_set("natural_log_exp_and_others")

                def soft(n, rows, src, e):
                    act.wait_ge(S["sb_done"], nb + n + 1)
                    if n >= 2:
                        act.wait_ge(S["sb_sp_ready"], nb + n - 1)
                    A(e, src, ACT.Abs).then_inc(S["act_step"], 1)
                    act.wait_ge(S["act_step"], st + 2 * n + 1)
                    A(e, e, ACT.Exp, scale=-1.0).then_inc(S["act_step"], 1)
                    act.wait_ge(S["act_step"], st + 2 * n + 2)
                    A(e, e, ACT.Ln, bias=1.0).then_inc(S["sb_soft"], 1)

                def weights(t):
                    h, j = t // 4, 3 - t % 4
                    w, at = SEQ - P * j, 128 * ((3 - j) * (4 - j) // 2)
                    act.wait_ge(S["sb_cum"], nb + t + 1)
                    if t % 4 == 0:
                        act.wait_ge(S["sb_pv"], l * 9 + h + 1)
                    A(sb_a[:, h % 2, at:at + w], PS[:, t % 4, 0:w], ACT.Exp).then_inc(S["sb_a_ready"], 1)

                def out_pair(p):
                    act.wait_ge(S["sb_pv"], l * 9 + 2 * p + 4)
                    A(qB[:, p, 0:SEQ], PS[:, 4 + p % 2, :], ACT.Copy).then_inc(S["sb_out"], 1)

                for t in range(N_B + 2):
                    if t < N_B:
                        w = P * (t % 4 + 1)
                        soft(t, P, PS[:, t % 4, 0:w], sb_e[:, t % 2, 0:w])
                    if t >= 2:
                        weights(t - 2)
                    if t % 8 == 7 and t >= 15:
                        out_pair(t // 8 - 1)
                out_pair(3)
                rows = [NEW, P, P]
                for n in range(3):
                    m = rows[n]
                    kt = 2 - n
                    soft(N_B + n, m, PS[0:m, 2 * kt:2 * kt + 2, 0:P],
                         sb_e[0:m, (N_B + n) % 2, 0:2 * P].rearrange("p (a b) -> p a b", a=2))
                for n in range(3):
                    m = rows[n]
                    kt = 2 - n
                    act.wait_ge(S["sb_cum"], nb + N_B + n + 1)
                    A(sb_a[0:m, 0, 256 * n:256 * n + 256].rearrange("p (a b) -> p a b", a=2), PS[0:m, 2 * kt:2 * kt + 2, 0:P],
                      ACT.Exp).then_inc(S["sb_a_ready"], 1)
                act.wait_ge(S["sb_pv"], l * 9 + 8 + 3)
                A(qB[:, :, SEQ:TOK], PS[:, 6, 0:P].rearrange("p (a b) -> p a b", a=4), ACT.Copy).then_inc(S["sb_out"], 1)

            def attend(l, c):
                n0, q0 = l * N_UNIT + c * 34, l * N_PAIR + 5 * c
                dst = (qAn, qC)[c]

                def softmax(i):
                    p, s, e = UNITS[i]
                    w = keys(s)[1]
                    q = 5 * c + p
                    act.wait_ge(S["bias_ready"], n0 + i + 1)
                    if (s, e) in ((0, 0), (4, 0)):
                        act.wait_ge(S["heads_normed"], q0 + p + 1)
                    if c == 0:
                        act.wait_ge(S["pt_done"], n0 + i + 1)
                        src = PS[:, score_bank(c, i), 0:w]
                    else:
                        src = probs(c, i)[:, 0:w]
                    col = 2 * s + e if s < 4 else e
                    A(probs(c, i)[:, 0:w], src, ACT.Exp, scale=SCALE_A if c == 0 else 1.0, bias=nbias[:, i % 2:i % 2 + 1],
                      accum_out=sums[:, q % 2, col:col + 1]).then_inc(S["probs_ready"], 1)

                def copy_t(i):
                    copy_probs(act, lambda o, x: A(o, x, ACT.Copy), n0, i)

                def out_pair(p):
                    q = 5 * c + p
                    act.wait_ge(S["ot_done"], q0 + p + 3)
                    if p < 4:
                        A(dst[:, p, 0:SEQ], PS[:, 7, :], ACT.Copy).then_inc(S["branch_out"], 1)
                        return
                    for e in range(2):
                        ins = A(dst[DH * e:DH * e + DH, :, SEQ:TOK],
                                PS[0:DH, 7, 0:2 * P].rearrange("p (a e b) -> p e a b", a=4, e=2)[:, e], ACT.Copy)
                    ins.then_inc(S["branch_out"], 1)

                n = len(UNITS)
                ends = {7: 0, 15: 1, 23: 2, 31: 3, 33: 4}
                for i in range(n + 4):
                    if i < n:
                        softmax(i)
                    if c == 1 and 2 <= i <= n + 1:
                        copy_t(i - 2)
                    if i - 4 in ends:
                        out_pair(ends[i - 4])

            act.wait_ge(S["x_in"], 16)
            with act.Fori(0, DEPTH) as l:
                ffn(l, T_A, CH_A, "pre_a", "post_a", 0)
                mixer(l)
                ffn(l, T_B, CH_B, "pre_b", "post_b", 2)

        N_DVE = [None]

        @blk.vector
        def _(dve):
            V = nc.vector
            V.memset(eps_c[:], EPS).then_inc(S["init_ready"], 1)
            dve.wait_ge(S["x_in"], 16)
            dve.sem_inc(S["xnew"], 8)
            dve.wait_ge(S["gain_in"], 16)
            dve.wait_ge(S["consts_in"], 16)

            per = DVE_STEPS
            count = [0]

            def link(l, ins):
                count[0] += 1
                ins.then_inc(S["dve_step"], 1)
                dve.wait_ge(S["dve_step"], l * per + count[0])
                alone(dve)

            def invert(l, norm):
                j = NORMS[norm][0]
                dve.wait_ge(S["root"], l * N_NORM + j + 2)
                V.reciprocal(rstd[:], rstd[:]).then_inc(S["inv"], 1)
                dve.wait_ge(S["inv"], l * N_NORM + j + 1)

            def pre_norm(l, norm, v, u_f, u_lo):
                invert(l, norm)
                c0 = NORMS[norm][1]

                def rest(k):
                    dve.wait_ge(S["u_high"], (l * 3 + v) * KD + k + 1)
                    V.tensor_tensor(u_lo[:, k, 0:TOK], u_f[:, k, 0:TOK], uT_r[:, k, 0:TOK].bitcast(F32), ALU.subtract).then_inc(S["hready"], 1)

                for k in range(KD):
                    V.scalar_tensor_tensor(out=u_f[:, k, 0:TOK], in0=xT[:, k, :], scalar=g_now[:, c0 + k:c0 + k + 1], in1=rstd[:],
                                           op0=ALU.mult, op1=ALU.mult).then_inc(S["u_norm"], 1)
                    if k:
                        rest(k - 1)
                rest(KD - 1)

            def post_norm(l, norm, y, half, n_y):
                c0 = NORMS[norm][1]
                for k in range(KD - 1):
                    dve.wait_ge(S["sq_ready"], l * N_SQ + c0 + k + 1)
                    if k:
                        dve.wait_ge(S["sq_used"], l * N_SQ + c0 + k + 2)
                    ins = V.tensor_tensor(rstd[:], rstd[:], sq[:, k % 2, :], ALU.add) if k else V.tensor_copy(rstd[:], sq[:, 0, :])
                    ins.then_inc(S["sq_used"], 1)
                invert(l, norm)

                def add(k):
                    dve.wait_ge(S["yscaled"], l * 24 + n_y * 8 + k + 1)
                    V.scalar_tensor_tensor(out=xT[:, k, :], in0=y[:, k, :], scalar=0.5 if half else 1.0, in1=xT[:, k, :],
                                           op0=ALU.mult, op1=ALU.add).then_inc(S["xnew"], 1)

                for k in range(KD):
                    V.scalar_tensor_tensor(out=y[:, k, :], in0=y[:, k, :], scalar=g_now[:, c0 + k:c0 + k + 1], in1=rstd[:],
                                           op0=ALU.mult, op1=ALU.mult).then_inc(S["yscaled"], 1)
                    if k:
                        add(k - 1)
                add(KD - 1)

            def filled(l, u, turn):
                dve.wait_ge(done[u], l * T_LAYER + turn + 1)

            def ffn(l, t0, pre, post, n_y):
                q, c0 = l * 2 + n_y // 2, NORMS[pre][1]
                for k in range(KD):
                    dve.wait_ge(S["u_high"], (l * 3 + n_y) * KD + k + 1)
                    V.scalar_tensor_tensor(out=u_l[:, k, :], in0=xT[:, k, :], scalar=g_now[:, c0 + k:c0 + k + 1],
                                           in1=uT_r[:, k, 0:TOK].bitcast(F32), op0=ALU.mult, op1=ALU.subtract).then_inc(S["hready"], 1)
                invert(l, pre)
                halves = lambda v: v.rearrange("p (a b) -> p a b", a=2)

                def gated(f, j):
                    g, up = gate_s[:, j, :], unit(1)[:, :, 0:HALF]
                    filled(l, 0, t0 + f)
                    dve.wait_ge(vacated[1], l * T_LAYER + t0 + f + 1)
                    V.tensor_tensor(halves(g), unit(0)[:, :, 0:HALF], halves(rstd[:]), ALU.mult).then_inc(vacated[0], 1)
                    dve.wait_ge(S["silu_done"], q * KF + f + 1)
                    V.tensor_tensor(g, g, rstd[:], ALU.mult).then_inc(S["gate_step"], 1)
                    hi = act_h[:, bass.ds(f, 1)].rearrange("p o n -> p (o n)")
                    lo = act_l[:, bass.ds(f, 1)].rearrange("p o n -> p (o n)")
                    filled(l, 1, t0 + f)
                    dve.wait_ge(S["gate_step"], q * 3 * KF + f * 3 + 1)
                    V.tensor_tensor(halves(hi), halves(g), up, ALU.mult).then_inc(S["gate_step"], 1)
                    V.tensor_tensor(halves(g), halves(g), up, ALU.mult).then_inc(S["gate_step"], 1)
                    dve.wait_ge(S["gate_step"], q * 3 * KF + f * 3 + 3)
                    V.tensor_tensor(lo, g, hi.bitcast(F32), ALU.subtract).then_inc(vacated[1], 1)

                if n_y == 0:
                    dve.wait_ge(S["table_out"], 16)
                alone(dve)
                with dve.Fori(0, KF // 2) as i:
                    gated(i * 2, 0)
                    gated(i * 2 + 1, 1)
                if n_y == 2:
                    first_gains(l * -1 + (DEPTH - 1))
                post_norm(l, post, y_f, True, n_y)
                if n_y == 2:
                    dve.wait_ge(S["gain_now"], l + 2)

            def mixer(l):
                pre_norm(l, "mix", 1, u_norm_m, u_lm)
                dve.wait_ge(S["hready"], l * 26 + 16)
                for part in (uT_r, u_lm):
                    V.tensor_copy(part[:, :, TOK:SEQ + P].rearrange("p k (a b) -> p k a b", a=3),
                                  part[:, :, SEQ:TOK].bitcast(F32).unsqueeze(2).broadcast_to([P, KD, 3, NEW])).then_inc(S["hready"], 1)
                for dst, src in ((ident_r, ident), (sb_mask_r, sb_mask), (chunk_mask_r, chunk_mask)):
                    V.tensor_copy(dst[:], src).then_inc(S["masks_ready"], 1)
                i = 0
                for s in range(1, 5):
                    w = MASK_W[s]
                    a = acc[:, ACC_AT[s]:ACC_AT[s] + w]
                    for h in range(H):
                        dve.wait_ge(S["idx_rel"], l * 32 + i + 3)
                        if h == 0:
                            V.tensor_scalar(a, rel[:, i % 2, 0:w], wI[:, s, h:h + 1], None, ALU.mult).then_inc(S["idx_acc"], 1)
                        else:
                            dve.wait_ge(S["idx_acc"], l * 32 + i + 2)
                            V.scalar_tensor_tensor(out=a, in0=rel[:, i % 2, 0:w], scalar=wI[:, s, h:h + 1], in1=a, op0=ALU.mult,
                                                   op1=ALU.add).then_inc(S["idx_acc"], 1)
                        i += 1
                dve.wait_ge(S["idx_acc"], l * 32 + 34)
                for s in range(1, 4):
                    w = MASK_W[s]
                    ins = V.memset(acc[0:CHUNK, ACC_AT[s] + w - CHUNK:ACC_AT[s] + w], LOWEST)
                link(l, ins)
                link(l, V.memset(msk[:, 0:P], 0.0))
                link(l, V.memset(msk[0:CHUNK, CHUNK:P], -BIG))
                for s in range(1, 5):
                    select(l, s)
                rotate_keys(l)
                invert(l, "q")
                for k in range(KQ):
                    V.scalar_tensor_tensor(out=ql[:, k, :], in0=ql[:, k, :], scalar=g_now[:, 24 + k:25 + k], in1=rstd[:],
                                           op0=ALU.mult, op1=ALU.mult).then_inc(S["lat_ready"], 1)
                invert(l, "kv")
                for k in range(KKV):
                    for a, b, c in ((0, SEQ, 0), (KEY_NEW, NKEY, SEQ)):
                        V.scalar_tensor_tensor(out=ckv[:, k, a:b], in0=ckv[:, k, a:b], scalar=g_now[:, 27 + k:28 + k],
                                               in1=rstd[:, c:c + b - a], op0=ALU.mult, op1=ALU.mult).then_inc(S["lat_ready"], 1)
                dve.wait_ge(S["rows_ki"], 16 * (l * 2 + 2))
                branch_b(l)
                dve.wait_ge(S["rows_out"], 16 * (l * 12 + 12))
                for g in range(2):
                    a2 = lambda v: v.rearrange("p (a b) -> p a b", a=2)
                    for e, (name, dst) in enumerate(((f"qr{g}", qAr[:, g, :]), (f"qs{g}", rope_t))):
                        u = TILE[name] % 2
                        filled(l, u, turn_of(name))
                        V.tensor_tensor(a2(dst), unit(u)[:, :, 0:HALF], a2(ropes[:, e, :]), ALU.mult).then_inc(vacated[u], 1)
                    for name in (f"qr{g}", f"qs{g}"):
                        dve.wait_ge(vacated[TILE[name] % 2], l * T_LAYER + turn_of(name) + 3)
                    V.tensor_tensor(qAr[:, g, :], qAr[:, g, :], rope_t, ALU.add).then_inc(S["qr_ready"], 1)
                    dve.wait_ge(S["qr_ready"], l * 2 + g + 1)
                attend(l, 0)
                attend(l, 1)
                dve.wait_ge(S["branch_out"], l * N_PAIR + N_PAIR + 2)
                V.tensor_copy(o_h[2][:], qC).then_inc(S["split_c"], 1)
                dve.wait_ge(S["split_c"], l * 2 + 1)
                V.tensor_tensor(o_l[2][:], qC, o_h[2][:].bitcast(F32), ALU.subtract).then_inc(S["split_c"], 1)
                halves = lambda v: v.rearrange("p (a b) -> p a b", a=2)
                with dve.Fori(0, 2) as i:
                    for j in range(4):
                        for b in range(3):
                            turn = turn_of("g0_0") + 3 * j + b + i * 12
                            filled(l, 1, turn)
                            dve.wait_ge(vacated[0], l * T_LAYER + turn + 3)
                            V.tensor_tensor(halves(mt[:, min(b, 1), :]), halves(sig[:, (3 * j + b) % 2, :]), unit(1)[:, :, 0:HALF],
                                            ALU.mult).then_inc(vacated[1], 1)
                            if b == 0:
                                continue
                            dve.wait_ge(vacated[1], l * T_LAYER + turn + 3)
                            if b == 2:
                                hi = merged_h[:, bass.ds(i * 4 + j, 1)].rearrange("p o n -> p (o n)")
                                lo = merged_l[:, bass.ds(i * 4 + j, 1)].rearrange("p o n -> p (o n)")
                                V.tensor_tensor(hi, mt[:, 0, :], mt[:, 1, :], ALU.add).then_inc(S["merge_step"], 1)
                            V.tensor_tensor(mt[:, 0, :], mt[:, 0, :], mt[:, 1, :], ALU.add).then_inc(S["merge_step"], 1)
                            dve.wait_ge(S["merge_step"], l * 3 * KD + i * 12 + 3 * j + (1 if b == 1 else 3))
                        V.tensor_tensor(lo, mt[:, 0, :], hi.bitcast(F32), ALU.subtract).then_inc(S["merge_ready"], 1)
                        dve.wait_ge(S["merge_ready"], l * KD + i * 4 + j + 1)
                post_norm(l, "mix_post", y_m, False, 1)

            def select(l, s):
                w, k = MASK_W[s], (TOPK if s < 4 else TOPK_S)
                a = acc[:, ACC_AT[s]:ACC_AT[s] + w]
                wk, eq, cu = topw[:, 0:w], eqv[:, 0:w], cum[:, 0:w]
                src = a
                for r in range(k // 8):
                    link(l, V.max(m8[:], src))
                    if r < k // 8 - 1:
                        link(l, V.match_replace(wk, m8[:], src, LOWEST))
                        src = wk
                link(l, V.tensor_scalar(wk, a, m8[:, 7:8], None, ALU.is_gt))
                link(l, V.tensor_reduce(cnt[:, 0:1], wk, AX_X, ALU.add))
                link(l, V.tensor_scalar(cnt[:, 1:2], cnt[:, 0:1], -1.0, float(k), ALU.mult, ALU.add))
                link(l, V.tensor_scalar(eq, a, m8[:, 7:8], None, ALU.is_equal))
                link(l, V.tensor_tensor_scan(cu, eq, eq, 0.0, ALU.add, ALU.max))
                link(l, V.scalar_tensor_tensor(out=cu, in0=cu, scalar=cnt[:, 1:2], in1=eq, op0=ALU.is_le, op1=ALU.mult))
                link(l, V.tensor_tensor(wk, wk, cu, ALU.add))
                V.tensor_scalar(msk[:, MASK_AT[s]:MASK_AT[s] + w], wk, -1.0, BIG, ALU.add, ALU.mult).then_inc(S["sel_ready"], 1)
                dve.wait_ge(S["sel_ready"], l * 4 + s)
                alone(dve)

            def rotate_keys(l):
                dve.wait_ge(S["ropes_in"], 16)
                for name in ("kr", "krs"):
                    dve.wait_ge(vacated[TILE[name] % 2], l * T_LAYER + turn_of(name) + 3)
                link(l, V.tensor_tensor(kr_raw[:, 1, :], kr_raw[:, 1, :], ropes[:, 1, :], ALU.mult))
                V.tensor_tensor(rope_t, kr_raw[:, 0, :], ropes[:, 0, :], ALU.mult).then_inc(S["rope_step"], 1)
                dve.wait_ge(S["rope_step"], l * 3 + 1)
                for a, b, c in ((0, SEQ, 0), (KEY_NEW, NKEY, SEQ)):
                    V.tensor_tensor(kr[:, a:b], rope_t[:, c:c + b - a], kr_raw[:, 1, c:c + b - a], ALU.add).then_inc(S["rope_step"], 1)
                dve.wait_ge(S["rope_step"], l * 3 + 3)

            def branch_b(l):
                nb = l * (N_B + 3)
                for t in range(N_B + 3):
                    dve.wait_ge(S["sb_soft"], nb + t + 1)
                    if t < N_B:
                        h, j = t // 4, 3 - t % 4
                        w, at = SEQ - P * j, 128 * ((3 - j) * (4 - j) // 2)
                        if t % 4 == 0 and h >= 2:
                            dve.wait_ge(S["sb_cum"], nb + t - 4)
                        V.scalar_tensor_tensor(out=sb_sp[:, h % 2, at:at + w], in0=PS[:, t % 4, 0:w], scalar=0.0,
                                               in1=sb_e[:, t % 2, 0:w], op0=ALU.max, op1=ALU.add).then_inc(S["sb_sp_ready"], 1)
                    else:
                        n = t - N_B
                        kt, m = 2 - n, (NEW, P, P)[n]
                        if n == 0:
                            dve.wait_ge(S["sb_cum"], nb + N_B)
                        V.scalar_tensor_tensor(out=sb_sp[0:m, 0, 256 * n:256 * n + 256].rearrange("p (a b) -> p a b", a=2),
                                               in0=PS[0:m, 2 * kt:2 * kt + 2, 0:P], scalar=0.0,
                                               in1=sb_e[0:m, t % 2, 0:2 * P].rearrange("p (a b) -> p a b", a=2),
                                               op0=ALU.max, op1=ALU.add).then_inc(S["sb_sp_ready"], 1)
                dve.wait_ge(S["sb_out"], l * 5 + 5)

            def attend(l, c):
                n0, q0 = l * N_UNIT + c * 34, l * N_PAIR + 5 * c

                def bias(i):
                    p, s, e = UNITS[i]
                    w = keys(s)[1]
                    x = PS[:, score_bank(c, i), 0:w]
                    dve.wait_ge(S["s_done"], n0 + i + 1)
                    dve.wait_ge(S["probs_ready"], n0 + i + 2)
                    if c == 1:
                        h = 2 * p + e
                        if s == 0:
                            if h < 4:
                                dve.wait_ge(S["t5_in01"], (l * 4 + 4) * 16)
                            else:
                                dve.wait_ge(S[f"t5_in{h // 2}"], (l * 2 + 2) * 16)
                        if s == 4 and e == 0:
                            dve.wait_ge(S["t5s_in"], (l * 8 + 8) * 16)
                        t5 = T5[:, h % 4, 384 - P * s:384 - P * s + w] if s < 4 else T5s[:, e, :]
                        dve.wait_ge(S["pt_done"], n0 + i + 1)
                        x = probs(c, i)[:, 0:w]
                        link(l, V.scalar_tensor_tensor(out=x, in0=PS[:, score_bank(c, i), 0:w], scalar=SCALE_C, in1=t5, op0=ALU.mult,
                                                       op1=ALU.add))
                        link(l, V.tensor_tensor(x, x, msk[:, MASK_AT[s]:MASK_AT[s] + w], ALU.add))
                    link(l, V.tensor_reduce(mx[:, i % 2:i % 2 + 1], x, AX_X, ALU.max))
                    V.tensor_scalar(nbias[:, i % 2:i % 2 + 1], mx[:, i % 2:i % 2 + 1], -SCALE_A if c == 0 else -1.0, None,
                                    ALU.mult).then_inc(S["bias_ready"], 1)

                def normalise(p, i):
                    q = 5 * c + p
                    n = 8 if p < 4 else 2
                    dve.wait_ge(S["pv_done"], n0 + i + 3)
                    dve.wait_ge(S["probs_ready"], n0 + i + 4)
                    dve.wait_ge(S["ot_done"], q0 + p + 1)
                    link(l, V.reciprocal(rinv[:, q % 2, 0:n], sums[:, q % 2, 0:n]))
                    V.tensor_tensor(OT[:, q % 2, 0:n * DH].rearrange("p (a b) -> p a b", a=n),
                                    PS[:, 4 + q % 2, 0:n * DH].rearrange("p (a b) -> p a b", a=n),
                                    rinv[:, q % 2, 0:n].unsqueeze(2).broadcast_to([P, n, DH]), ALU.mult).then_inc(S["heads_normed"], 1)

                n = len(UNITS)
                ends = {7: 0, 15: 1, 23: 2, 31: 3, 33: 4}
                for i in range(n + 3):
                    if i < n:
                        bias(i)
                    if c == 0 and 2 <= i <= n + 1:
                        copy_probs(dve, V.tensor_copy, n0, i - 2)
                    if i - 3 in ends:
                        normalise(ends[i - 3], i - 3)

            def first_gains(l):
                V.tensor_copy(g_now[:, 0:KD], gain[:, bass.ds(l, 1), 0:KD].rearrange("p o n -> p (o n)")).then_inc(S["gain_now"], 1)

            first_gains(0)
            dve.wait_ge(S["gain_now"], 1)
            with dve.Fori(0, DEPTH) as l:
                count[0] = 0
                link(l, V.tensor_copy(g_now[:, KD:], gain[:, bass.ds(l, 1), KD:].rearrange("p o n -> p (o n)")))
                ffn(l, T_A, "pre_a", "post_a", 0)
                mixer(l)
                ffn(l, T_B, "pre_b", "post_b", 2)
                assert count[0] == per, count[0]


DVE_STEPS = (1 + 1 + 2 + sum(2 * (k // 8) - 1 + 7 for k in (TOPK, TOPK, TOPK, TOPK_S)) + 1
             + len(UNITS) * (1 + 3) + N_PAIR)


def t5_buckets():
    rel = np.arange(NREL) - (SEQ - 1)
    nb, max_exact = 16, 8
    n = np.abs(rel)
    large = max_exact + (np.log(np.maximum(n, 1).astype(np.float32) / np.float32(max_exact)) / np.float32(math.log(256 / max_exact))
                         * np.float32(nb - max_exact)).astype(np.int32)
    return np.where(rel > 0, nb, 0) + np.where(n < max_exact, n, np.minimum(large, nb - 1))


def shape_constants():
    onehot = np.zeros((32, NREL), np.float32)
    onehot[t5_buckets(), np.arange(NREL)] = 1
    k, q = np.arange(P)[:, None], np.arange(P)[None, :]
    cst = np.zeros((P, 6, P), np.float32)
    cst[:, 0] = 1
    cst[:, 1] = -1
    cst[:, 2] = np.where(k >= q, -1, 0)
    cst[:, 3] = np.eye(P)
    cst[:, 4] = np.where(k >= q, -BIG, 0)
    cst[:, 5] = np.where((k < CHUNK) & (q >= CHUNK), -BIG, 0)
    pos = np.concatenate([np.arange(SEQ), PAST + np.arange(NEW)]).astype(np.float32)
    half = ROPE // 2
    inv = np.float32(10000.0) ** (-np.arange(half, dtype=np.float32) / np.float32(half))
    ang = pos[None, :] * inv[:, None]
    c, s = np.cos(ang), np.sin(ang)
    ropes = np.stack([np.tile(np.concatenate([c, c]), (4, 1)), np.tile(np.concatenate([-s, s]), (4, 1))], axis=1)
    return onehot, cst, np.ascontiguousarray(ropes.astype(np.float32))


def kernel(**inputs):
    from concourse import bacc as _bacc
    from concourse.bass_utils import run_bass_kernel_spmd as _run

    a = {k: np.asarray(v) for k, v in inputs.items()}
    L = DEPTH
    onehot, cst, ropes = shape_constants()

    at = np.concatenate([[0], np.cumsum([384, 256, 32, 512, 512, 512, 512, 64, 64, 512, 64, 8, 1024, 1024, 1024])])
    part = {n: np.arange(at[i], at[i + 1]) for i, n in enumerate(
        ["ql", "kv", "kr", "qb", "kb", "vb", "qc", "kc", "vc", "qi", "ki", "wi", "ga", "gb", "gc"])}
    swap = np.concatenate([np.arange(16, 32), np.arange(16)])
    krs = part["kr"][swap]
    cols = np.concatenate([part["ki"], part["ki"], part["qi"], part["kc"], part["kc"], part["qc"], part["qb"], part["kb"],
                           part["kr"], part["kr"], part["kr"], part["kr"], krs, krs, krs, krs, part["ql"], part["kv"], part["kv"][:128]])
    w_in = a["w_in"].reshape(L, KD, P, -1)

    def tiles(w, n):
        k = w.shape[1]
        return w.reshape(L, k, P, n, P).transpose(0, 3, 2, 1, 4).reshape(L, n, P, k * P)

    def groups(w, g):
        n, f = w.shape[1], w.shape[3]
        return w.reshape(L, n // g, g, P, f).transpose(0, 1, 3, 2, 4).reshape(L, n // g, P, g * f)

    uq = a["w_mla_uq"].reshape(L, KQ, P, H * 96)
    h = np.arange(H)[:, None]
    nope = (h * 96 + np.arange(64)).reshape(-1)
    rp = h * 96 + 64 + np.arange(32)
    rs = h * 96 + 64 + swap
    uq_cols = np.concatenate([nope, rp[:4].reshape(-1), rs[:4].reshape(-1), rp[4:].reshape(-1), rs[4:].reshape(-1)])
    ukv = a["w_mla_ukv"].reshape(L, KKV, P, H * 128)
    un = (h * 128 + np.arange(64)).reshape(-1)
    uv = (h * 128 + 64 + np.arange(64)).reshape(-1)
    gates = np.stack([tiles(w_in[..., part[g]], KD) for g in ("ga", "gb", "gc")], axis=2)
    br = a["w_branch"].reshape(L, 3, 4, P, KD, P).transpose(0, 4, 1, 3, 2, 5).reshape(L, KD, 3, P, 4 * P)
    vcwi = np.concatenate([part["vc"], part["wi"]])

    def gcols(g):
        return g.reshape(L, -1, P).transpose(2, 0, 1)

    def feat(x):
        return x.reshape(L, PAST, -1).transpose(0, 2, 1)

    def tokm(x):
        return x.reshape(L, 2, P, -1).transpose(0, 2, 1, 3)

    f = a["ffn_pre_gain"]
    g = a["ffn_post_gain"]
    arrays = {
        "x": np.concatenate([a["x_prompt"][0], a["x_sample"][0]]).T.reshape(KD, P, TOK).transpose(1, 0, 2),
        "cst": cst, "ropes": ropes, "onehot": onehot, "rel_bias": a["rel_bias"],
        "gains": np.concatenate([gcols(v) for v in (f[:, 0], g[:, 0], a["mix_pre_gain"], a["mla_q_norm"], a["mla_kv_norm"],
                                                    a["mix_post_gain"], f[:, 1], g[:, 1])], axis=2),
        "w_up": a["w_ffn_up"].reshape(L, 2, KD, P, 2, KF, P).transpose(0, 1, 5, 3, 4, 2, 6).reshape(L, 2 * KF, P, 2048),
        "w_dn": a["w_ffn_down"].reshape(L, 2, 2, 11, P, KD, P).transpose(0, 1, 5, 2, 4, 3, 6).reshape(L, 32, P, 1408),
        "w_in": groups(tiles(w_in[..., cols], 26), 2),
        "w_vb": w_in[..., part["vb"]].reshape(L, 2, 4, P, 512).transpose(0, 1, 3, 2, 4).reshape(L, 2, P, 2048),
        "w_vw": tiles(np.concatenate([w_in[..., vcwi], np.zeros((L, KD, P, P - len(vcwi)), np.float32)], axis=3), 1),
        "w_uq": groups(tiles(uq[..., uq_cols], 8), 4),
        "w_ukn": groups(tiles(ukv[..., un], 4), 4),
        "w_ukv": ukv[..., uv].transpose(0, 2, 1, 3).reshape(L, 1, P, 1024),
        "w_mg": np.concatenate([gates, br], axis=4).reshape(L, 3 * KD, P, 1536),
        "w_out": groups(tiles(a["w_o"].reshape(L, KD, P, D), KD), 2),
        "c_kidx": np.concatenate([feat(a["cache_dsa_kidx"])] * 2, axis=1)[:, :, None],
        "c_dsk": np.concatenate([feat(a["cache_dsa_k"])] * 2, axis=1)[:, :, None],
        "c_dsv": tokm(a["cache_dsa_v"]),
        "c_sbk": feat(a["cache_sb_k"]).reshape(L, 4, P, PAST).transpose(0, 2, 1, 3),
        "c_sbv": tokm(a["cache_sb_v"]),
        "c_kr": np.concatenate([feat(a["cache_mla_krope"])] * 4, axis=1)[:, :, None],
        "c_ckv": feat(a["cache_mla_ckv"]).reshape(L, KKV, P, PAST).transpose(0, 2, 1, 3),
    }
    outs = {"y": (P, KD, TOK), "o_kr": (L, ROPE, TOK),
            "p_ki": (L, DH, 1, SEQ), "s_ki": (L, DH, 1, NEW), "p_kc": (L, DH, 1, SEQ), "s_kc": (L, DH, 1, NEW),
            "p_vb": (L, P, 4, 512), "s_vb": (L, NEW, 1, 512), "p_vc": (L, P, 4, DH), "s_vc": (L, NEW, 1, DH),
            "p_kb": (L, P, 4, SEQ), "s_kb": (L, P, 4, NEW), "p_ckv": (L, P, 2, SEQ), "s_ckv": (L, P, 2, NEW)}

    nc = _bacc.Bacc("TRN2", target_bir_lowering=False, num_devices=1)
    arrays = {f"in_{k}": np.ascontiguousarray(v) for k, v in arrays.items()}
    dram = {k[3:]: nc.dram_tensor(k, v.shape, F32, kind="ExternalInput").ap() for k, v in arrays.items()}
    dram |= {k: nc.dram_tensor(f"out_{k}", v, F32, kind="ExternalOutput").ap() for k, v in outs.items()}
    dram["t5"] = nc.dram_tensor("t5_by_distance", (H, P, NREL), F32, kind="Internal").ap()
    build(nc, dram)
    r = {k: _run_out for k, _run_out in _run(nc, [arrays], core_ids=[0]).results[0].items()}
    o = {k: r[f"out_{k}"] for k in outs}
    y = o["y"].transpose(2, 1, 0).reshape(TOK, D)

    def rows(v, width):
        return v.transpose(0, 3, 2, 1).reshape(L, 1, v.shape[3], width)

    def token_rows(v, width):
        return v.transpose(0, 2, 1, 3).reshape(L, 1, -1, width)

    def group(c, sl):
        return (rows(o[f"{c}_ckv"], KV_LORA), o["o_kr"][:, :, sl].transpose(0, 2, 1)[:, None],
                rows(o[f"{c}_kb"], MIX).reshape(L, 1, -1, H, DH), token_rows(o[f"{c}_vb"], MIX).reshape(L, 1, -1, H, DH),
                rows(o[f"{c}_kc"], DH), token_rows(o[f"{c}_vc"], DH), rows(o[f"{c}_ki"], DH))

    return tuple(np.ascontiguousarray(v) for v in (
        y[None, :SEQ], y[None, SEQ:], *group("p", slice(0, SEQ)), *group("s", slice(SEQ, TOK))))
```
